# Optimizing a Trainium2 kernel written in Bass

```python
import math
import jax, jax.numpy as jnp
from jax import lax
import numpy as np

D_MODEL = 1024
BATCH = 1
SEQ = 1024
DEPTH = 1

CHUNK = 64
EPS = 1e-6
D_MIX = D_MODEL
CONV_K = 4

SSD_HEADS = 8
SSD_HEAD_DIM = 64
SSD_DIM = SSD_HEADS * SSD_HEAD_DIM
SSD_GROUPS = 2
SSD_STATE = 128
SSD_CONV_DIM = SSD_DIM + 2 * SSD_GROUPS * SSD_STATE

ATT_HEADS = 4
ATT_KV_HEADS = 2
ATT_HEAD_DIM = 64
ATT_DIM = ATT_HEADS * ATT_HEAD_DIM
ATT_KV_DIM = ATT_KV_HEADS * ATT_HEAD_DIM
WINDOW = 128
WIN_CHUNKS = WINDOW // CHUNK

GDN_HEADS = 4
GDN_HEAD_K = 64
GDN_HEAD_V = 64
GDN_KDIM = GDN_HEADS * GDN_HEAD_K
GDN_DIM = GDN_HEADS * GDN_HEAD_V
GDN_CONV_DIM = 2 * GDN_KDIM + GDN_DIM

FF = ((8 * D_MODEL // 3 + 255) // 256) * 256

IN_SIZES = (ATT_DIM, ATT_KV_DIM, ATT_KV_DIM,
            SSD_DIM, SSD_CONV_DIM, SSD_HEADS,
            GDN_CONV_DIM, GDN_DIM, GDN_HEADS, GDN_HEADS)
IN_COLS = sum(IN_SIZES)


def _offsets(sizes):
    out, acc = [], 0
    for s in sizes[:-1]:
        acc += s
        out.append(acc)
    return out

def rmsnorm(x, w):
    xf = x.astype(jnp.float32)
    y = xf * lax.rsqrt(jnp.mean(xf * xf, axis=-1, keepdims=True) + EPS)
    return (y * w.astype(jnp.float32)).astype(x.dtype)

def l2norm(x):
    return x * lax.rsqrt(jnp.sum(x * x, axis=-1, keepdims=True) + EPS)

def causal_dwconv(x, w, b=None):
    k = w.shape[0]
    t = x.shape[1]
    xp = jnp.pad(x, ((0, 0), (k - 1, 0), (0, 0)))
    y = xp[:, 0:t] * w[0]
    for i in range(1, k):
        y = y + xp[:, i:i + t] * w[i]
    if b is not None:
        y = y + b
    return y

def alibi_slopes(n):
    return 2.0 ** (-8.0 * jnp.arange(1, n + 1, dtype=jnp.float32) / n)

def lower_exp_diff(cs):
    n = cs.shape[-1]
    tril = jnp.tril(jnp.ones((n, n), dtype=bool))
    diff = cs[..., :, None] - cs[..., None, :]
    return jnp.where(tril, jnp.exp(jnp.where(tril, diff, 0.0)), 0.0)

def swa_sink_alibi(q, k, v, sinks):
    bsz, t = q.shape[0], q.shape[1]
    nc = t // CHUNK
    grp = ATT_HEADS // ATT_KV_HEADS
    band = (WIN_CHUNKS + 1) * CHUNK
    qc = q.reshape(bsz, nc, CHUNK, ATT_KV_HEADS, grp, ATT_HEAD_DIM)
    padw = ((0, 0), (WIN_CHUNKS * CHUNK, 0), (0, 0))
    kp = jnp.pad(k, padw).reshape(bsz, nc + WIN_CHUNKS, CHUNK, ATT_KV_HEADS, ATT_HEAD_DIM)
    vp = jnp.pad(v, padw).reshape(bsz, nc + WIN_CHUNKS, CHUNK, ATT_KV_HEADS, ATT_HEAD_DIM)
    kb = jnp.concatenate([kp[:, j:j + nc] for j in range(WIN_CHUNKS + 1)], axis=2)
    vb = jnp.concatenate([vp[:, j:j + nc] for j in range(WIN_CHUNKS + 1)], axis=2)
    s = jnp.einsum('bcikgd,bcjkd->bckgij', qc, kb).astype(jnp.float32) * (ATT_HEAD_DIM ** -0.5)
    qi = jnp.arange(CHUNK)[:, None]
    kj = jnp.arange(band)[None, :]
    dist = jnp.abs(qi + WIN_CHUNKS * CHUNK - kj).astype(jnp.float32)
    slopes = alibi_slopes(ATT_HEADS).reshape(ATT_KV_HEADS, grp)
    s = s - slopes[:, :, None, None] * dist
    key_chunk = jnp.arange(nc)[:, None] - WIN_CHUNKS + (jnp.arange(band) // CHUNK)[None, :]
    valid = key_chunk >= 0
    s = jnp.where(valid[None, :, None, None, None, :], s, -jnp.inf)
    sink = jnp.broadcast_to(sinks.astype(jnp.float32).reshape(1, 1, ATT_KV_HEADS, grp, 1, 1),
                            s.shape[:-1] + (1,))
    p = jax.nn.softmax(jnp.concatenate([s, sink], axis=-1), axis=-1)[..., :band]
    o = jnp.einsum('bckgij,bcjkd->bcikgd', p.astype(v.dtype), vb)
    return o.reshape(bsz, t, ATT_DIM)

def ssd_mixer(z, xbc, dt, conv_w, conv_b, dt_bias, a_log, d_skip, norm_w):
    bsz, t = xbc.shape[0], xbc.shape[1]
    nc = t // CHUNK
    hpg = SSD_HEADS // SSD_GROUPS
    xbc = jax.nn.silu(causal_dwconv(xbc, conv_w, conv_b)).astype(jnp.float32)
    xs, bm, cm = jnp.split(xbc, [SSD_DIM, SSD_DIM + SSD_GROUPS * SSD_STATE], axis=-1)
    xs = xs.reshape(bsz, t, SSD_HEADS, SSD_HEAD_DIM)
    bm = jnp.repeat(bm.reshape(bsz, t, SSD_GROUPS, SSD_STATE), hpg, axis=2)
    cm = jnp.repeat(cm.reshape(bsz, t, SSD_GROUPS, SSD_STATE), hpg, axis=2)
    dt = jax.nn.softplus(dt.astype(jnp.float32) + dt_bias.astype(jnp.float32))
    a = -jnp.exp(a_log.astype(jnp.float32))
    xc = (xs * dt[..., None]).reshape(bsz, nc, CHUNK, SSD_HEADS, SSD_HEAD_DIM)
    bc = bm.reshape(bsz, nc, CHUNK, SSD_HEADS, SSD_STATE)
    cc = cm.reshape(bsz, nc, CHUNK, SSD_HEADS, SSD_STATE)
    da = (dt * a).reshape(bsz, nc, CHUNK, SSD_HEADS).transpose(0, 3, 1, 2)
    a_cs = jnp.cumsum(da, axis=-1)
    lmat = lower_exp_diff(a_cs)
    scores = jnp.einsum('bclhn,bcshn->bhcls', cc, bc) * lmat
    y_diag = jnp.einsum('bhcls,bcshp->bclhp', scores, xc)
    decay_states = jnp.exp(a_cs[..., -1:] - a_cs)
    chunk_states = jnp.einsum('bclhn,bhcl,bclhp->bchpn', bc, decay_states, xc)
    chunk_decay = jnp.exp(a_cs[..., -1])

    def step(state, inp):
        new, dec = inp
        return state * dec[..., None, None] + new, state

    init = jnp.zeros((bsz, SSD_HEADS, SSD_HEAD_DIM, SSD_STATE), jnp.float32)
    _, prev = lax.scan(step, init, (chunk_states.transpose(1, 0, 2, 3, 4),
                                    chunk_decay.transpose(2, 0, 1)))
    prev = prev.transpose(1, 0, 2, 3, 4)
    y_off = jnp.einsum('bclhn,bchpn,bhcl->bclhp', cc, prev, jnp.exp(a_cs))
    y = (y_diag + y_off).reshape(bsz, t, SSD_HEADS, SSD_HEAD_DIM) + xs * d_skip.astype(jnp.float32)[:, None]
    g = y.reshape(bsz, t, SSD_DIM) * jax.nn.silu(z.astype(jnp.float32))
    g = g.reshape(bsz, t, SSD_GROUPS, SSD_DIM // SSD_GROUPS)
    g = g * lax.rsqrt(jnp.mean(g * g, axis=-1, keepdims=True) + EPS)
    return (g.reshape(bsz, t, SSD_DIM) * norm_w.astype(jnp.float32)).astype(z.dtype)

def gdn_mixer(qkv, z, b, a, conv_w, dt_bias, a_log, norm_w):
    bsz, t = qkv.shape[0], qkv.shape[1]
    nc = t // CHUNK
    qkv = jax.nn.silu(causal_dwconv(qkv, conv_w)).astype(jnp.float32)
    q, k, v = jnp.split(qkv, [GDN_KDIM, 2 * GDN_KDIM], axis=-1)
    q = l2norm(q.reshape(bsz, t, GDN_HEADS, GDN_HEAD_K)) * (GDN_HEAD_K ** -0.5)
    k = l2norm(k.reshape(bsz, t, GDN_HEADS, GDN_HEAD_K))
    v = v.reshape(bsz, t, GDN_HEADS, GDN_HEAD_V)
    beta = jax.nn.sigmoid(b.astype(jnp.float32))
    g = -jnp.exp(a_log.astype(jnp.float32)) * jax.nn.softplus(a.astype(jnp.float32) + dt_bias.astype(jnp.float32))

    def chunks(u):
        return u.reshape(bsz, nc, CHUNK, GDN_HEADS, u.shape[-1]).transpose(0, 3, 1, 2, 4)

    qc, kc, vc = chunks(q), chunks(k), chunks(v)
    betac = beta.reshape(bsz, nc, CHUNK, GDN_HEADS).transpose(0, 3, 1, 2)
    gc = jnp.cumsum(g.reshape(bsz, nc, CHUNK, GDN_HEADS).transpose(0, 3, 1, 2), axis=-1)
    decay = lower_exp_diff(gc)
    kbeta = kc * betac[..., None]
    strict = jnp.tril(jnp.einsum('bhcid,bhcjd->bhcij', kbeta, kc) * decay, -1)
    rhs = jnp.concatenate([vc * betac[..., None], kbeta * jnp.exp(gc)[..., None]], axis=-1)
    sol = lax.linalg.triangular_solve(strict, rhs, left_side=True, lower=True, unit_diagonal=True)
    u, w = jnp.split(sol, [GDN_HEAD_V], axis=-1)
    qk = jnp.einsum('bhcid,bhcjd->bhcij', qc, kc) * decay

    def step(state, inp):
        q_i, k_i, u_i, w_i, qk_i, g_i = inp
        v_new = u_i - jnp.einsum('bhld,bhde->bhle', w_i, state)
        o = (jnp.einsum('bhld,bhde->bhle', q_i * jnp.exp(g_i)[..., None], state)
             + jnp.einsum('bhls,bhse->bhle', qk_i, v_new))
        g_last = g_i[..., -1]
        state = (state * jnp.exp(g_last)[..., None, None]
                 + jnp.einsum('bhld,bhle->bhde', k_i * jnp.exp(g_last[..., None] - g_i)[..., None], v_new))
        return state, o

    xs = tuple(jnp.moveaxis(u_, 2, 0) for u_ in (qc, kc, u, w, qk, gc))
    init = jnp.zeros((bsz, GDN_HEADS, GDN_HEAD_K, GDN_HEAD_V), jnp.float32)
    _, o = lax.scan(step, init, xs)
    o = o.transpose(1, 0, 3, 2, 4).reshape(bsz, t, GDN_HEADS, GDN_HEAD_V)
    o = o * lax.rsqrt(jnp.mean(o * o, axis=-1, keepdims=True) + EPS) * norm_w.astype(jnp.float32)
    o = o * jax.nn.silu(z.astype(jnp.float32).reshape(bsz, t, GDN_HEADS, GDN_HEAD_V))
    return o.reshape(bsz, t, GDN_DIM).astype(z.dtype)

def first_inputs(seed: int = 0) -> dict:
    key = jax.random.key(seed)
    ks = jax.random.split(key, 24)
    L = DEPTH

    def nrm(k, shape, scale):
        return jax.random.normal(k, shape, jnp.float32) * scale

    def gain(k, shape):
        return 1.0 + 0.05 * jax.random.normal(k, shape, jnp.float32)

    def dt_bias_init(k, shape):
        u = jax.random.uniform(k, shape, jnp.float32, math.log(1e-3), math.log(1e-1))
        dtv = jnp.exp(u)
        return dtv + jnp.log(-jnp.expm1(-dtv))

    def a_log_init(k, shape):
        return jnp.log(jax.random.uniform(k, shape, jnp.float32, 1.0, 16.0))

    return {
        "x": nrm(ks[0], (BATCH, SEQ, D_MODEL), 1.0),
        "pre_mix_norm": gain(ks[1], (L, D_MODEL)),
        "post_mix_norm": gain(ks[2], (L, D_MODEL)),
        "pre_ffn_norm": gain(ks[3], (L, D_MODEL)),
        "post_ffn_norm": gain(ks[4], (L, D_MODEL)),
        "w_in": nrm(ks[5], (L, D_MODEL, IN_COLS), D_MODEL ** -0.5),
        "w_out": nrm(ks[6], (L, D_MIX, D_MODEL), D_MIX ** -0.5),
        "attn_sinks": nrm(ks[7], (L, ATT_HEADS), 0.5),
        "ssd_conv_w": nrm(ks[8], (L, CONV_K, SSD_CONV_DIM), CONV_K ** -0.5),
        "ssd_conv_b": nrm(ks[9], (L, SSD_CONV_DIM), 0.01),
        "ssd_dt_bias": dt_bias_init(ks[10], (L, SSD_HEADS)),
        "ssd_A_log": a_log_init(ks[11], (L, SSD_HEADS)),
        "ssd_D": 1.0 + 0.1 * jax.random.normal(ks[12], (L, SSD_HEADS), jnp.float32),
        "ssd_norm_w": gain(ks[13], (L, SSD_DIM)),
        "gdn_conv_w": nrm(ks[14], (L, CONV_K, GDN_CONV_DIM), CONV_K ** -0.5),
        "gdn_dt_bias": dt_bias_init(ks[15], (L, GDN_HEADS)),
        "gdn_A_log": a_log_init(ks[16], (L, GDN_HEADS)),
        "gdn_norm_w": gain(ks[17], (L, GDN_HEAD_V)),
        "ffn_w_gate": nrm(ks[18], (L, D_MODEL, FF), D_MODEL ** -0.5),
        "ffn_w_up": nrm(ks[19], (L, D_MODEL, FF), D_MODEL ** -0.5),
        "ffn_w_down": nrm(ks[20], (L, FF, D_MODEL), FF ** -0.5),
    }

def first_block(x, pre_mix_norm, post_mix_norm, pre_ffn_norm, post_ffn_norm, w_in, w_out,
              attn_sinks, ssd_conv_w, ssd_conv_b, ssd_dt_bias, ssd_A_log, ssd_D, ssd_norm_w,
              gdn_conv_w, gdn_dt_bias, gdn_A_log, gdn_norm_w, ffn_w_gate, ffn_w_up, ffn_w_down):
    offs = _offsets(IN_SIZES)
    for l in range(DEPTH):
        h = rmsnorm(x, pre_mix_norm[l])
        proj = h @ w_in[l]
        (a_q, a_k, a_v, s_z, s_xbc, s_dt, g_qkv, g_z, g_b, g_a) = jnp.split(proj, offs, axis=-1)
        att = swa_sink_alibi(a_q, a_k, a_v, attn_sinks[l])
        ssd = ssd_mixer(s_z, s_xbc, s_dt, ssd_conv_w[l], ssd_conv_b[l], ssd_dt_bias[l],
                        ssd_A_log[l], ssd_D[l], ssd_norm_w[l])
        gdn = gdn_mixer(g_qkv, g_z, g_b, g_a, gdn_conv_w[l], gdn_dt_bias[l], gdn_A_log[l], gdn_norm_w[l])
        mix = jnp.concatenate([att, ssd, gdn], axis=-1) @ w_out[l]
        x = x + rmsnorm(mix, post_mix_norm[l])
        h = rmsnorm(x, pre_ffn_norm[l])
        f = (jax.nn.silu(h @ ffn_w_gate[l]) * (h @ ffn_w_up[l])) @ ffn_w_down[l]
        x = x + rmsnorm(f, post_ffn_norm[l])
    return x


GRID_W = 64
HEAD_DIM = 64
N_Q_HEADS = 8
N_KV_HEADS = 2
GQA_GROUP = N_Q_HEADS // N_KV_HEADS
ATTN_WIDTH = N_Q_HEADS * HEAD_DIM
KV_WIDTH = N_KV_HEADS * HEAD_DIM
Q_BLOCK = 128
AXIAL_DIM = HEAD_DIM // 2
ROPE_THETA = 10000.0
CHUNK_2 = 128
N_GROUPS = 8
GMLP_WIDTH = 512
GROUP_DIM = GMLP_WIDTH // N_GROUPS
N_BRANCHES = 2

IN_SIZES_2 = (ATTN_WIDTH, KV_WIDTH, KV_WIDTH, ATTN_WIDTH,
            GMLP_WIDTH, GMLP_WIDTH, GMLP_WIDTH, N_BRANCHES * D_MODEL)
IN_WIDTH = sum(IN_SIZES_2)
IN_SPLITS = tuple(int(s) for s in np.cumsum(IN_SIZES_2)[:-1])


def rmsnorm_2(x, gain):
    x32 = x.astype(jnp.float32)
    y = x32 * lax.rsqrt(jnp.mean(x32 * x32, axis=-1, keepdims=True) + EPS)
    return (y * gain.astype(jnp.float32)).astype(x.dtype)

def layernorm(x, gain, bias):
    x32 = x.astype(jnp.float32)
    mu = jnp.mean(x32, axis=-1, keepdims=True)
    var = jnp.mean(jnp.square(x32 - mu), axis=-1, keepdims=True)
    y = (x32 - mu) * lax.rsqrt(var + EPS)
    return (y * gain.astype(jnp.float32) + bias.astype(jnp.float32)).astype(x.dtype)

def rope_half(x, ang):
    n = x.shape[-1] // 2
    x1, x2 = x[..., :n], x[..., n:]
    cos, sin = jnp.cos(ang).astype(x.dtype), jnp.sin(ang).astype(x.dtype)
    return jnp.concatenate([x1 * cos - x2 * sin, x1 * sin + x2 * cos], axis=-1)

def axial_rope(x, row_ang, col_ang):
    return jnp.concatenate([rope_half(x[..., :AXIAL_DIM], row_ang),
                            rope_half(x[..., AXIAL_DIM:], col_ang)], axis=-1)

def block_attention(q, k, v):
    B, S = q.shape[0], q.shape[1]
    n_blk = S // Q_BLOCK
    scale = 1.0 / math.sqrt(HEAD_DIM)
    qb = q.reshape(B, n_blk, Q_BLOCK, N_KV_HEADS, GQA_GROUP, HEAD_DIM).transpose(1, 0, 3, 4, 2, 5)
    kt = k.transpose(0, 2, 1, 3)
    vt = v.transpose(0, 2, 1, 3)

    def one_block(q_blk):
        s = jnp.einsum('bhgqd,bhkd->bhgqk', q_blk, kt).astype(jnp.float32) * scale
        p = jax.nn.softmax(s, axis=-1).astype(vt.dtype)
        return jnp.einsum('bhgqk,bhkd->bhgqd', p, vt)

    o = lax.map(one_block, qb)
    return o.transpose(1, 0, 4, 2, 3, 5).reshape(B, S, ATTN_WIDTH)

def hybrid_layer(x, norm_gain, w_in, q_gain, k_gain, w_proj_attn,
                 ln_v_gain, ln_v_bias, w_spatial, b_spatial, w_proj_gmlp,
                 b_merge, w_out):
    B, S, _ = x.shape
    rows = S // GRID_W
    h = rmsnorm_2(x, norm_gain)
    z = jnp.einsum('bsd,de->bse', h, w_in)
    q, k, v, gate_a, u_in, v_in, gate_b, g_merge = jnp.split(z, IN_SPLITS, axis=-1)

    row_idx = jnp.repeat(jnp.arange(rows, dtype=jnp.float32), GRID_W)
    col_idx = jnp.tile(jnp.arange(GRID_W, dtype=jnp.float32), rows)
    inv_freq = ROPE_THETA ** (-jnp.arange(0, AXIAL_DIM, 2, dtype=jnp.float32) / AXIAL_DIM)
    row_ang = (row_idx[:, None] * inv_freq)[:, None, :]
    col_ang = (col_idx[:, None] * inv_freq)[:, None, :]
    q = axial_rope(rmsnorm_2(q.reshape(B, S, N_Q_HEADS, HEAD_DIM), q_gain), row_ang, col_ang)
    k = axial_rope(rmsnorm_2(k.reshape(B, S, N_KV_HEADS, HEAD_DIM), k_gain), row_ang, col_ang)
    v = v.reshape(B, S, N_KV_HEADS, HEAD_DIM)
    attn = block_attention(q, k, v) * jax.nn.silu(gate_a)
    y_a = jnp.einsum('bse,ed->bsd', attn, w_proj_attn)

    u = jax.nn.gelu(u_in)
    vv = layernorm(jax.nn.gelu(v_in), ln_v_gain, ln_v_bias)
    vv = vv.reshape(B, S // CHUNK_2, CHUNK_2, N_GROUPS, GROUP_DIM)
    v_mix = jnp.einsum('gij,bcjgd->bcigd', w_spatial, vv) + b_spatial.T[:, :, None]
    gm = u * v_mix.reshape(B, S, GMLP_WIDTH) * jax.nn.silu(gate_b)
    y_b = jnp.einsum('bse,ed->bsd', gm, w_proj_gmlp)

    g = jax.nn.sigmoid(g_merge.reshape(B, S, N_BRANCHES, D_MODEL) + b_merge)
    y = g[:, :, 0, :] * y_a + g[:, :, 1, :] * y_b
    return x + jnp.einsum('bsd,de->bse', y, w_out)

def second_inputs(seed: int = 0) -> dict:
    key = jax.random.key(seed)
    ks = jax.random.split(key, 16)
    L = DEPTH
    nrm = lambda k, shape, fan: jax.random.normal(k, shape, jnp.float32) * (fan ** -0.5)
    return {
        "x": jax.random.normal(ks[0], (BATCH, SEQ, D_MODEL), jnp.float32),
        "norm_gain": 1.0 + 0.05 * jax.random.normal(ks[1], (L, D_MODEL), jnp.float32),
        "w_in": nrm(ks[2], (L, D_MODEL, IN_WIDTH), D_MODEL),
        "q_gain": 1.0 + 0.05 * jax.random.normal(ks[3], (L, HEAD_DIM), jnp.float32),
        "k_gain": 1.0 + 0.05 * jax.random.normal(ks[4], (L, HEAD_DIM), jnp.float32),
        "w_proj_attn": nrm(ks[5], (L, ATTN_WIDTH, D_MODEL), ATTN_WIDTH),
        "ln_v_gain": 1.0 + 0.05 * jax.random.normal(ks[6], (L, GMLP_WIDTH), jnp.float32),
        "ln_v_bias": 0.02 * jax.random.normal(ks[7], (L, GMLP_WIDTH), jnp.float32),
        "w_spatial": nrm(ks[8], (L, N_GROUPS, CHUNK_2, CHUNK_2), CHUNK_2),
        "b_spatial": 1.0 + 0.05 * jax.random.normal(ks[9], (L, N_GROUPS, CHUNK_2), jnp.float32),
        "w_proj_gmlp": nrm(ks[10], (L, GMLP_WIDTH, D_MODEL), GMLP_WIDTH),
        "b_merge": 0.02 * jax.random.normal(ks[11], (L, N_BRANCHES, D_MODEL), jnp.float32),
        "w_out": nrm(ks[12], (L, D_MODEL, D_MODEL), D_MODEL),
        "final_gain": 1.0 + 0.05 * jax.random.normal(ks[13], (D_MODEL,), jnp.float32),
    }

def second_block(x, norm_gain, w_in, q_gain, k_gain, w_proj_attn, ln_v_gain, ln_v_bias,
              w_spatial, b_spatial, w_proj_gmlp, b_merge, w_out, final_gain):
    for l in range(DEPTH):
        x = hybrid_layer(x, norm_gain[l], w_in[l], q_gain[l], k_gain[l], w_proj_attn[l],
                         ln_v_gain[l], ln_v_bias[l], w_spatial[l], b_spatial[l],
                         w_proj_gmlp[l], b_merge[l], w_out[l])
    return rmsnorm_2(x, final_gain)


def setup_inputs(seed=0):
    out = dict(first_inputs(seed))
    for name, value in second_inputs(seed + 1).items():
        if name != "x":
            out[name + "_2"] = value
    return out


def reference(
    x, pre_mix_norm, post_mix_norm, pre_ffn_norm, post_ffn_norm, w_in, w_out, attn_sinks,
    ssd_conv_w, ssd_conv_b, ssd_dt_bias, ssd_A_log, ssd_D, ssd_norm_w, gdn_conv_w, gdn_dt_bias,
    gdn_A_log, gdn_norm_w, ffn_w_gate, ffn_w_up, ffn_w_down, norm_gain_2, w_in_2, q_gain_2,
    k_gain_2, w_proj_attn_2, ln_v_gain_2, ln_v_bias_2, w_spatial_2, b_spatial_2, w_proj_gmlp_2,
    b_merge_2, w_out_2, final_gain_2,
):
    x = first_block(
        x, pre_mix_norm, post_mix_norm, pre_ffn_norm, post_ffn_norm, w_in, w_out, attn_sinks,
        ssd_conv_w, ssd_conv_b, ssd_dt_bias, ssd_A_log, ssd_D, ssd_norm_w, gdn_conv_w,
        gdn_dt_bias, gdn_A_log, gdn_norm_w, ffn_w_gate, ffn_w_up, ffn_w_down,
    )
    return second_block(
        x, norm_gain_2, w_in_2, q_gain_2, k_gain_2, w_proj_attn_2, ln_v_gain_2, ln_v_bias_2,
        w_spatial_2, b_spatial_2, w_proj_gmlp_2, b_merge_2, w_out_2, final_gain_2,
    )


_drawn_inputs = setup_inputs


def setup_inputs(seed=0):
    import zlib

    import numpy as np

    out = dict(_drawn_inputs(seed))
    spreads = {}
    factors = {'attn_sinks': 64.0,
     'ssd_conv_b': 5.304,
     'gdn_dt_bias': 33.688,
     'gdn_norm_w': 3.557,
     'norm_gain_2': 3.81,
     'q_gain_2': 8.0,
     'k_gain_2': 8.0,
     'ln_v_gain_2': 8.0,
     'ln_v_bias_2': 33.575,
     'b_spatial_2': 8.0,
     'b_merge_2': 8.0,
     'gdn_A_log': 8.0}
    for name, (base, spread) in spreads.items():
        noise = np.random.default_rng([zlib.crc32(name.encode()), seed]).standard_normal(out[name].shape)
        drawn = base * np.exp(spread * noise) if base else spread * noise
        out[name] = __import__('jax').numpy.asarray(drawn.astype(out[name].dtype))
    for name, factor in factors.items():
        out[name] = (out[name] * factor).astype(out[name].dtype)
    return out
```

```python
from contextlib import ExitStack

import numpy as np
import concourse.bass as bass
from concourse import mybir

F32 = mybir.dt.float32
F32R = mybir.dt.float32r
BF16 = mybir.dt.bfloat16
I32 = mybir.dt.int32
ALU = mybir.AluOpType
ACT = mybir.ActivationFunctionType
AX = mybir.AxisListType.X

P = 128
T = 1024
NT = T // P
D = 1024
KD = D // P
FF = 2816
NF = FF // P
EPS = 1e-6
NEG = -1e30
SWDGE_RING = 1024
SBUF_BASE = SWDGE_RING + 128

O_AQ, O_AK, O_AV, O_SZ, O_XBC, O_DT, O_QKV, O_GZ, O_B = 0, 256, 384, 512, 1024, 2048, 2056, 2824, 3080
O2_Q, O2_K, O2_V, O2_GA, O2_U, O2_VI, O2_GB, O2_M = 0, 512, 640, 768, 1280, 1792, 2304, 2816


def consts_of_shapes():
    i = np.arange(P)
    ident = np.eye(P)
    upper = (i[:, None] <= i[None, :]).astype(float)
    block = (i[:, None] // 64 == i[None, :] // 64).astype(float)
    levels = []
    for b in range(7):
        n = 1 << b
        m = ((i[:, None] // (2 * n) == i[None, :] // (2 * n)) & (i[:, None] // n % 2 == 1) & (i[None, :] // n % 2 == 0))
        levels.append(m.T if b == 0 else m)
    neg = np.where(upper > 0, 0.0, NEG)
    j = np.arange(2 * P)
    dist = np.abs(i[:, None] + P - j[None, :])
    seen = np.where(i[:, None] < 64, j[None, :] < 192, j[None, :] >= 64)
    alibi = [np.where(seen, -(2.0 ** (-2.0 * (h + 1))) * dist, NEG) for h in (0, 2, 1, 3)]
    c1 = np.concatenate([ident, upper, block, *levels, neg, *alibi], axis=1).astype(np.float32)
    t = np.arange(T)
    inv = (10000.0 ** (-np.arange(0, 32, 2, dtype=np.float32) / 32)).astype(np.float32)
    ang = np.stack([(t // 64).astype(np.float32)[:, None] * inv, (t % 64).astype(np.float32)[:, None] * inv], 1)
    cos, sin = np.cos(ang), np.sin(ang)
    ct = np.stack([cos, cos], 2).reshape(T, 64)
    st = np.stack([-sin, sin], 2).reshape(T, 64)
    two = [np.tile(m, (1, 2)).reshape(NT, P, 2 * 64).transpose(1, 0, 2).reshape(P, NT * P) for m in (ct, st)]
    return np.ascontiguousarray(c1), np.ascontiguousarray(np.concatenate(two, 1).astype(np.float32))


C_ID, C_UP, C_BLK, C_LV, C_NEG, C_ALI = 0, 128, 256, 384, 384 + 7 * 128, 512 + 7 * 128
C_END = C_ALI + 4 * 256


def weight_units():
    ws, units = [], []

    def add(name, kt, row, pieces, kinds):
        ws.append((name, kt, row, pieces))
        per = (1024 // kt) // P
        assert len(kinds) == per
        for s, kind in enumerate(kinds):
            units.append(dict(w=len(ws) - 1, kt=kt, sub=s, kind=kind, last=s == per - 1))

    for j in range(4):
        add("w_in", 8, 0, [(O_XBC + 128 * j, 128)], [("conv", j)])
    for j in range(4, 8):
        add("w_in", 8, 0, [(O_XBC + 128 * j, 128)], [("conv", j)])
    for j in range(6):
        add("w_in", 8, 0, [(O_QKV + 128 * j, 128)], [("conv", 8 + j)])
    for j in range(4):
        add("w_in", 8, 0, [(O_SZ + 128 * j, 128)], [("z", j)])
    for j in range(2):
        add("w_in", 8, 0, [(O_GZ + 128 * j, 128)], [("z", 4 + j)])
    for j in range(2):
        add("w_in", 8, 0, [(O_AQ + 64 * j, 64), (O_AQ + 64 * (j + 2), 64)], [("aq", j)])
    add("w_in", 8, 0, [(O_AK, 128)], [("ak", 0)])
    add("w_in", 8, 0, [(O_AV, 128)], [("av", 0)])
    for j in range(8):
        add("w_out", 8, 0, [(128 * j, 128)], [("wo", j)])
    groups = [(4 * g, min(4, NF - 4 * g)) for g in range((NF + 3) // 4)]

    def gate(f):
        add("ffn_w_gate", 8, 0, [(128 * f, 128)], [("gate", f)])

    def up(f):
        add("ffn_w_up", 8, 0, [(128 * f, 128)], [("up", f)])

    gate(0)
    for g, (f0, n) in enumerate(groups):
        up(f0)
        for f in range(f0 + 1, f0 + n):
            gate(f)
            up(f)
        if g + 1 < len(groups):
            gate(f0 + n)
        per = (1024 // n) // P
        for j in range(8 // per):
            add("ffn_w_down", n, f0, [(j * 1024 // n, 1024 // n)],
                [("down", (g, j * per + s)) for s in range(per)])
    for j in range(4):
        add("w_in_2", 8, 0, [(O2_Q + 64 * j, 64), (O2_Q + 64 * (j + 4), 64)], [("q2", j)])
    add("w_in_2", 8, 0, [(O2_K, 128)], [("q2", 4)])
    add("w_in_2", 8, 0, [(O2_V, 128)], [("v2", 0)])
    for o, kind in ((O2_VI, "vi"), (O2_GA, "ga"), (O2_U, "u2"), (O2_GB, "gb")):
        for j in range(4):
            add("w_in_2", 8, 0, [(o + 128 * j, 128)], [(kind, j)])
    for j in range(0, 8, 2):
        for s in range(2):
            add("w_in_2", 8, 0, [(O2_M + 128 * (j + s), 128)], [("sga", j + s)])
        for s in range(2):
            add("w_in_2", 8, 0, [(O2_M + 1024 + 128 * (j + s), 128)], [("sgb", j + s)])
        add("w_proj_attn_2", 4, 0, [(128 * j, 256)], [("ya", j), ("ya", j + 1)])
        add("w_proj_gmlp_2", 4, 0, [(128 * j, 256)], [("yb", j), ("yb", j + 1)])
    for j in range(8):
        add("w_out_2", 8, 0, [(128 * j, 128)], [("wo2", j)])
    return ws, units


def schedule(units):
    by = {u["kind"]: n for n, u in enumerate(units)}
    s, late = [], []

    def run(kinds, after=lambda kd: []):
        for kd in kinds:
            s.append(("unit", by[kd]))
            for it in [x for d, x in late if d <= 0]:
                s.append(it)
            late[:] = [(d - 1, x) for d, x in late if d > 0] + list(after(kd))

    def flush():
        for _, it in sorted(late, key=lambda x: x[0]):
            s.append(it)
        late.clear()

    s += [("cols", 0), ("norm", 0), ("small", 0)]
    run([("conv", j) for j in range(3)], lambda kd: [(0, ("convT", kd[1]))])
    s.append(("acs", 0))
    run([("conv", j) for j in range(3, 14)], lambda kd: [(0, ("convT", kd[1]))] if kd[1] not in (6, 7) else [])
    run([("z", j) for j in range(6)], lambda kd: [(0, ("zT", kd[1]))])
    run([("aq", 0), ("aq", 1), ("ak", 0)])
    run([("av", 0)], lambda kd: [(0, ("avT", 0))])
    flush()
    s.append(("prep", 0))
    s += [("att", c) for c in range(NT)]
    s += [("rec", c) for c in range(NT)]
    s.append(("load", 0))
    run([("wo", j) for j in range(8)], lambda kd: [(0, ("woT", kd[1]))])
    flush()
    s += [("resid", 0), ("norm", 1), ("load", 1)]
    s += [("unit", n) for n, u in enumerate(units) if u["kind"][0] in ("gate", "up", "down")]
    s += [("downT", 0), ("resid", 1), ("norm", 2), ("load", 2)]
    run([("q2", j) for j in range(5)], lambda kd: [(0, ("q2T", kd[1])), (1, ("q2B", kd[1]))])
    run([("v2", 0)], lambda kd: [(0, ("v2T", 0))])
    run([("vi", j) for j in range(4)], lambda kd: [(0, ("viT", kd[1]))])
    flush()
    s += [("load", 3), ("ln", 0)]
    rest = [(k, j) for k in ("ga", "u2", "gb") for j in range(4)]
    s.append(("a2s", 0))
    for n in range(NT * 8):
        if n + 1 < NT * 8:
            s.append(("a2s", n + 1))
        s.append(("a2p", n))
        if rest and (n in (0, 2, 4, 6) or (n > 8 and n % 6 == 0)):
            s.append(("unit", by[rest.pop(0)]))
        if n % 8 == 7:
            s.append(("a2t", n // 8))
    assert not rest
    s += [("sp", c) for c in range(NT)]
    s.append(("split4", 0))
    for j in range(0, 8, 2):
        run([("sga", j), ("sga", j + 1), ("sgb", j), ("sgb", j + 1), ("ya", j), ("ya", j + 1), ("yb", j), ("yb", j + 1)])
    s += [("splity", 0), ("load", 4)]
    run([("wo2", j) for j in range(8)], lambda kd: [(0, ("wo2T", kd[1]))])
    flush()
    s.append(("final", 0))
    return s


def products_of(item):
    kind, _ = item
    if kind == "rec":
        return (["bc0", "bc1", "bc2", "kT", "qT", "g", "kq0", "kq1", "xT", "yo"]
                + ["y1", "x1", "t1", "yd", "y2", "x2", "t2", "st"]
                + [f"{x}{b}" for b in (3, 4, 5) for x in "yxt"] + ["y6", "t6", "uw", "r1", "r2", "m0", "m1"])
    if kind == "att":
        return ["s0", "s1", "p0", "p1", "o", "t"]
    return list(range({"cols": 1, "norm": 16, "small": 1, "acs": 1, "convT": 2, "zT": 2, "avT": 2, "woT": 2,
                       "downT": 16, "q2T": 2, "q2B": 2, "v2T": 2, "viT": 2, "ln": 2, "a2s": 2, "a2p": 3, "a2t": 1,
                       "sp": 1, "wo2T": 2}.get(kind, 0)))


def build_program(nc, a, out):
    ws, units = weight_units()
    unit_of = {u["kind"]: n for n, u in enumerate(units)}
    last_unit_of = {u["w"]: n for n, u in enumerate(units) if u["last"]}
    sched = schedule(units)
    assert [x[1] for x in sched if x[0] == "unit"] == list(range(len(units)))
    prod, n = {}, 0
    for it in sched:
        for key in products_of(it):
            prod[it, key] = n
            n += 1
    stage_uses = {}
    for it in sched:
        if it[0] == "unit":
            kd = units[it[1]]["kind"]
            reader = {"conv": "convT", "z": "zT", "av": "avT", "wo": "woT", "q2": "q2T", "v2": "v2T", "vi": "viT",
                      "wo2": "wo2T"}.get(kd[0])
            if reader:
                stage_uses[kd] = (len(stage_uses), (reader, kd[1]))
    stage_reader = {m: r for m, r in stage_uses.values()}

    z_dram = nc.dram_tensor("z_spill", [T, 768], F32).ap()
    x2_dram = nc.dram_tensor("x2_spill", [T, D], F32).ap()

    ctx = ExitStack()
    with ctx:
        def sem(name):
            return ctx.enter_context(nc.semaphore(name))

        def sbuf(name, shape, kb, dt=F32):
            return nc.alloc_sbuf_tensor_at(name, [P] + list(shape), dt, offset=SBUF_BASE + int(kb * 1024))

        hT = [sbuf("h_hi", [KD, T], 0, F32R), sbuf("h_lo", [KD, T], 32, F32R)]
        raw = [sbuf(f"w_raw{i}", [1024], 64 + 4 * i) for i in range(4)]
        whi = [sbuf(f"w_hi{i}", [1024], 80 + 4 * i, F32R) for i in range(2)]
        wlo = [sbuf(f"w_lo{i}", [1024], 88 + 4 * i, F32R) for i in range(2)]
        con = sbuf("con", [C_END], 96)
        ident = con[:, C_ID:C_ID + P]
        upper = con[:, C_UP:C_UP + P]
        blk = con[:, C_BLK:C_BLK + P]
        identb = sbuf("identb", [P], 105.5, BF16)
        negb = sbuf("negb", [P], 105.75, BF16)
        cols = sbuf("cols", [112], 106)
        bias16 = sbuf("bias16", [16], 106.5)
        alog = sbuf("alog", [12], 106.5625)
        dskip = sbuf("dskip", [8], 106.625)
        sinkb = sbuf("sinkb", [4], 106.6875)
        ss = sbuf("ss", [NT], 106.75)
        rs = sbuf("rs", [NT], 106.8125)
        nv = sbuf("nv", [64], 106.875)
        nt_ = sbuf("nt_", [64], 107.125)
        mean = sbuf("mean", [NT], 107.375)
        a2m = sbuf("a2m", [8], 107.4375)
        a2s_ = sbuf("a2s_", [2, 2], 107.46875)
        a2r = sbuf("a2r", [2], 107.5)
        rr = sbuf("rr", [64], 107.75)
        diag = sbuf("diag", [NT, P], 218.75)

        xin = sbuf("xin", [NT, D], 108)
        nsq = sbuf("nsq", [D], 176)
        BC = sbuf("BC", [4, T], 108)
        xs = sbuf("xs", [NT, 512], 124)
        Bt = sbuf("Bt", [NT, 256], 140)
        qkv = sbuf("qkv", [NT, 768], 148)
        aqT = sbuf("aqT", [2, T], 172)
        akT = sbuf("akT", [2, P + T], 180)
        av = sbuf("av", [1 + NT, P], 189)
        da = sbuf("da", [NT, 12], 193.5)
        nacs = sbuf("nacs", [NT, 12], 193.875)
        eacs = sbuf("eacs", [NT, 12], 194.25)
        dts = sbuf("dts", [NT, 16], 194.625)
        beta = sbuf("beta", [NT, 4], 195.125)
        bge = sbuf("bge", [NT, 4], 195.25)
        cin = sbuf("cin", [3 + T], 196)
        cacc = [sbuf(f"cacc{i}", [T], 200.5 + 4 * i) for i in range(2)]
        zst = sbuf("zst", [2, 4, P], 208.5)
        sm = [sbuf(f"sm{i}", [NT, 16], 212.5 + 0.5 * i) for i in range(6)]
        w16r = sbuf("w16r", [KD, 16], 215.5)
        w16 = [sbuf("w16_hi", [KD, 16], 216, F32R), sbuf("w16_lo", [KD, 16], 216.5, F32R)]
        rows = sbuf("rows", [P], 217)
        easm = sbuf("easm", [12], 217.5)
        psq = sbuf("psq", [NT, 512], 196)

        asb = sbuf("asb", [4, 256], 196)
        apT = sbuf("apT", [4, 2, P], 200)
        atok = sbuf("atok", [256], 204)
        amx = sbuf("amx", [4], 205)
        anm = sbuf("anm", [4], 205.0625)
        ads = sbuf("ads", [4], 205.125)
        asum = sbuf("asum", [4], 205.1875)
        aden = sbuf("aden", [4], 205.25)

        E = sbuf("E", [12, P], 172)
        kTp = sbuf("kTp", [4, P], 178)
        kq = sbuf("kq", [2, 2, P], 180)
        SQ = sbuf("SQ", [4, 2, P], 182)
        X = sbuf("X", [4, P], 186)
        XT = sbuf("XT", [4, P], 188)
        Y = sbuf("Y", [4, P], 190)
        cd = sbuf("cd", [12], 192)
        cdc = sbuf("cdc", [2], 192.0625)
        nss = sbuf("nss", [6], 192.125)
        nrs = sbuf("nrs", [6], 192.1875)
        kbv = sbuf("kbv", [4, 256], 195.5)
        uw = sbuf("uw", [512], 199.5)
        vn = sbuf("vn", [256], 201.5)
        o1 = sbuf("o1", [256], 202.5)
        Sbd = sbuf("Sbd", [2, P], 203.5)
        tS = sbuf("tS", [2, P], 202.5)
        Sst = sbuf("Sst", [512], 204.5)
        xc = sbuf("xc", [2, 512], 206.5)
        mix = sbuf("mix", [768], 210.5)
        msq = sbuf("msq", [768], 213.5)
        zt = sbuf("zt", [768], 216.5)
        gmix = sbuf("gmix", [768], 219.5)

        mo = sbuf("mo", [NT, D], 108)
        x1 = sbuf("x1", [NT, D], 140)
        ost = [sbuf(f"ost{i}", [T], 172 + 4 * i) for i in range(2)]
        gbc = sbuf("gbc", [2, D], 180)
        fT = [sbuf("f_hi", [4, T], 108, F32R), sbuf("f_lo", [4, T], 124, F32R)]
        accT = sbuf("accT", [KD, T], 172)
        sg = [sbuf(f"sg{i}", [T], 204 + 4 * i) for i in range(2)]
        ft = sbuf("ft", [T], 212)
        fo = sbuf("fo", [NT, D], 108)
        rsq = sbuf("rsq", [D], 212)
        gbc2 = sbuf("gbc2", [D], 216)

        gaT = sbuf("gaT", [4, T], 108)
        uT = sbuf("uT", [4, T], 124)
        vv = sbuf("vv", [NT, 512], 140)
        qT2 = sbuf("qT2", [4, T], 156)
        kT2 = sbuf("kT2", [2, T], 172)
        v2k = sbuf("v2k", [NT, P], 180)
        st2 = [sbuf("st2_0", [T], 184), sbuf("st2_1", [T], 209)]
        tok = sbuf("tok", [NT, P], 188)
        rp1 = sbuf("rp1", [NT, P], 192)
        rp2 = sbuf("rp2", [NT, P], 205)
        rope = sbuf("rope", [2, NT, P], 196)
        qkg = sbuf("qkg", [2, 64], 204)
        gbt = sbuf("gbt", [T], 184)
        wsr = sbuf("wsr", [8, P], 188)
        wsT = sbuf("wsT", [8, P], 192)
        bsp = sbuf("bsp", [4, P], 196)
        lnp = sbuf("lnp", [2, 512], 198)
        lsq = sbuf("lsq", [512], 217)
        Pb = [sbuf(f"Pb{i}", [T], 205 + 4 * i) for i in range(2)]
        PT = sbuf("PT", [NT, P], 213)
        ot = sbuf("ot", [512], 217)
        spt = sbuf("spt", [4, P], 205)

        atT = [sbuf("at_hi", [4, T], 140, F32R), sbuf("at_lo", [4, T], 156, F32R)]
        gmT = [sbuf("gm_hi", [4, T], 172, F32R), sbuf("gm_lo", [4, T], 188, F32R)]
        yT = sbuf("yT", [KD, T], 108)
        sig = [[sbuf(f"sig{i}{k}", [T], 204 + 4 * (2 * i + k)) for k in range(2)] for i in range(2)]
        ob = sbuf("ob", [NT, D], 108)
        x2 = sbuf("x2", [NT, D], 140)
        fst = [sbuf(f"fst{i}", [T], 204 + 4 * i) for i in range(2)]
        fgb = sbuf("fgb", [D], 172)

        G = [ctx.enter_context(nc.psum_tensor(f"gemm{i}", [P, T], F32)) for i in range(2)]
        S = [ctx.enter_context(nc.psum_tensor(f"side{i}", [P, 512], F32)) for i in range(4)]

        con_loaded, small_loaded = sem("con_loaded"), sem("small_loaded")
        x_loaded = sem("x_loaded")
        raw_loaded = [sem(f"raw_loaded{i}") for i in range(4)]
        w_split = sem("w_split")
        pool_hi = sem("pool_hi")
        gemm_done = [sem(f"gemm_done{i}") for i in range(2)]
        gemm_read = [sem(f"gemm_read{i}") for i in range(2)]
        side_done = [sem(f"side_done{i}") for i in range(4)]
        side_read = [sem(f"side_read{i}") for i in range(4)]
        act_step, dve_step = sem("act_step"), sem("dve_step")
        N = {k: sem(k) for k in (
            "init_done", "ss_ready", "diag_ready", "hi_ready", "conv_acc", "conv_act", "w16_ready", "sm_abs",
            "sm_exp", "sm_arg", "beta_ready", "da_ready", "nacs_ready", "eacs_ready", "prep_done", "att_max",
            "att_exp", "att_out", "rec_kb", "rec_dec", "rec_x0", "rec_y", "rec_vn", "rec_S", "rec_mix",
            "resid_done", "staged", "f_mul", "f_hi", "f_lo", "rope_done", "gb_act", "gb_used", "mean_done",
            "ln_done", "a2_max", "a2_out", "split_hi", "split_lo", "sig_ready", "y_done", "yT_hi", "yT_lo",
            "final_sum", "final_done", "ak_done", "att_ready", "x0_ready", "y_ready")}
        z_out = [sem(f"z_out{i}") for i in range(2)]
        z_in, res_loaded, x2_out, gain_loaded, rope_loaded, ln_loaded, x2_in, out_stored = (
            sem(x) for x in ("z_in", "res_loaded", "x2_out", "gain_loaded", "rope_loaded", "ln_loaded", "x2_in",
                             "out_stored"))

        def gemm_product(eng, n):
            eng.wait_ge(gemm_done[n % 2], n // 2 + 1)

        def gemm_consumed(eng, n):
            eng.wait_ge(gemm_read[n % 2], n // 2 + 1)

        def side_product(eng, key):
            p = prod[key]
            eng.wait_ge(side_done[p % 4], p // 4 + 1)
            return S[p % 4]

        def side_consumed(eng, key):
            p = prod[key]
            eng.wait_ge(side_read[p % 4], p // 4 + 1)

        class Steps:

            def __init__(self, eng, own):
                self.eng, self.own, self.count = eng, own, {}

            def __call__(self, ins, name=None):
                s = N[name] if name else self.own
                self.count[name] = self.count.get(name, 0) + 1
                ins.then_inc(s, 1)
                self.eng.wait_ge(s, self.count[name])

            def frees(self, ins, key):
                p = prod[key]
                ins.then_inc(side_read[p % 4], 1)
                self.eng.wait_ge(side_read[p % 4], p // 4 + 1)

            def frees_gemm(self, ins, n):
                ins.then_inc(gemm_read[n % 2], 1)
                self.eng.wait_ge(gemm_read[n % 2], n // 2 + 1)

        block = ctx.enter_context(nc.Block())

        def hslice(c):
            return slice(c * P, (c + 1) * P)

        def widen(ap, n):
            return ap.unsqueeze(2).to_broadcast([P, ap.shape[1], n])

        def over(ap, m):
            return ap.unsqueeze(1).to_broadcast([P, m, ap.shape[1]])

        def stage_of(kd):
            m = stage_uses[kd][0]
            bufs = {"conv": cacc, "z": cacc, "av": cacc, "wo": ost, "wo2": fst}.get(kd[0], st2)
            return m, bufs[m % 2]

        def stage_free(eng, m):
            r = stage_reader.get(m - 2)
            if r is not None and (r, 1) in prod:
                p = prod[r, 1]
                eng.wait_ge(side_done[p % 4], p // 4 + 1)

        tok_items = {"convT", "zT", "avT", "woT", "v2T", "viT", "wo2T", "q2T"}

        def tok_dest(it, hf):
            kind, j = it
            t = slice(4 * hf, 4 * hf + 4)
            if kind == "convT":
                if j < 4:
                    return xs[:, t, hslice(j)]
                return Bt[:, t, hslice(j - 4)] if j < 6 else qkv[:, t, hslice(j - 8)]
            if kind == "zT":
                return zst[:, hf]
            if kind == "avT":
                return av[:, 1 + 4 * hf:5 + 4 * hf, :]
            return {"woT": mo, "viT": vv, "wo2T": ob}[kind][:, t, hslice(j)] if kind in ("woT", "viT", "wo2T") else \
                {"v2T": v2k, "q2T": tok}[kind][:, t, :]

        norm_src = [xin, x1, x1]
        sq_scratch = [nsq, rsq, rsq]
        act_ready = {("conv", 0): [("norm", 0)], ("gate", 0): [("norm", 1)], ("q2", 0): [("norm", 2)]}

        @block.sync
        def _(sp):
            def bcast(ap, n, off=0):
                return bass.AP(ap.tensor, ap.offset + off, [[0, P], [1, n]])

            for c in range(NT):
                sp.dma_start(xin[:, c, :], a["x"][hslice(c), :]).then_inc(x_loaded, 16)
            sp.dma_start(con[:], a["con1"]).then_inc(con_loaded, 16)
            for r0, src in ((0, a["ssd_conv_w"].rearrange("i (j p) -> (i j) p", p=P)),
                            (32, a["gdn_conv_w"].rearrange("i (j p) -> (i j) p", p=P)),
                            (56, a["ssd_conv_b"].rearrange("(j p) -> j p", p=P)),
                            (64, a["pre_mix_norm"].rearrange("(j p) -> j p", p=P)),
                            (72, a["pre_ffn_norm"].rearrange("(j p) -> j p", p=P)),
                            (80, a["norm_gain_2"].rearrange("(j p) -> j p", p=P)),
                            (88, a["b_merge_2"].rearrange("i (j p) -> (i j) p", p=P))):
                sp.dma_start(rows[r0:r0 + src.shape[0], :], src).then_inc(con_loaded, 16)
            w = a["w_in"].rearrange("(k p) n -> p k n", p=P)
            sp.dma_start(w16r[:, :, 0:8], w[:, :, O_DT:O_DT + 8]).then_inc(small_loaded, 16)
            sp.dma_start(w16r[:, :, 8:16], w[:, :, O_B:O_B + 8]).then_inc(small_loaded, 16)
            sp.dma_start(bias16[:, 0:8], bcast(a["ssd_dt_bias"], 8)).then_inc(small_loaded, 16)
            sp.dma_start(bias16[:, 12:16], bcast(a["gdn_dt_bias"], 4)).then_inc(small_loaded, 16)
            sp.dma_start(alog[:, 0:8], bcast(a["ssd_A_log"], 8)).then_inc(small_loaded, 16)
            sp.dma_start(alog[:, 8:12], bcast(a["gdn_A_log"], 4)).then_inc(small_loaded, 16)
            sp.dma_start(dskip[:], bcast(a["ssd_D"], 8)).then_inc(small_loaded, 16)
            s = a["attn_sinks"]
            for p in range(2):
                sp.dma_start(sinkb[:, 2 * p:2 * p + 2], bass.AP(s.tensor, s.offset + p, [[0, P], [2, 2]]), allow_slow_non_contiguous=True).then_inc(small_loaded, 16)
            for w, (name, kt, row, pieces) in enumerate(ws):
                if w >= 4:
                    sp.wait_ge(w_split, w - 3)
                src = a[name].rearrange("(k p) n -> p k n", p=P)
                dst = raw[w % 4][:].rearrange("p (k n) -> p k n", k=kt)
                o = 0
                for c0, width in pieces:
                    sp.dma_start(dst[:, :, o:o + width], src[:, row:row + kt, c0:c0 + width]).then_inc(raw_loaded[w % 4], 16)
                    o += width
            sp.wait_ge(out_stored, 16 * NT)

        @block.gpsimd
        def _(pool):
            pieces_so_far = [0] * 4
            for w, (name, kt, row, pieces) in enumerate(ws):
                pieces_so_far[w % 4] += len(pieces)
                pool.wait_ge(raw_loaded[w % 4], 16 * pieces_so_far[w % 4])
                if w >= 2:
                    gemm_product(pool, last_unit_of[w - 2])
                nc.gpsimd.tensor_scalar(whi[w % 2][:], raw[w % 4][:], 1.0, 0.0, ALU.mult, ALU.add).then_inc(pool_hi, 1)
                pool.wait_ge(pool_hi, w + 1)
                nc.gpsimd.tensor_tensor(wlo[w % 2][:], raw[w % 4][:], whi[w % 2][:], ALU.subtract).then_inc(w_split, 1)
                pool.wait_ge(w_split, w + 1)

        @block.tensor
        def _(pe):
            mm, tr = nc.tensor.matmul, nc.tensor.transpose

            def bank(key):
                p = prod[key]
                if p >= 4:
                    pe.wait_ge(side_read[p % 4], p // 4)
                return S[p % 4]

            def done(last, key):
                last.then_inc(side_done[prod[key] % 4], 1)

            def unit(n):
                u = units[n]
                kd, kt, w = u["kind"], u["kt"], u["w"]
                pe.wait_ge(w_split, w + 1)
                if n >= 2:
                    pe.wait_ge(gemm_read[n % 2], n // 2)
                act = {"down": fT, "ya": atT, "yb": gmT}.get(kd[0], hT)
                if kd[0] == "down":
                    pe.wait_ge(N["f_lo"], min(4 * kd[1][0] + 4, NF))
                if kd[0] in ("ya", "yb"):
                    pe.wait_ge(N["split_lo"], 4 if kd[0] == "ya" else 8)
                hi = whi[w % 2][:].rearrange("p (k n) -> p k n", k=kt)
                lo = wlo[w % 2][:].rearrange("p (k n) -> p k n", k=kt)
                m = slice(u["sub"] * P, u["sub"] * P + P)
                for hf in range(2):
                    if kd in act_ready:
                        for k in range(4, 8):
                            side_consumed(pe, (act_ready[kd][0], hf * 8 + k))
                    if kd == ("wo", 0):
                        side_consumed(pe, (("rec", 4 * hf + 3), "m0"))
                        side_consumed(pe, (("rec", 4 * hf + 3), "m1"))
                    t = slice(hf * 512, hf * 512 + 512)
                    o = G[n % 2][:, t]
                    for k in range(kt):
                        if kd == ("wo2", 0) and hf == 0:
                            pe.wait_ge(N["yT_lo"], k + 1)
                        mm(o, hi[:, k, m], act[0][:, k, t], start=k == 0, stop=False)
                        mm(o, hi[:, k, m], act[1][:, k, t], start=False, stop=False)
                        last = mm(o, lo[:, k, m], act[0][:, k, t], start=False, stop=k == kt - 1)
                last.then_inc(gemm_done[n % 2], 1)

            def transposed(it, blocks):
                for h in range(2):
                    b = bank((it, h))
                    for i, x in enumerate(blocks(h)):
                        last = tr(b[:, hslice(i)], x, ident)
                    done(last, (it, h))

            for it in sched:
                kind, j = it
                if kind == "unit":
                    unit(j)
                elif kind == "cols":
                    pe.wait_ge(con_loaded, 16 * 8)
                    b = bank((it, 0))
                    done(tr(b[:, 0:104], rows[0:104, :], ident[0:104, 0:104]), (it, 0))
                elif kind == "norm":
                    pe.wait_ge(N["diag_ready"], j + 1)
                    for hf in range(2):
                        for k in range(KD):
                            key = (it, hf * 8 + k)
                            b = bank(key)
                            for i in range(4):
                                c = 4 * hf + i
                                last = mm(b[:, hslice(i)], norm_src[j][:, c, hslice(k)], diag[:, c, :], start=True, stop=True)
                            done(last, key)
                elif kind == "small":
                    pe.wait_ge(N["w16_ready"], 1)
                    b = bank((it, 0))
                    for k in range(12, 16):
                        side_consumed(pe, (("norm", 0), k))
                    for c in range(NT):
                        for k in range(KD):
                            for x, (h, w) in enumerate(((0, 0), (1, 0), (0, 1))):
                                last = mm(b[:, 16 * c:16 * c + 16], hT[h][:, k, hslice(c)], w16[w][:, k, :],
                                          start=k == 0 and x == 0, stop=k == KD - 1 and x == 2)
                    done(last, (it, 0))
                elif kind == "acs":
                    pe.wait_ge(N["da_ready"], 1)
                    b = bank((it, 0))
                    done(mm(b[:, 0:96], upper, da[:].rearrange("p c h -> p (c h)"), start=True, stop=True), (it, 0))
                elif kind in ("convT", "zT", "avT", "v2T", "viT", "woT", "wo2T", "q2T"):
                    kd = {"convT": "conv", "zT": "z", "avT": "av", "v2T": "v2", "viT": "vi", "woT": "wo",
                          "wo2T": "wo2", "q2T": "q2"}[kind], j
                    src = stage_of(kd)[1]
                    if kind == "convT":
                        pe.wait_ge(N["conv_act"], j + 1)
                        if j in (4, 5):
                            src = BC[:, j - 4, :]
                    else:
                        gemm_consumed(pe, unit_of[kd])
                    transposed(it, lambda h, src=src: [src[:, (4 * h + i) * P:(4 * h + i + 1) * P] for i in range(4)])
                elif kind == "att":
                    c = j
                    if c == 0:
                        for kd in (("aq", 0), ("aq", 1), ("ak", 0)):
                            gemm_consumed(pe, unit_of[kd])
                        side_consumed(pe, (("avT", 0), 0))
                        side_consumed(pe, (("avT", 0), 1))
                    for p in range(2):
                        b = bank((it, f"s{p}"))
                        for kv in range(2):
                            last = mm(b[:, kv * 256:kv * 256 + 256], aqT[:, p, hslice(c)], akT[:, kv, c * P:c * P + 2 * P],
                                      start=True, stop=True)
                        done(last, (it, f"s{p}"))
                    pe.wait_ge(N["att_exp"], c + 1)
                    for p in range(2):
                        b = bank((it, f"p{p}"))
                        for i in range(4):
                            last = tr(b[:, hslice(i)], asb[:, 2 * p + i // 2, hslice(i % 2)], ident)
                        done(last, (it, f"p{p}"))
                    side_consumed(pe, (it, "p0"))
                    side_consumed(pe, (it, "p1"))
                    b = bank((it, "o"))
                    for i in range(4):
                        p, kv = i // 2, i % 2
                        h = p + 2 * kv
                        for s in range(2):
                            last = mm(b[:, h * 64:h * 64 + 64], apT[:, i, s, :], av[:, c + s, kv * 64:kv * 64 + 64],
                                      start=s == 0, stop=s == 1)
                    done(last, (it, "o"))
                    pe.wait_ge(N["att_out"], c + 1)
                    b = bank((it, "t"))
                    for i in range(2):
                        last = tr(b[:, hslice(i)], atok[:, hslice(i)], ident)
                    done(last, (it, "t"))
                elif kind == "rec":
                    c = j
                    for key in products_of(it):
                        b = bank((it, key))
                        if key[:2] == "bc":
                            i = int(key[2])
                            mm(b[:].rearrange("p (h n) -> p h n", h=4), identb[:], over(negb[:], 4), start=True, stop=False)
                            for h in range(4):
                                last = mm(b[:, hslice(h)], da[:, c, 4 * i + h:4 * i + h + 1].to_broadcast([P, P]), upper,
                                          start=False, stop=h == 3)
                        elif key == "kT":
                            pe.wait_ge(N["rec_kb"], c + 1)
                            for p in range(2):
                                tr(b[:, hslice(p)], qkv[:, c, 256 + p * P:256 + (p + 1) * P], ident)
                            for p in range(2):
                                last = tr(b[:, hslice(2 + p)], kbv[:, 0, hslice(p)], ident)
                        elif key == "qT":
                            for p in range(2):
                                last = tr(b[:, hslice(p)], qkv[:, c, hslice(p)], ident)
                        elif key == "g":
                            for g in range(2):
                                last = mm(b[:, hslice(g)], BC[:, g, hslice(c)], BC[:, 2 + g, hslice(c)], start=True, stop=True)
                        elif key[:2] == "kq":
                            p = int(key[2])
                            if p == 0:
                                side_consumed(pe, (it, "kT"))
                                side_consumed(pe, (it, "qT"))
                            for h in range(2):
                                last = mm(b[:, h * 256:h * 256 + 256], kTp[:, 2 * p + h, :],
                                          kq[:, p, :, :].rearrange("p a n -> p (a n)"), start=True, stop=True)
                        elif key == "xT":
                            pe.wait_ge(N["rec_x0"], c + 1)
                            for h in range(4):
                                last = tr(b[:, hslice(h)], XT[:, h, :], ident)
                        elif key == "yo":
                            if c > 0:
                                side_consumed(pe, (("rec", c - 1), "st"))
                            else:
                                pe.wait_ge(N["init_done"], 2)
                            for g in range(2):
                                last = mm(b[:, g * 256:g * 256 + 256], BC[:, 2 + g, hslice(c)], Sst[:, g * 256:g * 256 + 256],
                                          start=True, stop=True)
                        elif key == "yd":
                            side_consumed(pe, (it, "g"))
                            pe.wait_ge(N["rec_dec"], c + 1)
                            for h in range(8):
                                last = mm(b[:, h * 64:h * 64 + 64], E[:, h, :], xc[:, 0, h * 64:h * 64 + 64], start=True, stop=True)
                        elif key == "st":
                            for g in range(2):
                                last = mm(b[:, g * 256:g * 256 + 256], Bt[:, c, hslice(g)], xc[:, 1, g * 256:g * 256 + 256],
                                          start=True, stop=True)
                        elif key[0] == "y":
                            lv = int(key[1])
                            side_consumed(pe, (it, "xT" if lv == 1 else f"x{lv - 1}"))
                            for h in range(4):
                                last = mm(b[:, hslice(h)], SQ[:, h, 0, :], X[:, h, :], start=True, stop=True)
                        elif key[0] == "x":
                            lv = int(key[1])
                            side_consumed(pe, (it, f"y{lv}"))
                            if lv > 1:
                                side_consumed(pe, (it, f"t{lv - 1}"))
                            for h in range(4):
                                last = mm(b[:, hslice(h)], XT[:, h, :], Y[:, h, :], start=True, stop=True)
                        elif key[0] == "t":
                            lv = int(key[1])
                            side_consumed(pe, (it, f"y{lv}"))
                            if lv > 1:
                                side_consumed(pe, (it, f"t{lv - 1}"))
                            for h in range(4):
                                last = mm(b[:, hslice(h)], Y[:, h, :], XT[:, h, :], start=True, stop=True)
                        elif key == "uw":
                            side_consumed(pe, (it, "t6"))
                            for h in range(4):
                                mm(b[:, h * 64:h * 64 + 64], XT[:, h, :], kbv[:, 1, h * 64:h * 64 + 64], start=True, stop=True)
                            for h in range(4):
                                r = 64 * (h % 2)
                                last = mm(b[r:r + 64, 256 + (h // 2) * P:256 + (h // 2) * P + P], kbv[:, 2, h * 64:h * 64 + 64],
                                          XT[:, h, :], start=True, stop=True)
                        elif key == "r1":
                            side_consumed(pe, (it, "uw"))
                            if c > 0:
                                pe.wait_ge(N["rec_S"], c)
                            for p in range(2):
                                mm(b[:, hslice(p)], uw[:, 256 + p * P:256 + (p + 1) * P], Sbd[:, p, :], start=True, stop=True)
                            for p in range(2):
                                last = mm(b[:, hslice(2 + p)], kq[:, p, 1, :], Sbd[:, p, :], start=True, stop=True)
                        elif key == "r2":
                            pe.wait_ge(N["rec_vn"], c + 1)
                            for h in range(4):
                                mm(b[:, h * 64:h * 64 + 64], SQ[:, h, 1, :], vn[:, h * 64:h * 64 + 64], start=True, stop=True)
                            for p in range(2):
                                last = mm(b[:, hslice(2 + p)], kbv[:, 3, hslice(p)], vn[:, hslice(p)], start=True, stop=True)
                        elif key in ("m0", "m1"):
                            pe.wait_ge(N["rec_mix"], c + 1)
                            for i in range(4 if key == "m0" else 2):
                                o = (0 if key == "m0" else 512) + i * P
                                last = tr(b[:, hslice(i)], mix[:, o:o + P], ident)
                        done(last, (it, key))
                elif kind == "downT":
                    gemm_consumed(pe, unit_of["down", (5, 6)])
                    gemm_consumed(pe, unit_of["down", (5, 7)])
                    for c in range(NT):
                        for hf in range(2):
                            key = (it, 2 * c + hf)
                            b = bank(key)
                            for i in range(4):
                                last = tr(b[:, hslice(i)], accT[:, 4 * hf + i, hslice(c)], ident)
                            done(last, key)
                elif kind == "q2B":
                    pe.wait_ge(N["rope_done"], j + 1)
                    transposed(it, lambda h: [rp1[:, 4 * h + i, :] for i in range(4)])
                elif kind == "ln":
                    pe.wait_ge(ln_loaded, 16 * 5)
                    transposed(it, lambda h: [wsr[:, 4 * h + i, :] for i in range(4)])
                elif kind == "a2s":
                    c, h = j // 8, j % 8
                    if j == 0:
                        for q in range(5):
                            for s in range(2):
                                side_consumed(pe, (("q2B", q), s))
                    for s in range(2):
                        b = bank((it, s))
                        done(mm(b[:], qT2[:, h % 4, hslice(c)], kT2[:, h // 4, s * 512:s * 512 + 512], start=True, stop=True), (it, s))
                elif kind == "a2p":
                    c, h = j // 8, j % 8
                    for s in range(2):
                        side_consumed(pe, (("a2s", j), s))
                    for s in range(2):
                        b = bank((it, s))
                        for i in range(4):
                            last = tr(b[:, hslice(i)], Pb[j % 2][:, (4 * s + i) * P:(4 * s + i + 1) * P], ident)
                        done(last, (it, s))
                    for s in range(2):
                        side_consumed(pe, (it, s))
                    b = bank((it, 2))
                    for i in range(NT):
                        last = mm(b[:, 0:P], PT[:, i, :], v2k[:, i, :], start=i == 0, stop=i == NT - 1)
                    done(last, (it, 2))
                elif kind == "a2t":
                    pe.wait_ge(N["a2_out"], 8 * j + 8)
                    b = bank((it, 0))
                    for i in range(4):
                        last = tr(b[:, hslice(i)], ot[:, hslice(i)], ident)
                    done(last, (it, 0))
                elif kind == "sp":
                    if j == 0:
                        pe.wait_ge(N["ln_done"], 1)
                        side_consumed(pe, (("ln", 0), 0))
                        side_consumed(pe, (("ln", 0), 1))
                    b = bank((it, 0))
                    for g in range(8):
                        r = 64 * (g % 2)
                        last = mm(b[r:r + 64, hslice(g // 2)], vv[:, j, g * 64:g * 64 + 64], wsT[:, g, :], start=True, stop=True)
                    done(last, (it, 0))

        @block.scalar
        def _(act):
            step = Steps(act, act_step)
            af = nc.scalar.activation

            def tokens_copied(it, hf):
                b = side_product(act, (it, hf))
                if it[0] == "zT" and it[1] > 0:
                    act.wait_ge(z_out[hf], 16 * it[1])
                step.frees(af(tok_dest(it, hf), b[:].rearrange("p (c n) -> p c n", c=4), ACT.Copy), (it, hf))

            def z_store(it, hf):
                j = it[1]
                dst = z_dram[hf * 512:hf * 512 + 512, hslice(j)].rearrange("(c p) n -> p c n", p=P)
                act.dma_start(dst, zst[:, hf]).then_inc(z_out[hf], 16)

            def squares(src, n, scratch):
                for c in range(NT):
                    ins = af(scratch, src[:, c, :], ACT.Square, accum_out=ss[:, c:c + 1])
                    step(ins, "ss_ready" if c == NT - 1 else None)

            def unit(n):
                kd = units[n]["kind"]
                kind, j = kd
                g = G[n % 2]
                if kind == "conv":
                    m, buf = stage_of(kd)
                    if j > 0:
                        act.wait_ge(N["conv_acc"], j)
                    gemm_product(act, n)
                    stage_free(act, m)
                    bcol, wcol = (56 + j, 24 + j) if j < 8 else (104, 50 + j - 8)
                    step(af(cin[:, 3:3 + T], g[:], ACT.Copy))
                    step.frees_gemm(af(buf[:], g[:], ACT.Identity, bias=cols[:, bcol:bcol + 1], scale=cols[:, wcol:wcol + 1]), n)
                    act.wait_ge(N["conv_acc"], j + 1)
                    step(af(BC[:, j - 4, :] if 4 <= j < 8 else buf[:], buf[:], ACT.Silu), "conv_act")
                elif kind in ("z", "av", "wo", "q2", "v2", "vi", "wo2"):
                    m, buf = stage_of(kd)
                    gemm_product(act, n)
                    stage_free(act, m)
                    f = {"z": ACT.Silu, "vi": ACT.Gelu_apprx_tanh}.get(kind, ACT.Copy)
                    step.frees_gemm(af(buf[:], g[:], f), n)
                elif kind == "aq":
                    gemm_product(act, n)
                    step.frees_gemm(af(aqT[:, j, :], g[:], ACT.Copy), n)
                elif kind == "ak":
                    gemm_product(act, n)
                    step(af(akT[0:64, 0, P:], g[0:64, :], ACT.Copy))
                    step.frees_gemm(af(akT[64:P, 1, P:], g[64:P, :], ACT.Copy), n)
                elif kind == "gate":
                    gemm_product(act, n)
                    if j >= 2:
                        gemm_consumed(act, unit_of["up", j - 2])
                    step.frees_gemm(af(sg[j % 2][:], g[:], ACT.Silu), n)
                elif kind == "up":
                    gemm_consumed(act, n)
                    step(af(fT[0][:, j % 4, :], ft[:], ACT.Copy), "f_hi")
                elif kind == "down" and j[0] == 0:
                    gemm_product(act, n)
                    step.frees_gemm(af(accT[:, j[1], :], g[:], ACT.Copy), n)
                elif kind in ("ga", "u2"):
                    gemm_product(act, n)
                    dst, f = (gaT, ACT.Silu) if kind == "ga" else (uT, ACT.Gelu_apprx_tanh)
                    step.frees_gemm(af(dst[:, j, :], g[:], f), n)
                elif kind == "gb":
                    gemm_product(act, n)
                    if j > 0:
                        act.wait_ge(N["gb_used"], j)
                    step.frees_gemm(af(gbt[:], g[:], ACT.Silu), n)
                elif kind in ("sga", "sgb"):
                    gemm_product(act, n)
                    i = 0 if kind == "sga" else 1
                    if j >= 2:
                        act.wait_ge(N["y_done"], j - 1)
                    step.frees_gemm(af(sig[i][j % 2][:], g[:], ACT.Sigmoid, bias=cols[:, 88 + 8 * i + j:89 + 8 * i + j]), n)

            for it in sched:
                kind, j = it
                if kind == "unit":
                    unit(j)
                elif kind == "norm":
                    if j == 0:
                        act.wait_ge(x_loaded, 16 * NT)
                        act.wait_ge(N["init_done"], 1)
                    else:
                        act.wait_ge(N["resid_done"], j)
                    squares(norm_src[j], D, sq_scratch[j][:])
                    for hf in range(2):
                        for k in range(KD):
                            b = side_product(act, (it, hf * 8 + k))
                            g0 = 64 + 8 * j + k
                            step(af(hT[0][:, k, hf * 512:hf * 512 + 512], b[:], ACT.Identity, scale=cols[:, g0:g0 + 1]), "hi_ready")
                elif kind == "small":
                    act.wait_ge(small_loaded, 16 * 9)
                    step(af(easm[:], alog[:], ACT.Exp))
                    act.wait_ge(N["sm_abs"], 1)
                    step(af(sm[2][:], sm[1][:], ACT.Exp, scale=-1.0), "sm_exp")
                elif kind == "acs":
                    act.wait_ge(N["sm_arg"], 1)
                    step(af(beta[:], sm[3][:, :, 8:12], ACT.Exp), "beta_ready")
                    act.wait_ge(N["nacs_ready"], 1)
                    step(af(eacs[:], nacs[:], ACT.Exp, scale=-1.0), "eacs_ready")
                elif kind in tok_items:
                    tokens_copied(it, 0)
                    if kind == "zT":
                        z_store(it, 0)
                        side_consumed(act, (it, 1))
                        z_store(it, 1)
                elif kind == "att":
                    act.wait_ge(N["att_max"], j + 1)
                    for i in range(4):
                        step(af(asb[:, i, :], asb[:, i, :], ACT.Exp, bias=anm[:, i:i + 1], accum_out=asum[:, i:i + 1]))
                    step(af(ads[:], ads[:], ACT.Exp), "att_exp")
                    b = side_product(act, (it, "p0"))
                    step.frees(af(apT[:, 0:2], b[:].rearrange("p (i s n) -> p i s n", i=2, s=2), ACT.Copy), (it, "p0"))
                    b = side_product(act, (it, "t"))
                    step(af(hT[0][:, 0:2, hslice(j)], b[:, 0:256].rearrange("p (i n) -> p i n", i=2), ACT.Copy), "hi_ready")
                elif kind == "rec":
                    c = j
                    if c == 0:
                        act.wait_ge(z_out[0], 16 * 6)
                        act.wait_ge(z_out[1], 16 * 6)
                        act.wait_ge(N["init_done"], 2)
                        src = a["ssd_norm_w"]
                        act.dma_start(gmix[:, 0:512], bass.AP(src.tensor, src.offset, [[0, P], [1, 512]])).then_inc(gain_loaded, 16)
                        src = a["gdn_norm_w"]
                        act.dma_start(gmix[:, 512:768].rearrange("p (h d) -> p h d", h=4),
                                      bass.AP(src.tensor, src.offset, [[0, P], [0, 4], [1, 64]])).then_inc(gain_loaded, 16)
                    act.dma_start(zt[:], z_dram[hslice(c), :]).then_inc(z_in, 16)
                    for i in range(3):
                        b = side_product(act, (it, f"bc{i}"))
                        for h in range(4):
                            step(af(E[:, 4 * i + h, :], b[:, hslice(h)], ACT.Exp, bias=nacs[:, c, 4 * i + h:4 * i + h + 1]))
                        step.frees(af(cd[:, 4 * i:4 * i + 4], b[:].rearrange("p (h n) -> p h n", h=4)[:, :, P - 1], ACT.Exp), (it, f"bc{i}"))
                    b = side_product(act, (it, "kT"))
                    v = b[:].rearrange("p (i n) -> p i n", i=4)
                    kv = kTp[:].rearrange("p (a b) n -> p a b n", b=2)
                    step(af(kv[0:64, :, 0, :], v[0:64, 0:2, :], ACT.Copy))
                    step(af(kv[64:P, :, 1, :], v[64:P, 0:2, :], ACT.Copy))
                    step.frees(af(kq[:, :, 0, :], v[:, 2:4, :], ACT.Copy), (it, "kT"))
                    b = side_product(act, (it, "xT"))
                    step.frees(af(X[:], b[:].rearrange("p (i n) -> p i n", i=4), ACT.Copy), (it, "xT"))
                    b = side_product(act, (it, "uw"))
                    step.frees(af(uw[:], b[:], ACT.Copy), (it, "uw"))
                    for key, k0, n in (("m0", 2, 4), ("m1", 6, 2)):
                        b = side_product(act, (it, key))
                        step(af(hT[0][:, k0:k0 + n, hslice(c)], b[:, 0:n * P].rearrange("p (i n) -> p i n", i=n), ACT.Copy), "hi_ready")
                elif kind == "load":
                    if j == 0:
                        side_consumed(act, (("rec", NT - 1), "m1"))
                        act.dma_start(x1[:], a["x"].rearrange("(c p) n -> p c n", p=P)).then_inc(res_loaded, 16)
                        for i, name in ((0, "post_mix_norm"),):
                            src = a[name]
                            act.dma_start(gbc[:, i, :], bass.AP(src.tensor, src.offset, [[0, P], [1, D]])).then_inc(res_loaded, 16)
                    elif j == 1:
                        pass
                    elif j == 2:
                        act.dma_start(x2_dram.rearrange("(c p) n -> p c n", p=P), x1[:]).then_inc(x2_out, 16)
                        act.dma_start(rope[:].rearrange("p a c n -> p (a c n)"), a["con2"]).then_inc(rope_loaded, 16)
                        for i, name in enumerate(("q_gain_2", "k_gain_2")):
                            src = a[name]
                            act.dma_start(qkg[:, i, :], bass.AP(src.tensor, src.offset, [[0, P], [1, 64]])).then_inc(rope_loaded, 16)
                    elif j == 3:
                        for q in range(5):
                            side_consumed(act, (("q2B", q), 1))
                        for v in range(4):
                            for h in range(2):
                                side_consumed(act, (("viT", v), h))
                        act.dma_start(wsr[:], a["w_spatial_2"].rearrange("g i j -> i g j")).then_inc(ln_loaded, 16)
                        src = a["b_spatial_2"]
                        for h in range(2):
                            act.dma_start(bsp[64 * h:64 * h + 64], bass.AP(src.tensor, src.offset + h * P, [[0, 64], [2 * P, 4], [1, P]])).then_inc(ln_loaded, 16)
                        for i, name in enumerate(("ln_v_gain_2", "ln_v_bias_2")):
                            src = a[name]
                            act.dma_start(lnp[:, i, :], bass.AP(src.tensor, src.offset, [[0, P], [1, 512]])).then_inc(ln_loaded, 16)
                    elif j == 4:
                        gemm_consumed(act, unit_of["yb", 7])
                        gemm_consumed(act, unit_of["yb", 6])
                        act.dma_start(x2[:], x2_dram.rearrange("(c p) n -> p c n", p=P)).then_inc(x2_in, 16)
                        src = a["final_gain_2"]
                        act.dma_start(fgb[:], bass.AP(src.tensor, src.offset, [[0, P], [1, D]])).then_inc(x2_in, 16)
                elif kind == "resid":
                    if j == 0:
                        for h in range(2):
                            side_consumed(act, (("woT", 7), h))
                    else:
                        for k in range(12, 16):
                            side_consumed(act, (("downT", 0), k))
                        src = a["post_ffn_norm"]
                        act.dma_start(gbc2[:], bass.AP(src.tensor, src.offset, [[0, P], [1, D]])).then_inc(gain_loaded, 16)
                    squares(mo if j == 0 else fo, D, rsq[:])
                elif kind == "downT":
                    for c in range(NT):
                        b = side_product(act, (it, 2 * c))
                        step.frees(af(fo[:, c, 0:512], b[:], ACT.Copy), (it, 2 * c))
                elif kind == "q2B":
                    if j == 0:
                        act.wait_ge(x2_out, 16)
                    b = side_product(act, (it, 0))
                    if j < 4:
                        step.frees(af(qT2[:, j, 0:512], b[:], ACT.Copy), (it, 0))
                    else:
                        step(af(kT2[0:64, 0, 0:512], b[0:64, :], ACT.Copy))
                        step.frees(af(kT2[64:P, 1, 0:512], b[64:P, :], ACT.Copy), (it, 0))
                elif kind == "ln":
                    b = side_product(act, (it, 0))
                    step.frees(af(wsT[:, 0:4], b[:].rearrange("p (i n) -> p i n", i=4), ACT.Copy), (it, 0))
                    act.wait_ge(N["mean_done"], 1)
                    squares(vv, 512, lsq[:])
                elif kind == "a2s":
                    act.wait_ge(N["a2_max"], j + 1)
                    if j >= 2:
                        side_product(act, (("a2p", j - 2), 1))
                    for s in range(2):
                        b = side_product(act, (it, s))
                        step.frees(af(Pb[j % 2][:, s * 512:s * 512 + 512], b[:], ACT.Exp, bias=a2m[:, 4 + j % 2:5 + j % 2], scale=0.125,
                                      accum_out=a2s_[:, j % 2, s:s + 1]), (it, s))
                elif kind == "a2p":
                    if j >= 1:
                        side_product(act, (("a2p", j - 1), 2))
                    b = side_product(act, (it, 0))
                    step.frees(af(PT[:, 0:4, :], b[:].rearrange("p (i n) -> p i n", i=4), ACT.Copy), (it, 0))
                elif kind in ("split4", "splity"):
                    for k in range(8):
                        if kind == "split4":
                            if k == 0:
                                side_consumed(act, (("sp", 7), 0))
                                act.wait_ge(N["y_ready"], 1)
                            step(af((atT if k < 4 else gmT)[0][:, k % 4, :], (gaT if k < 4 else uT)[:, k % 4, :], ACT.Copy), "split_hi")
                        else:
                            if k == 0:
                                act.wait_ge(N["y_done"], 8)
                            step(af(hT[0][:, k, :], yT[:, k, :], ACT.Copy), "yT_hi")
                elif kind == "final":
                    act.wait_ge(N["final_sum"], 1)
                    squares(ob, D, fst[0][:])
                    for c in range(NT):
                        act.wait_ge(N["final_done"], c + 1)
                        act.dma_start(out[hslice(c), :], ob[:, c, :]).then_inc(out_stored, 16)

        @block.vector
        def _(dve):
            step = Steps(dve, dve_step)
            v = nc.vector
            hi_count = [0]

            def rsqrt(dst, src, scale, name=None):
                x, t = nv[:, 0:src.shape[1]], nt_[:, 0:src.shape[1]]
                step(v.tensor_scalar(x, src, scale, EPS, ALU.mult, ALU.add))
                step(v.tensor_scalar(dst.bitcast(I32), x.bitcast(I32), -0.5, float(0x5F3759DF), ALU.mult, ALU.add))
                step(v.tensor_scalar(x, x, -0.5, None, ALU.mult))
                for i in range(4):
                    step(v.tensor_tensor(t, x, dst, ALU.mult))
                    step(v.tensor_tensor(t, t, dst, ALU.mult))
                    step(v.scalar_tensor_tensor(out=dst, in0=t, scalar=1.5, in1=dst, op0=ALU.add, op1=ALU.mult),
                         name if i == 3 else None)

            def low(dst, b, hi, key=None, gain=None):
                hi_count[0] += 1
                dve.wait_ge(N["hi_ready"], hi_count[0])
                if gain is None:
                    ins = v.tensor_tensor(dst, b, hi, ALU.subtract)
                else:
                    ins = v.scalar_tensor_tensor(out=dst, in0=b, scalar=gain, in1=hi, op0=ALU.mult, op1=ALU.subtract)
                step.frees(ins, key)

            def unit(n):
                kd = units[n]["kind"]
                kind, j = kd
                g = G[n % 2]
                if kind == "conv":
                    m, buf = stage_of(kd)
                    gemm_consumed(dve, n)
                    for i in range(3):
                        wcol = i * 8 + j if j < 8 else 32 + i * 6 + j - 8
                        step(v.scalar_tensor_tensor(out=buf[:], in0=cin[:, i:i + T], scalar=cols[:, wcol:wcol + 1], in1=buf[:],
                                                    op0=ALU.mult, op1=ALU.add), "conv_acc" if i == 2 else None)
                elif kind == "up":
                    gemm_consumed(dve, unit_of["gate", j])
                    gemm_product(dve, n)
                    step.frees_gemm(v.tensor_tensor(ft[:], sg[j % 2][:], g[:], ALU.mult), n)
                    dve.wait_ge(N["f_hi"], j + 1)
                    step(v.tensor_tensor(fT[1][:, j % 4, :], ft[:], fT[0][:, j % 4, :], ALU.subtract), "f_lo")
                elif kind == "down" and j[0] > 0:
                    gemm_consumed(dve, unit_of["down", (j[0] - 1, j[1])])
                    gemm_product(dve, n)
                    step.frees_gemm(v.tensor_tensor(accT[:, j[1], :], accT[:, j[1], :], g[:], ALU.add), n)
                elif kind == "gb":
                    gemm_consumed(dve, n)
                    gemm_consumed(dve, unit_of["u2", j])
                    step(v.tensor_tensor(uT[:, j, :], uT[:, j, :], gbt[:], ALU.mult), "gb_used")
                elif kind == "ya":
                    gemm_consumed(dve, unit_of["sga", j])
                    gemm_product(dve, n)
                    step.frees_gemm(v.tensor_tensor(yT[:, j, :], sig[0][j % 2][:], g[:], ALU.mult), n)
                elif kind == "yb":
                    gemm_consumed(dve, unit_of["sgb", j])
                    gemm_product(dve, n)
                    step.frees_gemm(v.tensor_tensor(sig[1][j % 2][:], sig[1][j % 2][:], g[:], ALU.mult), n)
                    step(v.tensor_tensor(yT[:, j, :], yT[:, j, :], sig[1][j % 2][:], ALU.add), "y_done")

            step(v.memset(akT[:], 0.0))
            step(v.memset(av[:, 0, :], 0.0))
            step(v.memset(cols[:, 104:105], 0.0))
            step(v.memset(cin[:, 0:3], 0.0))
            step(v.memset(bias16[:, 8:12], 0.0))
            dve.wait_ge(con_loaded, 16 * 8)
            step(v.tensor_copy(identb[:], ident))
            step(v.tensor_copy(negb[:], con[:, C_NEG:C_NEG + P]))
            b = side_product(dve, (("cols", 0), 0))
            step.frees(v.tensor_copy(cols[:, 0:104], b[:, 0:104]), (("cols", 0), 0))
            dve.wait_ge(small_loaded, 16 * 9)
            step(v.tensor_copy(w16[0][:], w16r[:]))
            step(v.tensor_tensor(w16[1][:], w16r[:], w16[0][:], ALU.subtract), "w16_ready")
            step(v.tensor_copy(nt_[:, 0:1], nt_[:, 0:1]) if False else v.memset(nt_[:], 0.0), "init_done")

            for it in sched:
                kind, j = it
                if kind == "unit":
                    unit(j)
                elif kind == "norm":
                    dve.wait_ge(N["ss_ready"], {0: 1, 1: 3, 2: 5}[j])
                    rsqrt(rs[:], ss[:], 1.0 / D)
                    for c in range(NT):
                        step(v.tensor_scalar(diag[:, c, :], ident, rs[:, c:c + 1], None, ALU.mult),
                             "diag_ready" if c == NT - 1 else None)
                    for hf in range(2):
                        for k in range(KD):
                            b = side_product(dve, (it, hf * 8 + k))
                            t = slice(hf * 512, hf * 512 + 512)
                            g0 = 64 + 8 * j + k
                            low(hT[1][:, k, t], b[:], hT[0][:, k, t], (it, hf * 8 + k), cols[:, g0:g0 + 1])
                elif kind == "small":
                    x, t1, e, s, s2, p = (t[:] for t in sm)
                    b = side_product(dve, (it, 0))
                    step.frees(v.tensor_tensor(x, b[:, 0:P].rearrange("p (c h) -> p c h", c=NT), over(bias16[:], NT), ALU.add), (it, 0))
                    step(v.tensor_scalar(t1, x, -1.0, None, ALU.mult))
                    step(v.tensor_tensor(t1, t1, x, ALU.max), "sm_abs")
                    dve.wait_ge(N["sm_exp"], 1)
                    step(v.tensor_scalar(s, e, 2.0, None, ALU.add))
                    step(v.reciprocal(s, s))
                    step(v.tensor_tensor(s, s, e, ALU.mult))
                    step(v.tensor_tensor(s2, s, s, ALU.mult))
                    step(v.tensor_scalar(p, s2, 1.0 / 19, None, ALU.mult))
                    for n in range(8, 0, -1):
                        step(v.scalar_tensor_tensor(out=p, in0=p, scalar=1.0 / (2 * n + 1), in1=s2, op0=ALU.add, op1=ALU.mult))
                    step(v.scalar_tensor_tensor(out=p, in0=p, scalar=1.0, in1=s, op0=ALU.add, op1=ALU.mult))
                    step(v.tensor_scalar(t1, x, 0.0, None, ALU.max))
                    step(v.scalar_tensor_tensor(out=dts[:], in0=p, scalar=2.0, in1=t1, op0=ALU.mult, op1=ALU.add))
                    step(v.tensor_tensor(s, x, dts[:], ALU.subtract), "sm_arg")
                    step(v.tensor_scalar(easm[:], easm[:], -1.0, None, ALU.mult))
                    step(v.tensor_tensor(da[:, :, 0:8], dts[:, :, 0:8], over(easm[:, 0:8], NT), ALU.mult))
                    step(v.tensor_tensor(da[:, :, 8:12], dts[:, :, 12:16], over(easm[:, 8:12], NT), ALU.mult), "da_ready")
                elif kind == "acs":
                    b = side_product(dve, (it, 0))
                    step.frees(v.tensor_scalar(nacs[:].rearrange("p c h -> p (c h)"), b[:, 0:96], -1.0, None, ALU.mult), (it, 0))
                    step(v.tensor_scalar(nt_[:, 0:1], nt_[:, 0:1], 0.0, None, ALU.mult), "nacs_ready")
                elif kind in tok_items:
                    b = side_product(dve, (it, 1))
                    if kind == "zT" and j > 0:
                        dve.wait_ge(z_out[1], 16 * j)
                    step.frees(v.tensor_copy(tok_dest(it, 1), b[:].rearrange("p (c n) -> p c n", c=4)), (it, 1))
                    if kind == "q2T":
                        side_consumed(dve, (it, 0))
                        if j == 0:
                            dve.wait_ge(rope_loaded, 16 * 3)
                        tk = tok[:].rearrange("p c (h d) -> p (c h) d", d=64)
                        r1, r2 = (t[:].rearrange("p c n -> p (c n)") for t in (rp1, rp2))
                        step(v.tensor_tensor(rp2[:], tok[:], tok[:], ALU.mult))
                        step(v.reduce_sum(rr[:, 0:16], rp2[:].rearrange("p c (h d) -> p (c h) d", d=64), axis=AX))
                        rsqrt(rr[:, 16:32], rr[:, 0:16], 1.0 / 64)
                        step(v.tensor_tensor(tk, tk, widen(rr[:, 16:32], 64), ALU.mult))
                        step(v.tensor_tensor(tk, tk, over(qkg[:, j // 4, :], 16), ALU.mult))
                        if j > 0:
                            side_product(dve, (("q2B", j - 1), 1))
                        step(v.tensor_tensor(rp1[:], tok[:], rope[:, 0], ALU.mult))
                        sw = tok[:].rearrange("p c (g x n) -> p (c g) x n", x=2, n=16)
                        sn = rope[:, 1].rearrange("p c (g x n) -> p (c g) x n", x=2, n=16)
                        ro = rp2[:].rearrange("p c (g x n) -> p (c g) x n", x=2, n=16)
                        for x in range(2):
                            step(v.tensor_tensor(ro[:, :, x, :], sw[:, :, 1 - x, :], sn[:, :, x, :], ALU.mult))
                        step(v.tensor_tensor(r1, r1, r2, ALU.add), "rope_done")
                elif kind == "prep":
                    qk = qkv[:, :, 0:512]
                    for h in range(2):
                        for q in (8, 9, 10, 11):
                            side_consumed(dve, (("convT", q), h))
                    for h in range(2):
                        dve.wait_ge(z_out[h], 16 * 6)
                    side_consumed(dve, (("avT", 0), 0))
                    step(v.tensor_tensor(psq[:], qk, qk, ALU.mult))
                    step(v.reduce_sum(rr[:].rearrange("p (c h) -> p c h", c=NT), psq[:].rearrange("p c (h d) -> p c h d", d=64), axis=AX))
                    rsqrt(psq[:, 0, 0:64], rr[:], 1.0)
                    r = psq[:, 0, 0:64].rearrange("p (c h) -> p c h", c=NT)
                    step(v.tensor_scalar(r[:, :, 0:4], r[:, :, 0:4], 0.125, None, ALU.mult))
                    for c in range(NT):
                        q = qkv[:, c, 0:512].rearrange("p (h d) -> p h d", d=64)
                        step(v.tensor_tensor(q, q, widen(r[:, c, :], 64), ALU.mult))
                    dve.wait_ge(N["eacs_ready"], 1)
                    step(v.tensor_tensor(bge[:], beta[:], eacs[:, :, 8:12], ALU.mult), "prep_done")
                elif kind == "att":
                    c = j
                    for p in range(2):
                        b = side_product(dve, (it, f"s{p}"))
                        bb = b[:].rearrange("p (i n) -> p i n", i=2)
                        al = con[:, C_ALI + 512 * p:C_ALI + 512 * p + 512].rearrange("p (i n) -> p i n", i=2)
                        n0 = P if c == 0 else 0
                        if c == 0:
                            step(v.memset(asb[:, 2 * p:2 * p + 2, 0:P], NEG))
                        step.frees(v.scalar_tensor_tensor(out=asb[:, 2 * p:2 * p + 2, n0:], in0=bb[:, :, n0:], scalar=0.125,
                                                          in1=al[:, :, n0:], op0=ALU.mult, op1=ALU.add), (it, f"s{p}"))
                    step(v.reduce_max(amx[:], asb[:], axis=AX))
                    step(v.tensor_tensor(amx[:], amx[:], sinkb[:], ALU.max))
                    step(v.tensor_scalar(anm[:], amx[:], -1.0, None, ALU.mult))
                    step(v.tensor_tensor(ads[:], sinkb[:], amx[:], ALU.subtract), "att_max")
                    dve.wait_ge(N["att_exp"], c + 1)
                    step(v.tensor_tensor(aden[:], asum[:], ads[:], ALU.add))
                    step(v.reciprocal(aden[:], aden[:]))
                    b = side_product(dve, (it, "p1"))
                    step.frees(v.tensor_copy(apT[:, 2:4], b[:].rearrange("p (i s n) -> p i s n", i=2, s=2)), (it, "p1"))
                    b = side_product(dve, (it, "o"))
                    for p in range(2):
                        o = atok[:].rearrange("p (k q d) -> p q k d", k=2, q=2)[:, p]
                        s = b[:, 0:256].rearrange("p (k q d) -> p q k d", k=2, q=2)[:, p]
                        ins = v.tensor_tensor(o, s, widen(aden[:, 2 * p:2 * p + 2], 64), ALU.mult)
                        if p == 0:
                            step(ins)
                        else:
                            step.frees(ins, (it, "o"))
                    step(v.tensor_scalar(aden[:], aden[:], 0.0, None, ALU.mult), "att_out")
                    b = side_product(dve, (it, "t"))
                    low(hT[1][:, 0:2, hslice(c)], b[:, 0:256].rearrange("p (i n) -> p i n", i=2), hT[0][:, 0:2, hslice(c)], (it, "t"))
                elif kind == "rec":
                    c = j
                    if c == 0:
                        step(v.memset(kTp[:], 0.0))
                        step(v.memset(Sbd[:], 0.0))
                        step(v.memset(Sst[:], 0.0), "init_done")
                    def h64(x):
                        return x.rearrange("p (h d) -> p h d", d=64)
                    k_, v_, x_ = h64(qkv[:, c, 256:512]), h64(qkv[:, c, 512:768]), h64(xs[:, c, :])
                    kb4 = [h64(kbv[:, i, :]) for i in range(4)]
                    step(v.tensor_tensor(kb4[1], v_, widen(beta[:, c, :], 64), ALU.mult))
                    step(v.tensor_tensor(kb4[2], k_, widen(bge[:, c, :], 64), ALU.mult))
                    step(v.tensor_tensor(kb4[0], k_, widen(beta[:, c, :], 64), ALU.mult), "rec_kb")
                    step(v.tensor_tensor(h64(xc[:, 0]), x_, widen(dts[:, c, 0:8], 64), ALU.mult))
                    for i in range(3):
                        side_consumed(dve, (it, f"bc{i}"))
                    step(v.tensor_tensor(kb4[3], k_, widen(E[:, 8:12, P - 1], 64), ALU.mult))
                    step(v.tensor_tensor(h64(xc[:, 1]), h64(xc[:, 0]), widen(E[:, 0:8, P - 1], 64), ALU.mult))
                    for r in range(2):
                        step(v.tensor_copy(cdc[64 * r:64 * r + 64, :], cd[64 * r:64 * r + 64, 8:12].rearrange("p (a b) -> p a b", b=2)[:, :, r]),
                             "rec_dec" if r == 1 else None)
                    b = side_product(dve, (it, "qT"))
                    step.frees(v.tensor_copy(kq[:, :, 1, :], b[:, 0:256].rearrange("p (a n) -> p a n", a=2)), (it, "qT"))
                    b = side_product(dve, (it, "g"))
                    step(v.tensor_tensor(E[:, 0:4, :], E[:, 0:4, :], over(b[:, 0:P], 4), ALU.mult))
                    step.frees(v.tensor_tensor(E[:, 4:8, :], E[:, 4:8, :], over(b[:, P:2 * P], 4), ALU.mult), (it, "g"))
                    for p in range(2):
                        b = side_product(dve, (it, f"kq{p}"))
                        e = E[:, 8 + 2 * p:10 + 2 * p, :].unsqueeze(2).to_broadcast([P, 2, 2, P])
                        step.frees(v.tensor_tensor(SQ[:, 2 * p:2 * p + 2], b[:].rearrange("p (h a n) -> p h a n", h=2, a=2), e, ALU.mult), (it, f"kq{p}"))
                    step(v.tensor_tensor(XT[:], SQ[:, :, 0, :], over(con[:, C_LV:C_LV + P], 4), ALU.mult))
                    step(v.scalar_tensor_tensor(out=XT[:], in0=XT[:], scalar=-1.0, in1=over(ident, 4), op0=ALU.mult, op1=ALU.add), "rec_x0")
                    b = side_product(dve, (it, "yo"))
                    step.frees(v.tensor_tensor(h64(mix[:, 0:512]), h64(b[:]), widen(eacs[:, c, 0:8], 64), ALU.mult), (it, "yo"))
                    step(v.tensor_tensor(h64(Sst[:]), h64(Sst[:]), widen(cd[:, 0:8], 64), ALU.mult))

                    def four(b):
                        return b[:].rearrange("p (h n) -> p h n", h=4)

                    for lv in range(1, 7):
                        b = side_product(dve, (it, f"y{lv}"))
                        step.frees(v.tensor_tensor(Y[:], four(b), over(con[:, C_LV + lv * P:C_LV + (lv + 1) * P], 4), ALU.mult), (it, f"y{lv}"))
                        if lv < 6:
                            b = side_product(dve, (it, f"x{lv}"))
                            side_product(dve, (it, f"t{lv}"))
                            step.frees(v.tensor_tensor(X[:], X[:], four(b), ALU.subtract), (it, f"x{lv}"))
                        b = side_product(dve, (it, f"t{lv}"))
                        step.frees(v.tensor_tensor(XT[:], XT[:], four(b), ALU.subtract), (it, f"t{lv}"))
                        if lv == 1:
                            b = side_product(dve, (it, "yd"))
                            step.frees(v.tensor_tensor(mix[:, 0:512], mix[:, 0:512], b[:], ALU.add), (it, "yd"))
                        if lv == 2:
                            b = side_product(dve, (it, "st"))
                            step.frees(v.tensor_tensor(Sst[:], Sst[:], b[:], ALU.add), (it, "st"))
                            step(v.tensor_tensor(h64(msq[:, 0:512]), x_, widen(dskip[:], 64), ALU.mult))
                            step(v.tensor_tensor(mix[:, 0:512], mix[:, 0:512], msq[:, 0:512], ALU.add))
                            dve.wait_ge(z_in, 16 * (c + 1))
                            step(v.tensor_tensor(mix[:, 0:512], mix[:, 0:512], zt[:, 0:512], ALU.mult))
                    side_consumed(dve, (it, "uw"))
                    b = side_product(dve, (it, "r1"))
                    step(v.tensor_tensor(vn[:], uw[:, 0:256], b[:, 0:256], ALU.subtract), "rec_vn")
                    step.frees(v.tensor_tensor(h64(o1[:]), h64(b[:, 256:512]), widen(eacs[:, c, 8:12], 64), ALU.mult), (it, "r1"))
                    b = side_product(dve, (it, "r2"))
                    step(v.tensor_tensor(mix[:, 512:768], o1[:], b[:, 0:256], ALU.add))
                    step.frees(v.tensor_tensor(tS[:], b[:, 256:512].rearrange("p (a n) -> p a n", a=2), over(blk, 2), ALU.mult), (it, "r2"))
                    for p in range(2):
                        step(v.scalar_tensor_tensor(out=Sbd[:, p, :], in0=Sbd[:, p, :], scalar=cdc[:, p:p + 1], in1=tS[:, p, :],
                                                    op0=ALU.mult, op1=ALU.add), "rec_S" if p else None)
                    step(v.tensor_tensor(msq[:], mix[:], mix[:], ALU.mult))
                    step(v.reduce_sum(nss[:, 0:2], msq[:, 0:512].rearrange("p (g n) -> p g n", g=2), axis=AX))
                    step(v.reduce_sum(nss[:, 2:6], h64(msq[:, 512:768]), axis=AX))
                    step(v.tensor_scalar(nss[:, 0:2], nss[:, 0:2], 0.25, None, ALU.mult))
                    rsqrt(nrs[:], nss[:], 1.0 / 64)
                    m2, m4 = mix[:, 0:512].rearrange("p (g n) -> p g n", g=2), h64(mix[:, 512:768])
                    step(v.tensor_tensor(m2, m2, widen(nrs[:, 0:2], 256), ALU.mult))
                    step(v.tensor_tensor(m4, m4, widen(nrs[:, 2:6], 64), ALU.mult))
                    step(v.tensor_tensor(mix[:, 512:768], mix[:, 512:768], zt[:, 512:768], ALU.mult))
                    dve.wait_ge(gain_loaded, 32)
                    step(v.tensor_tensor(mix[:], mix[:], gmix[:], ALU.mult), "rec_mix")
                    for key, k0, n in (("m0", 2, 4), ("m1", 6, 2)):
                        b = side_product(dve, (it, key))
                        low(hT[1][:, k0:k0 + n, hslice(c)], b[:, 0:n * P].rearrange("p (i n) -> p i n", i=n),
                            hT[0][:, k0:k0 + n, hslice(c)], (it, key))
                elif kind == "resid":
                    dve.wait_ge(N["ss_ready"], 2 + 2 * j)
                    rsqrt(rs[:], ss[:], 1.0 / D)
                    src = mo if j == 0 else fo
                    if j == 0:
                        dve.wait_ge(res_loaded, 32)
                    else:
                        dve.wait_ge(gain_loaded, 48)
                    gb = gbc[:, 0, :] if j == 0 else gbc2[:]
                    for c in range(NT):
                        step(v.scalar_tensor_tensor(out=src[:, c, :], in0=src[:, c, :], scalar=rs[:, c:c + 1], in1=gb,
                                                    op0=ALU.mult, op1=ALU.mult))
                        step(v.tensor_tensor(x1[:, c, :], x1[:, c, :], src[:, c, :], ALU.add), "resid_done" if c == NT - 1 else None)
                elif kind == "downT":
                    for c in range(NT):
                        b = side_product(dve, (it, 2 * c + 1))
                        step.frees(v.tensor_copy(fo[:, c, 512:1024], b[:]), (it, 2 * c + 1))
                elif kind == "q2B":
                    if j == 0:
                        dve.wait_ge(x2_out, 16)
                    b = side_product(dve, (it, 1))
                    if j < 4:
                        step.frees(v.tensor_copy(qT2[:, j, 512:1024], b[:]), (it, 1))
                    else:
                        step(v.memset(kT2[64:P, 0, :], 0.0))
                        step(v.memset(kT2[0:64, 1, :], 0.0))
                        step(v.tensor_copy(kT2[0:64, 0, 512:1024], b[0:64, :]))
                        step.frees(v.tensor_copy(kT2[64:P, 1, 512:1024], b[64:P, :]), (it, 1))
                elif kind == "ln":
                    b = side_product(dve, (it, 1))
                    step.frees(v.tensor_copy(wsT[:, 4:8], b[:].rearrange("p (i n) -> p i n", i=4)), (it, 1))
                    for q in range(4):
                        side_consumed(dve, (("viT", q), 0))
                    step(v.reduce_sum(mean[:], vv[:], axis=AX))
                    step(v.tensor_scalar(mean[:], mean[:], -1.0 / 512, None, ALU.mult))
                    for c in range(NT):
                        step(v.tensor_scalar(vv[:, c, :], vv[:, c, :], mean[:, c:c + 1], None, ALU.add), "mean_done" if c == NT - 1 else None)
                    dve.wait_ge(N["ss_ready"], 6)
                    rsqrt(rs[:], ss[:], 1.0 / 512)
                    for c in range(NT):
                        step(v.scalar_tensor_tensor(out=vv[:, c, :], in0=vv[:, c, :], scalar=rs[:, c:c + 1], in1=lnp[:, 0, :],
                                                    op0=ALU.mult, op1=ALU.mult))
                        step(v.tensor_tensor(vv[:, c, :], vv[:, c, :], lnp[:, 1, :], ALU.add), "ln_done" if c == NT - 1 else None)
                elif kind == "a2s":
                    m = a2m[:, 2 * (j % 2):2 * (j % 2) + 2]
                    for s in range(2):
                        b = side_product(dve, (it, s))
                        step(v.reduce_max(m[:, s:s + 1], b[:], axis=AX))
                    if j >= 2:
                        side_consumed(dve, (("a2s", j - 2), 1))
                    d = a2m[:, 4 + j % 2:5 + j % 2]
                    step(v.tensor_tensor(d, m[:, 0:1], m[:, 1:2], ALU.max))
                    step(v.tensor_scalar(d, d, -0.125, None, ALU.mult), "a2_max")
                elif kind == "a2p":
                    c, h = j // 8, j % 8
                    b = side_product(dve, (it, 1))
                    step.frees(v.tensor_copy(PT[:, 4:8, :], b[:].rearrange("p (i n) -> p i n", i=4)), (it, 1))
                    side_consumed(dve, (("a2s", j), 0))
                    side_consumed(dve, (("a2s", j), 1))
                    r = a2r[:, 0:1]
                    step(v.tensor_tensor(r, a2s_[:, j % 2, 0:1], a2s_[:, j % 2, 1:2], ALU.add))
                    step(v.reciprocal(r, r))
                    b = side_product(dve, (it, 2))
                    kv = h // 4
                    step.frees(v.tensor_scalar(ot[:, h * 64:h * 64 + 64], b[:, kv * 64:kv * 64 + 64], r, None, ALU.mult), (it, 2))
                    step(v.tensor_scalar(a2r[:, 1:2], r, 0.0, None, ALU.mult), "a2_out")
                elif kind == "a2t":
                    if j == 0:
                        for q in range(4):
                            gemm_consumed(dve, unit_of["ga", q])
                    b = side_product(dve, (it, 0))
                    step.frees(v.tensor_tensor(gaT[:, :, hslice(j)], gaT[:, :, hslice(j)], b[:].rearrange("p (i n) -> p i n", i=4), ALU.mult), (it, 0))
                elif kind == "sp":
                    b = side_product(dve, (it, 0))
                    step.frees(v.tensor_tensor(spt[:], b[:].rearrange("p (i n) -> p i n", i=4), bsp[:], ALU.add), (it, 0))
                    step(v.tensor_tensor(uT[:, :, hslice(j)], uT[:, :, hslice(j)], spt[:], ALU.mult), "y_ready" if j == NT - 1 else None)
                elif kind in ("split4", "splity"):
                    for k in range(8):
                        if kind == "split4":
                            dve.wait_ge(N["split_hi"], k + 1)
                            d = atT if k < 4 else gmT
                            step(v.tensor_tensor(d[1][:, k % 4, :], (gaT if k < 4 else uT)[:, k % 4, :], d[0][:, k % 4, :], ALU.subtract), "split_lo")
                        else:
                            dve.wait_ge(N["yT_hi"], k + 1)
                            step(v.tensor_tensor(hT[1][:, k, :], yT[:, k, :], hT[0][:, k, :], ALU.subtract), "yT_lo")
                elif kind == "final":
                    dve.wait_ge(x2_in, 32)
                    for h in range(2):
                        for q in range(8):
                            side_consumed(dve, (("wo2T", q), h))
                    for c in range(NT):
                        step(v.tensor_tensor(ob[:, c, :], ob[:, c, :], x2[:, c, :], ALU.add), "final_sum" if c == NT - 1 else None)
                    dve.wait_ge(N["ss_ready"], 7)
                    rsqrt(rs[:], ss[:], 1.0 / D)
                    for c in range(NT):
                        step(v.scalar_tensor_tensor(out=ob[:, c, :], in0=ob[:, c, :], scalar=rs[:, c:c + 1], in1=fgb[:],
                                                    op0=ALU.mult, op1=ALU.mult), "final_done")



def kernel(**inputs):
    import concourse.bacc as bacc
    from concourse.bass_utils import run_bass_kernel_spmd

    nc = bacc.Bacc("TRN2", target_bir_lowering=False, num_devices=1, dynamic_dma_scratch_size=SWDGE_RING)
    arrays, aps = {}, {}
    for name, value in inputs.items():
        v = np.ascontiguousarray(value)
        arrays[f"in_{name}"] = v
        ap = nc.dram_tensor(f"in_{name}", v.shape, mybir.dt.from_np(v.dtype), kind="ExternalInput").ap()
        aps[name] = ap[0] if name != "final_gain_2" else ap
    for name, v in zip(("con1", "con2"), consts_of_shapes()):
        arrays[name] = v
        aps[name] = nc.dram_tensor(name, v.shape, F32, kind="ExternalInput").ap()
    out = nc.dram_tensor("out", (1, T, D), F32, kind="ExternalOutput").ap()
    build_program(nc, aps, out[0])
    r = run_bass_kernel_spmd(nc, [arrays], core_ids=[0])
    return r.results[0]["out"]
```

```python
from contextlib import ExitStack

import numpy as np
import concourse.bass as bass
from concourse import mybir

F32 = mybir.dt.float32
F32R = mybir.dt.float32r
BF16 = mybir.dt.bfloat16
I32 = mybir.dt.int32
ALU = mybir.AluOpType
ACT = mybir.ActivationFunctionType
AX = mybir.AxisListType.X

P = 128
T = 1024
NT = T // P
D = 1024
KD = D // P
FF = 2816
NF = FF // P
EPS = 1e-6
NEG = -1e30
SWDGE_RING = 1024
SBUF_BASE = SWDGE_RING + 128

O_AQ, O_AK, O_AV, O_SZ, O_XBC, O_DT, O_QKV, O_GZ, O_B = 0, 256, 384, 512, 1024, 2048, 2056, 2824, 3080
O2_Q, O2_K, O2_V, O2_GA, O2_U, O2_VI, O2_GB, O2_M = 0, 512, 640, 768, 1280, 1792, 2304, 2816


def consts_of_shapes():
    i = np.arange(P)
    ident = np.eye(P)
    upper = (i[:, None] <= i[None, :]).astype(float)
    block = (i[:, None] // 64 == i[None, :] // 64).astype(float)
    levels = []
    for b in range(7):
        n = 1 << b
        m = ((i[:, None] // (2 * n) == i[None, :] // (2 * n)) & (i[:, None] // n % 2 == 1) & (i[None, :] // n % 2 == 0))
        levels.append(m.T if b == 0 else m)
    neg = np.where(upper > 0, 0.0, NEG)
    j = np.arange(2 * P)
    dist = np.abs(i[:, None] + P - j[None, :])
    seen = np.where(i[:, None] < 64, j[None, :] < 192, j[None, :] >= 64)
    alibi = [np.where(seen, -(2.0 ** (-2.0 * (h + 1))) * dist, NEG) for h in (0, 2, 1, 3)]
    c1 = np.concatenate([ident, upper, block, *levels, neg, *alibi], axis=1).astype(np.float32)
    t = np.arange(T)
    inv = (10000.0 ** (-np.arange(0, 32, 2, dtype=np.float32) / 32)).astype(np.float32)
    ang = np.stack([(t // 64).astype(np.float32)[:, None] * inv, (t % 64).astype(np.float32)[:, None] * inv], 1)
    cos, sin = np.cos(ang), np.sin(ang)
    ct = np.stack([cos, cos], 2).reshape(T, 64)
    st = np.stack([-sin, sin], 2).reshape(T, 64)
    two = [np.tile(m, (1, 2)).reshape(NT, P, 2 * 64).transpose(1, 0, 2).reshape(P, NT * P) for m in (ct, st)]
    return np.ascontiguousarray(c1), np.ascontiguousarray(np.concatenate(two, 1).astype(np.float32))


C_ID, C_UP, C_BLK, C_LV, C_NEG, C_ALI = 0, 128, 256, 384, 384 + 7 * 128, 512 + 7 * 128
C_END = C_ALI + 4 * 256


def weight_units():
    ws, units = [], []

    def add(name, kt, row, pieces, kinds):
        ws.append((name, kt, row, pieces))
        per = (1024 // kt) // P
        assert len(kinds) == per
        for s, kind in enumerate(kinds):
            units.append(dict(w=len(ws) - 1, kt=kt, sub=s, kind=kind, last=s == per - 1))

    for j in range(4):
        add("w_in", 8, 0, [(O_XBC + 128 * j, 128)], [("conv", j)])
    for j in range(4, 8):
        add("w_in", 8, 0, [(O_XBC + 128 * j, 128)], [("conv", j)])
    for j in range(6):
        add("w_in", 8, 0, [(O_QKV + 128 * j, 128)], [("conv", 8 + j)])
    add("w_in", 8, 0, [(O_DT, 8), (O_B, 8), (0, 112)], [("sm", 0)])
    for j in range(4):
        add("w_in", 8, 0, [(O_SZ + 128 * j, 128)], [("z", j)])
    for j in range(2):
        add("w_in", 8, 0, [(O_GZ + 128 * j, 128)], [("z", 4 + j)])
    for j in range(2):
        add("w_in", 8, 0, [(O_AQ + 64 * j, 64), (O_AQ + 64 * (j + 2), 64)], [("aq", j)])
    add("w_in", 8, 0, [(O_AK, 128)], [("ak", 0)])
    add("w_in", 8, 0, [(O_AV, 128)], [("av", 0)])
    for j in range(8):
        add("w_out", 8, 0, [(128 * j, 128)], [("wo", j)])
    groups = [(4 * g, min(4, NF - 4 * g)) for g in range((NF + 3) // 4)]

    def gate(f):
        add("ffn_w_gate", 8, 0, [(128 * f, 128)], [("gate", f)])

    def up(f):
        add("ffn_w_up", 8, 0, [(128 * f, 128)], [("up", f)])

    gate(0)
    for g, (f0, n) in enumerate(groups):
        up(f0)
        for f in range(f0 + 1, f0 + n):
            gate(f)
            up(f)
        if g + 1 < len(groups):
            gate(f0 + n)
        per = (1024 // n) // P
        for j in range(8 // per):
            add("ffn_w_down", n, f0, [(j * 1024 // n, 1024 // n)],
                [("down", (g, j * per + s)) for s in range(per)])
    for j in range(4):
        add("w_in_2", 8, 0, [(O2_Q + 64 * j, 64), (O2_Q + 64 * (j + 4), 64)], [("q2", j)])
    add("w_in_2", 8, 0, [(O2_K, 128)], [("q2", 4)])
    add("w_in_2", 8, 0, [(O2_V, 128)], [("v2", 0)])
    for o, kind in ((O2_VI, "vi"), (O2_GA, "ga"), (O2_U, "u2"), (O2_GB, "gb")):
        for j in range(4):
            add("w_in_2", 8, 0, [(o + 128 * j, 128)], [(kind, j)])
    for j in range(0, 8, 2):
        for s in range(2):
            add("w_in_2", 8, 0, [(O2_M + 128 * (j + s), 128)], [("sga", j + s)])
        for s in range(2):
            add("w_in_2", 8, 0, [(O2_M + 1024 + 128 * (j + s), 128)], [("sgb", j + s)])
        add("w_proj_attn_2", 4, 0, [(128 * j, 256)], [("ya", j), ("ya", j + 1)])
        add("w_proj_gmlp_2", 4, 0, [(128 * j, 256)], [("yb", j), ("yb", j + 1)])
    for j in range(8):
        add("w_out_2", 8, 0, [(128 * j, 128)], [("wo2", j)])
    return ws, units


def schedule(units):
    by = {u["kind"]: n for n, u in enumerate(units)}
    s, late, begun = [], [], set()

    def begin(kd, before, between):
        begun.add(kd)
        s.extend(before + [("half", (by[kd], 0))] + between + [("half", (by[kd], 1))])

    def run(kinds, after=lambda kd: []):
        for kd in kinds:
            if kd not in begun:
                s.append(("unit", by[kd]))
            s.extend([x for d, x in late if d <= 0])
            late[:] = [(d - 1, x) for d, x in late if d > 0] + list(after(kd))

    def flush():
        s.extend([it for _, it in sorted(late, key=lambda x: x[0])])
        late.clear()

    s.append(("cols", 0))
    begin(("conv", 0), [("norm", (0, 0))], [("norm", (0, 1))])
    run([("conv", j) for j in range(14)], lambda kd: [(0, ("convT", kd[1]))] if kd[1] not in (6, 7) else [])
    run([("sm", 0)], lambda kd: [(0, ("smT", 0)), (1, ("prep", 0)), (2, ("acs", 0))])
    run([("z", j) for j in range(6)], lambda kd: [(0, ("zT", kd[1]))])
    run([("aq", 0), ("aq", 1), ("ak", 0)])
    run([("av", 0)], lambda kd: [(0, ("avT", 0))])
    flush()
    for c in range(NT + 1):
        fill = [[] for _ in range(13)]
        if c > 0:
            for i, k in enumerate(("r1", "yo", "yd", "r2", "st")):
                fill[i].append((k, c - 1))
            fill[6].append(("rn", c - 1))
        if c < NT:
            fill[5].append(("as", c))
            fill[7].append(("ap", c))
            fill[9].append(("ao", c))
            s.append(("ra", c))
        s.extend(fill[0])
        for lv in range(1, 7):
            if c < NT:
                s.append(("ly", (c, lv)))
            s.extend(fill[2 * lv - 1])
            if c < NT:
                s.append(("lx", (c, lv)))
            s.extend(fill[2 * lv])
        if c < NT:
            s.append(("uw", c))
    begin(("wo", 0), [("mx", 0)], [("mx", 1), ("load", 0)])
    run([("wo", j) for j in range(8)], lambda kd: [(0, ("woT", kd[1]))])
    flush()
    begin(("gate", 0), [("resid", (0, 0)), ("norm", (1, 0)), ("resid", (0, 1))], [("norm", (1, 1))])
    run([u["kind"] for u in units if u["kind"][0] in ("gate", "up", "down")])
    s += [("downT", 0), ("downT", 1)]
    begin(("q2", 0), [("resid", (1, 0)), ("norm", (2, 0)), ("resid", (1, 1))], [("norm", (2, 1))])
    s.append(("load", 2))
    run([("q2", j) for j in range(5)], lambda kd: [(0, ("q2T", kd[1])), (1, ("q2B", kd[1]))])
    run([("v2", 0)], lambda kd: [(0, ("v2T", 0))])
    run([("vi", j) for j in range(4)], lambda kd: [(0, ("viT", kd[1]))])
    flush()
    s += [("load", 3), ("ln", 0)]
    rest = [(k, j) for k in ("ga", "u2", "gb") for j in range(4)]
    s += [("a2s", 0), ("a2s", 1), ("a2x", 0)]
    for n in range(NT * 8):
        if n + 2 < NT * 8:
            s.append(("a2s", n + 2))
        if n + 1 < NT * 8:
            s.append(("a2x", n + 1))
        s.append(("a2o", n))
        if rest and (n in (0, 2, 4, 6) or (n > 8 and n % 6 == 0)):
            s.append(("unit", by[rest.pop(0)]))
        if n % 8 == 7:
            s.append(("a2t", n // 8))
    assert not rest
    s += [("sp", c) for c in range(NT)]
    s.append(("split4", 0))
    for j in range(0, 8, 2):
        run([("sga", j), ("sga", j + 1), ("sgb", j), ("sgb", j + 1), ("ya", j), ("ya", j + 1), ("yb", j), ("yb", j + 1)])
    s += [("splity", 0), ("load", 4)]
    run([("wo2", j) for j in range(8)], lambda kd: [(0, ("wo2T", kd[1]))])
    flush()
    s += [("final", 0), ("final", 1)]
    return s


def products_of(item):
    kind, a = item
    if kind == "ra":
        return ["bc0", "bc1", "bc2", "kT", "qT", "g", "kq0", "kq1", "xT"]
    if kind == "lx":
        return ["x", "t"] if a[1] < 6 else ["t"]
    return list(range({"cols": 1, "norm": 8, "mx": 8, "smT": 1, "acs": 1, "convT": 2, "zT": 2, "avT": 2, "woT": 2,
                       "downT": 8, "q2T": 2, "q2B": 2, "v2T": 2, "viT": 2, "ln": 2, "a2s": 2, "a2x": 2, "a2o": 1,
                       "a2t": 1, "sp": 1, "wo2T": 2, "ly": 1, "uw": 1, "yo": 1, "yd": 1, "st": 1, "r1": 1, "r2": 1,
                       "as": 2, "ap": 2, "ao": 1}.get(kind, 0)))


def build_program(nc, a, out):
    ws, units = weight_units()
    unit_of = {u["kind"]: n for n, u in enumerate(units)}
    last_unit_of = {u["w"]: n for n, u in enumerate(units) if u["last"]}
    sched = schedule(units)
    assert [x[1] if x[0] == "unit" else x[1][0] for x in sched if x[0] == "unit" or x[0] == "half" and x[1][1]] \
        == list(range(len(units)))
    prod, n = {}, 0
    for it in sched:
        for key in products_of(it):
            prod[it, key] = n
            n += 1
    stage_uses = {}
    for it in sched:
        if it[0] == "unit" or it[0] == "half" and it[1][1]:
            kd = units[it[1] if it[0] == "unit" else it[1][0]]["kind"]
            reader = {"conv": "convT", "sm": "smT", "z": "zT", "av": "avT", "wo": "woT", "q2": "q2T", "v2": "v2T", "vi": "viT",
                      "wo2": "wo2T"}.get(kd[0])
            if reader:
                stage_uses[kd] = (len(stage_uses), (reader, kd[1]))
    stage_reader = {m: r for m, r in stage_uses.values()}

    z_dram = nc.dram_tensor("z_spill", [T, 768], F32).ap()
    x2_dram = nc.dram_tensor("x2_spill", [T, D], F32).ap()

    ctx = ExitStack()
    with ctx:
        def sem(name):
            return ctx.enter_context(nc.semaphore(name))

        def sbuf(name, shape, kb, dt=F32):
            return nc.alloc_sbuf_tensor_at(name, [P] + list(shape), dt, offset=SBUF_BASE + int(kb * 1024), align_bytes=8)

        hT = [sbuf("h_hi", [KD, T], 0, F32R), sbuf("h_lo", [KD, T], 32, F32R)]
        raw = [sbuf(f"w_raw{i}", [1024], 64 + 4 * i) for i in range(4)]
        whi = [sbuf(f"w_hi{i}", [1024], 80 + 4 * i, F32R) for i in range(2)]
        wlo = [sbuf(f"w_lo{i}", [1024], 88 + 4 * i, F32R) for i in range(2)]
        con = sbuf("con", [C_END], 96)
        ident = con[:, C_ID:C_ID + P]
        upper = con[:, C_UP:C_UP + P]
        blk = con[:, C_BLK:C_BLK + P]
        identb = sbuf("identb", [P], 105.5, BF16)
        negb = sbuf("negb", [P], 105.75, BF16)
        cols = sbuf("cols", [112], 106)
        bias16 = sbuf("bias16", [16], 106.5)
        alog = sbuf("alog", [12], 106.5625)
        dskip = sbuf("dskip", [8], 106.625)
        sinkb = sbuf("sinkb", [4], 106.6875)
        ss = sbuf("ss", [NT], 106.75)
        rs = sbuf("rs", [NT], 106.8125)
        nv = sbuf("nv", [64], 106.875)
        nt_ = sbuf("nt_", [64], 107.125)
        mean = sbuf("mean", [NT], 107.375)
        a2m = sbuf("a2m", [8], 107.4375)
        a2s_ = sbuf("a2s_", [2, 2], 107.46875)
        a2r = sbuf("a2r", [2], 107.5)
        rr = sbuf("rr", [64], 107.75)
        diag = sbuf("diag", [NT, P], 218.75)

        xin = sbuf("xin", [NT, D], 108)
        nsq = sbuf("nsq", [D], 176)
        BC = sbuf("BC", [4, T], 108)
        xs = sbuf("xs", [NT, 512], 124)
        Bt = sbuf("Bt", [NT, 256], 140)
        qkv = sbuf("qkv", [NT, 768], 148)
        aqT = sbuf("aqT", [2, T], 172)
        akT = sbuf("akT", [2, P + T], 180)
        av = sbuf("av", [1 + NT, P], 189)
        da = sbuf("da", [NT, 12], 193.5)
        nacs = sbuf("nacs", [NT, 12], 193.875)
        eacs = sbuf("eacs", [NT, 12], 194.25)
        dts = sbuf("dts", [NT, 16], 194.625)
        beta = sbuf("beta", [NT, 4], 195.125)
        bge = sbuf("bge", [NT, 4], 195.25)
        cin = sbuf("cin", [3 + T], 196)
        cacc = [sbuf(f"cacc{i}", [T], 200.5 + 4 * i) for i in range(2)]
        zst = sbuf("zst", [2, 4, P], 208.5)
        sm = [sbuf(f"sm{i}", [NT, 16], 212.5 + 0.5 * i) for i in range(6)]
        rows = sbuf("rows", [P], 217)
        easm = sbuf("easm", [12], 217.5)
        psq = sbuf("psq", [NT, 512], 172)

        asb = sbuf("asb", [4, 256], 195.5)
        apT = sbuf("apT", [4, 2, P], 199.5)
        atts = sbuf("atts", [NT, 256], 203.5)
        amx = sbuf("amx", [4], 221.5)
        anm = sbuf("anm", [4], 221.5625)
        ads = sbuf("ads", [4], 221.625)
        asum = sbuf("asum", [4], 221.6875)
        aden = sbuf("aden", [4], 221.75)

        def slots(name, shape, kb):
            return [sbuf(f"{name}{i}", shape, kb + 30 * i) for i in range(2)]

        E = slots("E", [12, P], 0)
        kTp = slots("kTp", [4, P], 6)
        kq = slots("kq", [2, 2, P], 8)
        SQ = slots("SQ", [4, 2, P], 10)
        X = slots("X", [4, P], 14)
        XT = slots("XT", [4, P], 16)
        Y = slots("Y", [4, P], 18)
        kbv = slots("kbv", [4, 256], 20)
        uw = slots("uw", [512], 24)
        xc = slots("xc", [2, 512], 26)
        msq = slots("msq", [768], 14)
        vn = sbuf("vn", [256], 60)
        Sbd = sbuf("Sbd", [2, P], 61)
        Sst = sbuf("Sst", [512], 62)
        cd = [sbuf(f"cd{i}", [12], 195.375 + i * 0.046875) for i in range(2)]
        cdc = [sbuf(f"cdc{i}", [2], 195.46875 + i * 0.0078125) for i in range(2)]
        nss, nrs = rr[:, 0:6], rr[:, 6:12]
        o1 = sbuf("o1", [256], 211.5)
        tS = sbuf("tS", [2, P], 211.5)
        mix = sbuf("mix", [768], 212.5)
        zt = sbuf("zt", [768], 215.5)
        gmix = sbuf("gmix", [768], 218.5)

        mo = sbuf("mo", [NT, D], 108)
        x1 = sbuf("x1", [NT, D], 140)
        ost = [sbuf(f"ost{i}", [T], 172 + 4 * i) for i in range(2)]
        gbc = sbuf("gbc", [2, D], 180)
        fT = [sbuf("f_hi", [4, T], 108, F32R), sbuf("f_lo", [4, T], 124, F32R)]
        accT = sbuf("accT", [KD, T], 172)
        sg = [sbuf(f"sg{i}", [T], 204 + 4 * i) for i in range(2)]
        ft = sbuf("ft", [T], 212)
        fo = sbuf("fo", [NT, D], 108)
        rsq = sbuf("rsq", [D], 212)
        gbc2 = sbuf("gbc2", [D], 204)

        gaT = sbuf("gaT", [4, T], 108)
        uT = sbuf("uT", [4, T], 124)
        vv = sbuf("vv", [NT, 512], 140)
        qT2 = sbuf("qT2", [4, T], 156)
        kT2 = sbuf("kT2", [2, T], 172)
        v2k = sbuf("v2k", [NT, P], 180)
        st2 = [sbuf("st2_0", [T], 184), sbuf("st2_1", [T], 209)]
        tok = sbuf("tok", [NT, P], 188)
        rp1 = sbuf("rp1", [NT, P], 192)
        rp2 = sbuf("rp2", [NT, P], 205)
        rope = sbuf("rope", [2, NT, P], 196)
        qkg = sbuf("qkg", [2, 64], 204)
        gbt = sbuf("gbt", [T], 184)
        wsr = sbuf("wsr", [8, P], 188)
        wsT = sbuf("wsT", [8, P], 192)
        bsp = sbuf("bsp", [4, P], 196)
        lnp = sbuf("lnp", [2, 512], 198)
        lsq = sbuf("lsq", [512], 217 - 0.25)
        Pb = [sbuf(f"Pb{i}", [T], 205 + 4 * i) for i in range(2)]
        PT = [sbuf("PT0", [NT, P], 213), sbuf("PT1", [NT, P], 218.75)]
        ot = sbuf("ot", [512], 202)
        spt = sbuf("spt", [4, P], 205)

        atT = [sbuf("at_hi", [4, T], 140, F32R), sbuf("at_lo", [4, T], 156, F32R)]
        gmT = [sbuf("gm_hi", [4, T], 172, F32R), sbuf("gm_lo", [4, T], 188, F32R)]
        yT = sbuf("yT", [KD, T], 108)
        sig = [[sbuf(f"sig{i}{k}", [T], 204 + 4 * (2 * i + k)) for k in range(2)] for i in range(2)]
        ob = sbuf("ob", [NT, D], 108)
        x2 = sbuf("x2", [NT, D], 140)
        fst = [sbuf(f"fst{i}", [T], 204 + 4 * i) for i in range(2)]
        fgb = sbuf("fgb", [D], 172)

        G = [ctx.enter_context(nc.psum_tensor(f"gemm{i}", [P, T], F32)) for i in range(2)]
        S = [ctx.enter_context(nc.psum_tensor(f"side{i}", [P, 512], F32)) for i in range(4)]

        con_loaded, small_loaded = sem("con_loaded"), sem("small_loaded")
        x_loaded = [sem(f"x_loaded{i}") for i in range(2)]
        raw_loaded = [sem(f"raw_loaded{i}") for i in range(4)]
        w_split = sem("w_split")
        pool_hi = sem("pool_hi")
        gemm_done = [sem(f"gemm_done{i}") for i in range(2)]
        gemm_read = [sem(f"gemm_read{i}") for i in range(2)]
        side_done = [sem(f"side_done{i}") for i in range(4)]
        side_read = [sem(f"side_read{i}") for i in range(4)]
        act_step, dve_step = sem("act_step"), sem("dve_step")
        N = {k: sem(k) for k in (
            "init_done", "ss_ready", "diag_ready", "hi_ready", "conv_acc", "conv_act", "w16_ready", "sm_abs",
            "sm_exp", "sm_arg", "beta_ready", "da_ready", "nacs_ready", "eacs_ready", "prep_done", "att_max",
            "att_exp", "att_out", "rec_kb", "rec_dec", "rec_x0", "rec_y", "rec_vn", "rec_S", "rec_mix",
            "resid_done", "staged", "f_mul", "f_hi", "f_lo", "rope_done", "gb_act", "gb_used", "mean_done",
            "ln_done", "a2_max", "a2_out", "split_hi", "split_lo", "sig_ready", "y_done", "yT_hi", "yT_lo",
            "final_sum", "final_done", "ak_done", "att_ready", "x0_ready", "y_ready")}
        z_out = [sem(f"z_out{i}") for i in range(2)]
        z_in, res_loaded, x2_out, gain_loaded, rope_loaded, ln_loaded, x2_in, out_stored = (
            sem(x) for x in ("z_in", "res_loaded", "x2_out", "gain_loaded", "rope_loaded", "ln_loaded", "x2_in",
                             "out_stored"))

        def gemm_product(eng, n):
            eng.wait_ge(gemm_done[n % 2], n // 2 + 1)

        def gemm_consumed(eng, n):
            eng.wait_ge(gemm_read[n % 2], n // 2 + 1)

        def side_product(eng, key):
            p = prod[key]
            eng.wait_ge(side_done[p % 4], p // 4 + 1)
            return S[p % 4]

        def side_consumed(eng, key):
            p = prod[key]
            eng.wait_ge(side_read[p % 4], p // 4 + 1)

        class Steps:

            def __init__(self, eng, own):
                self.eng, self.own, self.count = eng, own, {}

            def __call__(self, ins, name=None):
                s = N[name] if name else self.own
                self.count[name] = self.count.get(name, 0) + 1
                ins.then_inc(s, 1)
                self.eng.wait_ge(s, self.count[name])

            def frees(self, ins, key):
                p = prod[key]
                ins.then_inc(side_read[p % 4], 1)
                self.eng.wait_ge(side_read[p % 4], p // 4 + 1)

            def frees_gemm(self, ins, n):
                ins.then_inc(gemm_read[n % 2], 1)
                self.eng.wait_ge(gemm_read[n % 2], n // 2 + 1)

        block = ctx.enter_context(nc.Block())

        def hslice(c):
            return slice(c * P, (c + 1) * P)

        def widen(ap, n):
            return ap.unsqueeze(2).to_broadcast([P, ap.shape[1], n])

        def over(ap, m):
            return ap.unsqueeze(1).to_broadcast([P, m, ap.shape[1]])

        def stage_of(kd):
            m = stage_uses[kd][0]
            bufs = {"conv": cacc, "sm": cacc, "z": cacc, "av": cacc, "wo": ost, "wo2": fst}.get(kd[0], st2)
            return m, bufs[m % 2]

        def stage_free(eng, m):
            r = stage_reader.get(m - 2)
            if r is not None and (r, 0) in prod:
                p = prod[r, 1 if (r, 1) in prod else 0]
                eng.wait_ge(side_done[p % 4], p // 4 + 1)

        tok_items = {"convT", "zT", "avT", "woT", "v2T", "viT", "wo2T", "q2T"}

        def tok_dest(it, hf):
            kind, j = it
            t = slice(4 * hf, 4 * hf + 4)
            if kind == "convT":
                if j < 4:
                    return xs[:, t, hslice(j)]
                return Bt[:, t, hslice(j - 4)] if j < 6 else qkv[:, t, hslice(j - 8)]
            if kind == "zT":
                return zst[:, hf]
            if kind == "avT":
                return av[:, 1 + 4 * hf:5 + 4 * hf, :]
            return {"woT": mo, "viT": vv, "wo2T": ob}[kind][:, t, hslice(j)] if kind in ("woT", "viT", "wo2T") else \
                {"v2T": v2k, "q2T": tok}[kind][:, t, :]

        norm_src = [xin, x1, x1]
        sq_scratch = [nsq, rsq, rsq]
        act_ready = {("conv", 0): lambda hf: ("norm", (0, hf)), ("wo", 0): lambda hf: ("mx", hf),
                     ("gate", 0): lambda hf: ("norm", (1, hf)), ("q2", 0): lambda hf: ("norm", (2, hf))}

        @block.sync
        def _(sp):
            def bcast(ap, n, off=0):
                return bass.AP(ap.tensor, ap.offset + off, [[0, P], [1, n]])

            for c in range(NT):
                sp.dma_start(xin[:, c, :], a["x"][hslice(c), :]).then_inc(x_loaded[c // 4], 16)
            sp.dma_start(con[:], a["con1"]).then_inc(con_loaded, 16)
            for r0, src in ((0, a["ssd_conv_w"].rearrange("i (j p) -> (i j) p", p=P)),
                            (32, a["gdn_conv_w"].rearrange("i (j p) -> (i j) p", p=P)),
                            (56, a["ssd_conv_b"].rearrange("(j p) -> j p", p=P)),
                            (64, a["pre_mix_norm"].rearrange("(j p) -> j p", p=P)),
                            (72, a["pre_ffn_norm"].rearrange("(j p) -> j p", p=P)),
                            (80, a["norm_gain_2"].rearrange("(j p) -> j p", p=P)),
                            (88, a["b_merge_2"].rearrange("i (j p) -> (i j) p", p=P))):
                sp.dma_start(rows[r0:r0 + src.shape[0], :], src).then_inc(con_loaded, 16)
            sp.dma_start(bias16[:, 0:8], bcast(a["ssd_dt_bias"], 8)).then_inc(small_loaded, 16)
            sp.dma_start(bias16[:, 12:16], bcast(a["gdn_dt_bias"], 4)).then_inc(small_loaded, 16)
            sp.dma_start(alog[:, 0:8], bcast(a["ssd_A_log"], 8)).then_inc(small_loaded, 16)
            sp.dma_start(alog[:, 8:12], bcast(a["gdn_A_log"], 4)).then_inc(small_loaded, 16)
            sp.dma_start(dskip[:], bcast(a["ssd_D"], 8)).then_inc(small_loaded, 16)
            s = a["attn_sinks"]
            for p in range(2):
                sp.dma_start(sinkb[:, 2 * p:2 * p + 2], bass.AP(s.tensor, s.offset + p, [[0, P], [2, 2]]), allow_slow_non_contiguous=True).then_inc(small_loaded, 16)
            for w, (name, kt, row, pieces) in enumerate(ws):
                if w >= 4:
                    sp.wait_ge(w_split, w - 3)
                src = a[name].rearrange("(k p) n -> p k n", p=P)
                dst = raw[w % 4][:].rearrange("p (k n) -> p k n", k=kt)
                o = 0
                for c0, width in pieces:
                    sp.dma_start(dst[:, :, o:o + width], src[:, row:row + kt, c0:c0 + width]).then_inc(raw_loaded[w % 4], 16)
                    o += width
            sp.wait_ge(out_stored, 16 * NT)

        @block.gpsimd
        def _(pool):
            pieces_so_far = [0] * 4
            for w, (name, kt, row, pieces) in enumerate(ws):
                pieces_so_far[w % 4] += len(pieces)
                pool.wait_ge(raw_loaded[w % 4], 16 * pieces_so_far[w % 4])
                if w >= 2:
                    gemm_product(pool, last_unit_of[w - 2])
                nc.gpsimd.tensor_scalar(whi[w % 2][:], raw[w % 4][:], 1.0, 0.0, ALU.mult, ALU.add).then_inc(pool_hi, 1)
                pool.wait_ge(pool_hi, w + 1)
                nc.gpsimd.tensor_tensor(wlo[w % 2][:], raw[w % 4][:], whi[w % 2][:], ALU.subtract).then_inc(w_split, 1)
                pool.wait_ge(w_split, w + 1)

        @block.tensor
        def _(pe):
            mm, tr = nc.tensor.matmul, nc.tensor.transpose

            def bank(key):
                p = prod[key]
                if p >= 4:
                    pe.wait_ge(side_read[p % 4], p // 4)
                return S[p % 4]

            def done(last, key):
                last.then_inc(side_done[prod[key] % 4], 1)

            def unit(n, halves=(0, 1)):
                u = units[n]
                kd, kt, w = u["kind"], u["kt"], u["w"]
                if 0 in halves:
                    pe.wait_ge(w_split, w + 1)
                    if n >= 2:
                        pe.wait_ge(gemm_read[n % 2], n // 2)
                act = {"down": fT, "ya": atT, "yb": gmT}.get(kd[0], hT)
                if kd[0] == "down":
                    pe.wait_ge(N["f_lo"], min(4 * kd[1][0] + 4, NF))
                if kd[0] in ("ya", "yb"):
                    pe.wait_ge(N["split_lo"], 4 if kd[0] == "ya" else 8)
                hi = whi[w % 2][:].rearrange("p (k n) -> p k n", k=kt)
                lo = wlo[w % 2][:].rearrange("p (k n) -> p k n", k=kt)
                m = slice(u["sub"] * P, u["sub"] * P + P)
                for hf in halves:
                    if kd in act_ready:
                        for k in range(4, 8):
                            side_consumed(pe, (act_ready[kd](hf), k))
                    t = slice(hf * 512, hf * 512 + 512)
                    o = G[n % 2][:, t]
                    for k in range(kt):
                        if kd == ("wo2", 0) and hf == 0:
                            pe.wait_ge(N["yT_lo"], k + 1)
                        mm(o, hi[:, k, m], act[0][:, k, t], start=k == 0, stop=False)
                        mm(o, hi[:, k, m], act[1][:, k, t], start=False, stop=False)
                        last = mm(o, lo[:, k, m], act[0][:, k, t], start=False, stop=k == kt - 1)
                if 1 in halves:
                    last.then_inc(gemm_done[n % 2], 1)

            def transposed(it, blocks):
                for h in range(2):
                    b = bank((it, h))
                    for i, x in enumerate(blocks(h)):
                        last = tr(b[:, hslice(i)], x, ident)
                    done(last, (it, h))

            for it in sched:
                kind, j = it
                if kind == "unit":
                    unit(j)
                elif kind == "half":
                    unit(j[0], (j[1],))
                elif kind == "cols":
                    pe.wait_ge(con_loaded, 16 * 8)
                    b = bank((it, 0))
                    done(tr(b[:, 0:104], rows[0:104, :], ident[0:104, 0:104]), (it, 0))
                elif kind == "norm":
                    stage, hf = j
                    pe.wait_ge(N["diag_ready"], 2 * stage + hf + 1)
                    for k in range(KD):
                        b = bank((it, k))
                        for i in range(4):
                            c = 4 * hf + i
                            last = mm(b[:, hslice(i)], norm_src[stage][:, c, hslice(k)], diag[:, c, :], start=True, stop=True)
                        done(last, (it, k))
                elif kind == "mx":
                    pe.wait_ge(N["rec_mix"], 4 * j + 4)
                    side_consumed(pe, (("ao", 4 * j + 3), 0))
                    for k in range(KD):
                        b = bank((it, k))
                        for i in range(4):
                            c = 4 * j + i
                            src = atts[:, c, hslice(k)] if k < 2 else xs[:, c, hslice(k - 2)] if k < 6 else qkv[:, c, hslice(k - 6)]
                            last = tr(b[:, hslice(i)], src, ident)
                        done(last, (it, k))
                elif kind == "smT":
                    gemm_consumed(pe, unit_of["sm", 0])
                    b = bank((it, 0))
                    src = stage_of(("sm", 0))[1]
                    for c in range(NT):
                        last = tr(b[:, 16 * c:16 * c + 16], src[0:16, hslice(c)], ident[0:16, 0:16])
                    done(last, (it, 0))
                elif kind == "acs":
                    pe.wait_ge(N["da_ready"], 1)
                    b = bank((it, 0))
                    done(mm(b[:, 0:96], upper, da[:].rearrange("p c h -> p (c h)"), start=True, stop=True), (it, 0))
                elif kind in ("convT", "zT", "avT", "v2T", "viT", "woT", "wo2T", "q2T"):
                    kd = {"convT": "conv", "zT": "z", "avT": "av", "v2T": "v2", "viT": "vi", "woT": "wo",
                          "wo2T": "wo2", "q2T": "q2"}[kind], j
                    src = stage_of(kd)[1]
                    if kind == "convT":
                        pe.wait_ge(N["conv_act"], j + 1)
                        if j in (4, 5):
                            src = BC[:, j - 4, :]
                    else:
                        gemm_consumed(pe, unit_of[kd])
                    transposed(it, lambda h, src=src: [src[:, (4 * h + i) * P:(4 * h + i + 1) * P] for i in range(4)])
                elif kind == "as":
                    if j == 0:
                        for kd in (("aq", 0), ("aq", 1), ("ak", 0)):
                            gemm_consumed(pe, unit_of[kd])
                    for p in range(2):
                        b = bank((it, p))
                        for kv in range(2):
                            last = mm(b[:, kv * 256:kv * 256 + 256], aqT[:, p, hslice(j)], akT[:, kv, j * P:j * P + 2 * P],
                                      start=True, stop=True)
                        done(last, (it, p))
                elif kind == "ap":
                    pe.wait_ge(N["att_exp"], j + 1)
                    for p in range(2):
                        b = bank((it, p))
                        for i in range(4):
                            last = tr(b[:, hslice(i)], asb[:, 2 * p + i // 2, hslice(i % 2)], ident)
                        done(last, (it, p))
                elif kind == "ao":
                    if j == 0:
                        side_consumed(pe, (("avT", 0), 0))
                        side_consumed(pe, (("avT", 0), 1))
                    side_consumed(pe, (("ap", j), 0))
                    side_consumed(pe, (("ap", j), 1))
                    b = bank((it, 0))
                    for i in range(4):
                        p, kv = i // 2, i % 2
                        h = p + 2 * kv
                        for s in range(2):
                            last = mm(b[:, h * 64:h * 64 + 64], apT[:, i, s, :], av[:, j + s, kv * 64:kv * 64 + 64],
                                      start=s == 0, stop=s == 1)
                    done(last, (it, 0))
                elif kind == "ra":
                    c, z = j, j % 2
                    for key in products_of(it):
                        b = bank((it, key))
                        if key[:2] == "bc":
                            i = int(key[2])
                            if c == 0 and i == 0:
                                pe.wait_ge(N["da_ready"], 1)
                            mm(b[:].rearrange("p (h n) -> p h n", h=4), identb[:], over(negb[:], 4), start=True, stop=False)
                            for h in range(4):
                                last = mm(b[:, hslice(h)], da[:, c, 4 * i + h:4 * i + h + 1].to_broadcast([P, P]), upper,
                                          start=False, stop=h == 3)
                        elif key == "kT":
                            pe.wait_ge(N["rec_kb"], c + 1)
                            for p in range(2):
                                tr(b[:, hslice(p)], qkv[:, c, 256 + p * P:256 + (p + 1) * P], ident)
                            for p in range(2):
                                last = tr(b[:, hslice(2 + p)], kbv[z][:, 0, hslice(p)], ident)
                        elif key == "qT":
                            for p in range(2):
                                last = tr(b[:, hslice(p)], qkv[:, c, hslice(p)], ident)
                        elif key == "g":
                            for g in range(2):
                                last = mm(b[:, hslice(g)], BC[:, g, hslice(c)], BC[:, 2 + g, hslice(c)], start=True, stop=True)
                        elif key[:2] == "kq":
                            p = int(key[2])
                            if p == 0:
                                side_consumed(pe, (it, "kT"))
                                side_consumed(pe, (it, "qT"))
                            for h in range(2):
                                last = mm(b[:, h * 256:h * 256 + 256], kTp[z][:, 2 * p + h, :],
                                          kq[z][:, p, :, :].rearrange("p a n -> p (a n)"), start=True, stop=True)
                        elif key == "xT":
                            pe.wait_ge(N["rec_x0"], c + 1)
                            for h in range(4):
                                last = tr(b[:, hslice(h)], XT[z][:, h, :], ident)
                        done(last, (it, key))
                elif kind == "ly":
                    c, lv = j
                    z = c % 2
                    side_consumed(pe, (("ra", c), "xT") if lv == 1 else (("lx", (c, lv - 1)), "x"))
                    b = bank((it, 0))
                    for h in range(4):
                        last = mm(b[:, hslice(h)], SQ[z][:, h, 0, :], X[z][:, h, :], start=True, stop=True)
                    done(last, (it, 0))
                elif kind == "lx":
                    c, lv = j
                    z = c % 2
                    side_consumed(pe, (("ly", j), 0))
                    if lv > 1:
                        side_consumed(pe, (("lx", (c, lv - 1)), "t"))
                    for key in products_of(it):
                        b = bank((it, key))
                        for h in range(4):
                            l, r = (XT, Y) if key == "x" else (Y, XT)
                            last = mm(b[:, hslice(h)], l[z][:, h, :], r[z][:, h, :], start=True, stop=True)
                        done(last, (it, key))
                elif kind in ("uw", "yo", "yd", "st", "r1", "r2"):
                    c, z = j, j % 2
                    b = bank((it, 0))
                    if kind == "yo":
                        if c > 0:
                            side_consumed(pe, (("st", c - 1), 0))
                        for g in range(2):
                            last = mm(b[:, g * 256:g * 256 + 256], BC[:, 2 + g, hslice(c)], Sst[:, g * 256:g * 256 + 256],
                                      start=True, stop=True)
                    elif kind == "yd":
                        for h in range(8):
                            last = mm(b[:, h * 64:h * 64 + 64], E[z][:, h, :], xc[z][:, 0, h * 64:h * 64 + 64], start=True, stop=True)
                    elif kind == "st":
                        for g in range(2):
                            last = mm(b[:, g * 256:g * 256 + 256], Bt[:, c, hslice(g)], xc[z][:, 1, g * 256:g * 256 + 256],
                                      start=True, stop=True)
                    elif kind == "uw":
                        side_consumed(pe, (("lx", (c, 6)), "t"))
                        for h in range(4):
                            mm(b[:, h * 64:h * 64 + 64], XT[z][:, h, :], kbv[z][:, 1, h * 64:h * 64 + 64], start=True, stop=True)
                        for h in range(4):
                            r = 64 * (h % 2)
                            last = mm(b[r:r + 64, 256 + (h // 2) * P:256 + (h // 2) * P + P], kbv[z][:, 2, h * 64:h * 64 + 64],
                                      XT[z][:, h, :], start=True, stop=True)
                    elif kind == "r1":
                        side_consumed(pe, (("uw", c), 0))
                        if c > 0:
                            pe.wait_ge(N["rec_S"], c)
                        for p in range(2):
                            mm(b[:, hslice(p)], uw[z][:, 256 + p * P:256 + (p + 1) * P], Sbd[:, p, :], start=True, stop=True)
                        for p in range(2):
                            last = mm(b[:, hslice(2 + p)], kq[z][:, p, 1, :], Sbd[:, p, :], start=True, stop=True)
                    elif kind == "r2":
                        pe.wait_ge(N["rec_vn"], c + 1)
                        for h in range(4):
                            mm(b[:, h * 64:h * 64 + 64], SQ[z][:, h, 1, :], vn[:, h * 64:h * 64 + 64], start=True, stop=True)
                        for p in range(2):
                            last = mm(b[:, hslice(2 + p)], kbv[z][:, 3, hslice(p)], vn[:, hslice(p)], start=True, stop=True)
                    done(last, (it, 0))
                elif kind == "downT":
                    gemm_consumed(pe, unit_of["down", (5, 6)])
                    gemm_consumed(pe, unit_of["down", (5, 7)])
                    for n in range(8):
                        c, hf = 4 * j + n // 2, n % 2
                        b = bank((it, n))
                        for i in range(4):
                            last = tr(b[:, hslice(i)], accT[:, 4 * hf + i, hslice(c)], ident)
                        done(last, (it, n))
                elif kind == "q2B":
                    pe.wait_ge(N["rope_done"], j + 1)
                    transposed(it, lambda h: [rp1[:, 4 * h + i, :] for i in range(4)])
                elif kind == "ln":
                    pe.wait_ge(ln_loaded, 16 * 5)
                    transposed(it, lambda h: [wsr[:, 4 * h + i, :] for i in range(4)])
                elif kind == "a2s":
                    c, h = j // 8, j % 8
                    if j == 0:
                        for q in range(5):
                            for s in range(2):
                                side_consumed(pe, (("q2B", q), s))
                    for s in range(2):
                        b = bank((it, s))
                        done(mm(b[:], qT2[:, h % 4, hslice(c)], kT2[:, h // 4, s * 512:s * 512 + 512], start=True, stop=True), (it, s))
                elif kind == "a2x":
                    for s in range(2):
                        side_consumed(pe, (("a2s", j), s))
                    for s in range(2):
                        b = bank((it, s))
                        for i in range(4):
                            last = tr(b[:, hslice(i)], Pb[j % 2][:, (4 * s + i) * P:(4 * s + i + 1) * P], ident)
                        done(last, (it, s))
                elif kind == "a2o":
                    for s in range(2):
                        side_consumed(pe, (("a2x", j), s))
                    b = bank((it, 0))
                    for i in range(NT):
                        last = mm(b[:, 0:P], PT[j % 2][:, i, :], v2k[:, i, :], start=i == 0, stop=i == NT - 1)
                    done(last, (it, 0))
                elif kind == "a2t":
                    side_consumed(pe, (("a2o", 8 * j + 7), 0))
                    b = bank((it, 0))
                    for i in range(4):
                        last = tr(b[:, hslice(i)], ot[:, hslice(i)], ident)
                    done(last, (it, 0))
                elif kind == "sp":
                    if j == 0:
                        pe.wait_ge(N["ln_done"], 1)
                        side_consumed(pe, (("ln", 0), 0))
                        side_consumed(pe, (("ln", 0), 1))
                    b = bank((it, 0))
                    for g in range(8):
                        r = 64 * (g % 2)
                        last = mm(b[r:r + 64, hslice(g // 2)], vv[:, j, g * 64:g * 64 + 64], wsT[:, g, :], start=True, stop=True)
                    done(last, (it, 0))

        @block.scalar
        def _(act):
            step = Steps(act, act_step)
            af = nc.scalar.activation

            def tokens_copied(it, hf):
                b = side_product(act, (it, hf))
                if it[0] == "zT" and it[1] > 0:
                    act.wait_ge(z_out[hf], 16 * it[1])
                step.frees(af(tok_dest(it, hf), b[:].rearrange("p (c n) -> p c n", c=4), ACT.Copy), (it, hf))

            def z_store(it, hf):
                j = it[1]
                dst = z_dram[hf * 512:hf * 512 + 512, hslice(j)].rearrange("(c p) n -> p c n", p=P)
                act.dma_start(dst, zst[:, hf]).then_inc(z_out[hf], 16)

            def squares(src, scratch, tiles):
                for c in tiles:
                    ins = af(scratch, src[:, c, :], ACT.Square, accum_out=ss[:, c:c + 1])
                    step(ins, "ss_ready" if c == tiles[-1] else None)

            def unit(n):
                kd = units[n]["kind"]
                kind, j = kd
                g = G[n % 2]
                if kind == "conv":
                    m, buf = stage_of(kd)
                    if j > 0:
                        act.wait_ge(N["conv_acc"], j)
                    gemm_product(act, n)
                    stage_free(act, m)
                    bcol, wcol = (56 + j, 24 + j) if j < 8 else (104, 50 + j - 8)
                    step(af(cin[:, 3:3 + T], g[:], ACT.Copy))
                    step.frees_gemm(af(buf[:], g[:], ACT.Identity, bias=cols[:, bcol:bcol + 1], scale=cols[:, wcol:wcol + 1]), n)
                    act.wait_ge(N["conv_acc"], j + 1)
                    step(af(BC[:, j - 4, :] if 4 <= j < 8 else buf[:], buf[:], ACT.Silu), "conv_act")
                elif kind == "sm":
                    m, buf = stage_of(kd)
                    gemm_product(act, n)
                    stage_free(act, m)
                    step.frees_gemm(af(buf[0:16, :], g[0:16, :], ACT.Copy), n)
                elif kind in ("z", "av", "wo", "q2", "v2", "vi", "wo2"):
                    m, buf = stage_of(kd)
                    gemm_product(act, n)
                    stage_free(act, m)
                    f = {"z": ACT.Silu, "vi": ACT.Gelu_apprx_tanh}.get(kind, ACT.Copy)
                    step.frees_gemm(af(buf[:], g[:], f), n)
                elif kind == "aq":
                    gemm_product(act, n)
                    step.frees_gemm(af(aqT[:, j, :], g[:], ACT.Copy), n)
                elif kind == "ak":
                    gemm_product(act, n)
                    step(af(akT[0:64, 0, P:], g[0:64, :], ACT.Copy))
                    step.frees_gemm(af(akT[64:P, 1, P:], g[64:P, :], ACT.Copy), n)
                elif kind == "gate":
                    gemm_product(act, n)
                    if j >= 2:
                        gemm_consumed(act, unit_of["up", j - 2])
                    step.frees_gemm(af(sg[j % 2][:], g[:], ACT.Silu), n)
                elif kind == "up":
                    gemm_consumed(act, n)
                    step(af(fT[0][:, j % 4, :], ft[:], ACT.Copy), "f_hi")
                elif kind == "down" and j[0] == 0:
                    gemm_product(act, n)
                    step.frees_gemm(af(accT[:, j[1], :], g[:], ACT.Copy), n)
                elif kind in ("ga", "u2"):
                    gemm_product(act, n)
                    dst, f = (gaT, ACT.Silu) if kind == "ga" else (uT, ACT.Gelu_apprx_tanh)
                    step.frees_gemm(af(dst[:, j, :], g[:], f), n)
                elif kind == "gb":
                    gemm_product(act, n)
                    if j > 0:
                        act.wait_ge(N["gb_used"], j)
                    step.frees_gemm(af(gbt[:], g[:], ACT.Silu), n)
                elif kind in ("sga", "sgb"):
                    gemm_product(act, n)
                    i = 0 if kind == "sga" else 1
                    if j >= 2:
                        act.wait_ge(N["y_done"], j - 1)
                    step.frees_gemm(af(sig[i][j % 2][:], g[:], ACT.Sigmoid, bias=cols[:, 88 + 8 * i + j:89 + 8 * i + j]), n)

            for it in sched:
                kind, j = it
                if kind == "unit":
                    unit(j)
                elif kind == "half":
                    if j[1]:
                        unit(j[0])
                elif kind == "norm":
                    stage, hf = j
                    if stage == 0:
                        act.wait_ge(x_loaded[hf], 16 * 4)
                        act.wait_ge(N["init_done"], 1)
                    else:
                        act.wait_ge(N["resid_done"], 2 * stage - 1 + hf)
                    squares(norm_src[stage], sq_scratch[stage][:], range(4 * hf, 4 * hf + 4))
                    for k in range(KD):
                        b = side_product(act, (it, k))
                        g0 = 64 + 8 * stage + k
                        step(af(hT[0][:, k, hf * 512:hf * 512 + 512], b[:], ACT.Identity, scale=cols[:, g0:g0 + 1]), "hi_ready")
                elif kind == "mx":
                    for k in range(KD):
                        b = side_product(act, (it, k))
                        step(af(hT[0][:, k, j * 512:j * 512 + 512], b[:], ACT.Copy), "hi_ready")
                elif kind == "smT":
                    act.wait_ge(small_loaded, 16 * 7)
                    step(af(easm[:], alog[:], ACT.Exp))
                    act.wait_ge(N["sm_abs"], 1)
                    step(af(sm[2][:], sm[1][:], ACT.Exp, scale=-1.0), "sm_exp")
                elif kind == "acs":
                    act.wait_ge(N["sm_arg"], 1)
                    step(af(beta[:], sm[3][:, :, 8:12], ACT.Exp), "beta_ready")
                    side_consumed(act, (it, 0))
                    step(af(eacs[:], nacs[:], ACT.Exp, scale=-1.0), "eacs_ready")
                elif kind in tok_items and kind != "wo2T":
                    tokens_copied(it, 0)
                    if kind == "zT":
                        z_store(it, 0)
                        side_consumed(act, (it, 1))
                        z_store(it, 1)
                elif kind == "as":
                    act.wait_ge(N["att_max"], j + 1)
                    for i in range(4):
                        step(af(asb[:, i, :], asb[:, i, :], ACT.Exp, bias=anm[:, i:i + 1], accum_out=asum[:, i:i + 1]))
                    step(af(ads[:], ads[:], ACT.Exp), "att_exp")
                elif kind == "ap":
                    b = side_product(act, (it, 0))
                    if j > 0:
                        side_product(act, (("ao", j - 1), 0))
                    step.frees(af(apT[:, 0:2], b[:].rearrange("p (i s n) -> p i s n", i=2, s=2), ACT.Copy), (it, 0))
                elif kind == "ra":
                    c, z = j, j % 2
                    if c == 0:
                        act.wait_ge(z_out[0], 16 * 6)
                        act.wait_ge(z_out[1], 16 * 6)
                        act.wait_ge(N["init_done"], 2)
                        src = a["ssd_norm_w"]
                        act.dma_start(gmix[:, 0:512], bass.AP(src.tensor, src.offset, [[0, P], [1, 512]])).then_inc(gain_loaded, 16)
                        src = a["gdn_norm_w"]
                        act.dma_start(gmix[:, 512:768].rearrange("p (h d) -> p h d", h=4),
                                      bass.AP(src.tensor, src.offset, [[0, P], [0, 4], [1, 64]])).then_inc(gain_loaded, 16)
                        act.dma_start(zt[:], z_dram[0:P, :]).then_inc(z_in, 16)
                    if c >= 2:
                        act.wait_ge(N["rec_mix"], c - 1)
                    for i in range(3):
                        b = side_product(act, (it, f"bc{i}"))
                        for h in range(4):
                            step(af(E[z][:, 4 * i + h, :], b[:, hslice(h)], ACT.Exp, bias=nacs[:, c, 4 * i + h:4 * i + h + 1]))
                        step.frees(af(cd[z][:, 4 * i:4 * i + 4], b[:].rearrange("p (h n) -> p h n", h=4)[:, :, P - 1], ACT.Exp), (it, f"bc{i}"))
                    b = side_product(act, (it, "kT"))
                    v = b[:].rearrange("p (i n) -> p i n", i=4)
                    kv = kTp[z][:].rearrange("p (a b) n -> p a b n", b=2)
                    step(af(kv[0:64, :, 0, :], v[0:64, 0:2, :], ACT.Copy))
                    step(af(kv[64:P, :, 1, :], v[64:P, 0:2, :], ACT.Copy))
                    step.frees(af(kq[z][:, :, 0, :], v[:, 2:4, :], ACT.Copy), (it, "kT"))
                    b = side_product(act, (it, "xT"))
                    step.frees(af(X[z][:], b[:].rearrange("p (i n) -> p i n", i=4), ACT.Copy), (it, "xT"))
                elif kind == "uw":
                    b = side_product(act, (it, 0))
                    step.frees(af(uw[j % 2][:], b[:], ACT.Copy), (it, 0))
                elif kind == "rn" and j + 1 < NT:
                    act.wait_ge(N["rec_mix"], j + 1)
                    act.dma_start(zt[:], z_dram[hslice(j + 1), :]).then_inc(z_in, 16)
                elif kind == "load":
                    if j == 0:
                        for k in range(4, 8):
                            side_consumed(act, (("mx", 1), k))
                        act.dma_start(x1[:], a["x"].rearrange("(c p) n -> p c n", p=P)).then_inc(res_loaded, 16)
                        for i, name in ((0, "post_mix_norm"),):
                            src = a[name]
                            act.dma_start(gbc[:, i, :], bass.AP(src.tensor, src.offset, [[0, P], [1, D]])).then_inc(res_loaded, 16)
                    elif j == 1:
                        pass
                    elif j == 2:
                        act.dma_start(x2_dram.rearrange("(c p) n -> p c n", p=P), x1[:]).then_inc(x2_out, 16)
                        act.dma_start(rope[:].rearrange("p a c n -> p (a c n)"), a["con2"]).then_inc(rope_loaded, 16)
                        for i, name in enumerate(("q_gain_2", "k_gain_2")):
                            src = a[name]
                            act.dma_start(qkg[:, i, :], bass.AP(src.tensor, src.offset, [[0, P], [1, 64]])).then_inc(rope_loaded, 16)
                    elif j == 3:
                        for q in range(5):
                            side_consumed(act, (("q2B", q), 1))
                        for v in range(4):
                            for h in range(2):
                                side_consumed(act, (("viT", v), h))
                        act.dma_start(wsr[:], a["w_spatial_2"].rearrange("g i j -> i g j")).then_inc(ln_loaded, 16)
                        src = a["b_spatial_2"]
                        for h in range(2):
                            act.dma_start(bsp[64 * h:64 * h + 64], bass.AP(src.tensor, src.offset + h * P, [[0, 64], [2 * P, 4], [1, P]])).then_inc(ln_loaded, 16)
                        for i, name in enumerate(("ln_v_gain_2", "ln_v_bias_2")):
                            src = a[name]
                            act.dma_start(lnp[:, i, :], bass.AP(src.tensor, src.offset, [[0, P], [1, 512]])).then_inc(ln_loaded, 16)
                    elif j == 4:
                        gemm_consumed(act, unit_of["yb", 7])
                        gemm_consumed(act, unit_of["yb", 6])
                        act.dma_start(x2[:], x2_dram.rearrange("(c p) n -> p c n", p=P)).then_inc(x2_in, 16)
                        src = a["final_gain_2"]
                        act.dma_start(fgb[:], bass.AP(src.tensor, src.offset, [[0, P], [1, D]])).then_inc(x2_in, 16)
                elif kind == "resid":
                    r, hf = j
                    if r == 0:
                        for h in range(2):
                            side_consumed(act, (("woT", 7), h))
                    else:
                        for k in range(4, 8):
                            side_consumed(act, (("downT", hf), k))
                        if hf == 0:
                            src = a["post_ffn_norm"]
                            act.dma_start(gbc2[:], bass.AP(src.tensor, src.offset, [[0, P], [1, D]])).then_inc(gain_loaded, 16)
                    squares(mo if r == 0 else fo, rsq[:], range(4 * hf, 4 * hf + 4))
                elif kind == "downT":
                    for n in range(0, 8, 2):
                        b = side_product(act, (it, n))
                        step.frees(af(fo[:, 4 * j + n // 2, 0:512], b[:], ACT.Copy), (it, n))
                elif kind == "q2B":
                    if j == 0:
                        act.wait_ge(x2_out, 16)
                    b = side_product(act, (it, 0))
                    if j < 4:
                        step.frees(af(qT2[:, j, 0:512], b[:], ACT.Copy), (it, 0))
                    else:
                        step(af(kT2[0:64, 0, 0:512], b[0:64, :], ACT.Copy))
                        step.frees(af(kT2[64:P, 1, 0:512], b[64:P, :], ACT.Copy), (it, 0))
                elif kind == "ln":
                    b = side_product(act, (it, 0))
                    step.frees(af(wsT[:, 0:4], b[:].rearrange("p (i n) -> p i n", i=4), ACT.Copy), (it, 0))
                    act.wait_ge(N["mean_done"], 1)
                    squares(vv, lsq[:], range(NT))
                elif kind == "a2s":
                    act.wait_ge(N["a2_max"], j + 1)
                    if j >= 2:
                        side_product(act, (("a2x", j - 2), 1))
                    for s in range(2):
                        b = side_product(act, (it, s))
                        step.frees(af(Pb[j % 2][:, s * 512:s * 512 + 512], b[:], ACT.Exp, bias=a2m[:, 4 + j % 2:5 + j % 2], scale=0.125,
                                      accum_out=a2s_[:, j % 2, s:s + 1]), (it, s))
                elif kind == "a2x":
                    if j >= 2:
                        side_product(act, (("a2o", j - 2), 0))
                    b = side_product(act, (it, 0))
                    step.frees(af(PT[j % 2][:, 0:4, :], b[:].rearrange("p (i n) -> p i n", i=4), ACT.Copy), (it, 0))
                elif kind in ("split4", "splity"):
                    for k in range(8):
                        if kind == "split4":
                            if k == 0:
                                side_consumed(act, (("sp", 7), 0))
                                act.wait_ge(N["y_ready"], 1)
                            step(af((atT if k < 4 else gmT)[0][:, k % 4, :], (gaT if k < 4 else uT)[:, k % 4, :], ACT.Copy), "split_hi")
                        else:
                            if k == 0:
                                act.wait_ge(N["y_done"], 8)
                            step(af(hT[0][:, k, :], yT[:, k, :], ACT.Copy), "yT_hi")
                elif kind == "final":
                    for h in range(2):
                        side_consumed(act, (("wo2T", 7), h))
                    side_product(act, (("wo2T", 7), 1))
                    squares(ob, fst[0][:], range(4 * j, 4 * j + 4))
                    for c in range(4 * j, 4 * j + 4):
                        act.wait_ge(N["final_done"], c + 1)
                        act.dma_start(out[hslice(c), :], ob[:, c, :]).then_inc(out_stored, 16)

        @block.vector
        def _(dve):
            step = Steps(dve, dve_step)
            v = nc.vector
            hi_count = [0]
            ss_count = [0]

            def sums_ready():
                ss_count[0] += 1
                dve.wait_ge(N["ss_ready"], ss_count[0])


            def rsqrt(dst, src, scale, name=None):
                x, t = nv[:, 0:src.shape[1]], nt_[:, 0:src.shape[1]]
                step(v.tensor_scalar(x, src, scale, EPS, ALU.mult, ALU.add))
                step(v.tensor_scalar(dst.bitcast(I32), x.bitcast(I32), -0.5, float(0x5F3759DF), ALU.mult, ALU.add))
                step(v.tensor_scalar(x, x, -0.5, None, ALU.mult))
                for i in range(3):
                    step(v.tensor_tensor(t, x, dst, ALU.mult))
                    step(v.tensor_tensor(t, t, dst, ALU.mult))
                    step(v.scalar_tensor_tensor(out=dst, in0=t, scalar=1.5, in1=dst, op0=ALU.add, op1=ALU.mult),
                         name if i == 2 else None)

            def low(dst, b, hi, key=None, gain=None):
                hi_count[0] += 1
                dve.wait_ge(N["hi_ready"], hi_count[0])
                if gain is None:
                    ins = v.tensor_tensor(dst, b, hi, ALU.subtract)
                else:
                    ins = v.scalar_tensor_tensor(out=dst, in0=b, scalar=gain, in1=hi, op0=ALU.mult, op1=ALU.subtract)
                step.frees(ins, key)

            def h64(x):
                return x.rearrange("p (h d) -> p h d", d=64)

            def four(b):
                return b[:].rearrange("p (h n) -> p h n", h=4)

            def unit(n):
                kd = units[n]["kind"]
                kind, j = kd
                g = G[n % 2]
                if kind == "conv":
                    m, buf = stage_of(kd)
                    gemm_consumed(dve, n)
                    for i in range(3):
                        wcol = i * 8 + j if j < 8 else 32 + i * 6 + j - 8
                        step(v.scalar_tensor_tensor(out=buf[:], in0=cin[:, i:i + T], scalar=cols[:, wcol:wcol + 1], in1=buf[:],
                                                    op0=ALU.mult, op1=ALU.add), "conv_acc" if i == 2 else None)
                elif kind == "up":
                    gemm_consumed(dve, unit_of["gate", j])
                    gemm_product(dve, n)
                    step.frees_gemm(v.tensor_tensor(ft[:], sg[j % 2][:], g[:], ALU.mult), n)
                    dve.wait_ge(N["f_hi"], j + 1)
                    step(v.tensor_tensor(fT[1][:, j % 4, :], ft[:], fT[0][:, j % 4, :], ALU.subtract), "f_lo")
                elif kind == "down" and j[0] > 0:
                    gemm_consumed(dve, unit_of["down", (j[0] - 1, j[1])])
                    gemm_product(dve, n)
                    step.frees_gemm(v.tensor_tensor(accT[:, j[1], :], accT[:, j[1], :], g[:], ALU.add), n)
                elif kind == "gb":
                    gemm_consumed(dve, n)
                    gemm_consumed(dve, unit_of["u2", j])
                    step(v.tensor_tensor(uT[:, j, :], uT[:, j, :], gbt[:], ALU.mult), "gb_used")
                elif kind == "ya":
                    gemm_consumed(dve, unit_of["sga", j])
                    gemm_product(dve, n)
                    step.frees_gemm(v.tensor_tensor(yT[:, j, :], sig[0][j % 2][:], g[:], ALU.mult), n)
                elif kind == "yb":
                    gemm_consumed(dve, unit_of["sgb", j])
                    gemm_product(dve, n)
                    step.frees_gemm(v.tensor_tensor(sig[1][j % 2][:], sig[1][j % 2][:], g[:], ALU.mult), n)
                    step(v.tensor_tensor(yT[:, j, :], yT[:, j, :], sig[1][j % 2][:], ALU.add), "y_done")

            step(v.memset(cols[:, 104:105], 0.0))
            step(v.memset(cin[:, 0:3], 0.0))
            step(v.memset(bias16[:, 8:12], 0.0))
            dve.wait_ge(con_loaded, 16 * 8)
            step(v.tensor_copy(identb[:], ident))
            step(v.tensor_copy(negb[:], con[:, C_NEG:C_NEG + P]))
            b = side_product(dve, (("cols", 0), 0))
            step.frees(v.tensor_copy(cols[:, 0:104], b[:, 0:104]), (("cols", 0), 0))
            dve.wait_ge(small_loaded, 16 * 7)
            step(v.memset(nt_[:], 0.0), "init_done")

            for it in sched:
                kind, j = it
                if kind == "unit":
                    unit(j)
                elif kind == "half":
                    if j[1]:
                        unit(j[0])
                elif kind == "norm":
                    stage, hf = j
                    h4 = slice(4 * hf, 4 * hf + 4)
                    sums_ready()
                    rsqrt(rs[:, h4], ss[:, h4], 1.0 / D)
                    for c in range(4 * hf, 4 * hf + 4):
                        step(v.tensor_scalar(diag[:, c, :], ident, rs[:, c:c + 1], None, ALU.mult),
                             "diag_ready" if c % 4 == 3 else None)
                    t = slice(hf * 512, hf * 512 + 512)
                    for k in range(KD):
                        b = side_product(dve, (it, k))
                        g0 = 64 + 8 * stage + k
                        low(hT[1][:, k, t], b[:], hT[0][:, k, t], (it, k), cols[:, g0:g0 + 1])
                elif kind == "mx":
                    t = slice(j * 512, j * 512 + 512)
                    for k in range(KD):
                        b = side_product(dve, (it, k))
                        low(hT[1][:, k, t], b[:], hT[0][:, k, t], (it, k))
                elif kind == "smT":
                    x, t1, e, s, s2, p = (t[:] for t in sm)
                    b = side_product(dve, (it, 0))
                    step.frees(v.tensor_tensor(x, b[:, 0:P].rearrange("p (c h) -> p c h", c=NT), over(bias16[:], NT), ALU.add), (it, 0))
                    step(v.tensor_scalar(t1, x, -1.0, None, ALU.mult))
                    step(v.tensor_tensor(t1, t1, x, ALU.max), "sm_abs")
                    dve.wait_ge(N["sm_exp"], 1)
                    step(v.tensor_scalar(s, e, 2.0, None, ALU.add))
                    step(v.reciprocal(s, s))
                    step(v.tensor_tensor(s, s, e, ALU.mult))
                    step(v.tensor_tensor(s2, s, s, ALU.mult))
                    step(v.tensor_scalar(p, s2, 1.0 / 19, None, ALU.mult))
                    for n in range(8, 0, -1):
                        step(v.scalar_tensor_tensor(out=p, in0=p, scalar=1.0 / (2 * n + 1), in1=s2, op0=ALU.add, op1=ALU.mult))
                    step(v.scalar_tensor_tensor(out=p, in0=p, scalar=1.0, in1=s, op0=ALU.add, op1=ALU.mult))
                    step(v.tensor_scalar(t1, x, 0.0, None, ALU.max))
                    step(v.scalar_tensor_tensor(out=dts[:], in0=p, scalar=2.0, in1=t1, op0=ALU.mult, op1=ALU.add))
                    step(v.tensor_tensor(s, x, dts[:], ALU.subtract), "sm_arg")
                    step(v.tensor_scalar(easm[:], easm[:], -1.0, None, ALU.mult))
                    step(v.tensor_tensor(da[:, :, 0:8], dts[:, :, 0:8], over(easm[:, 0:8], NT), ALU.mult))
                    step(v.tensor_tensor(da[:, :, 8:12], dts[:, :, 12:16], over(easm[:, 8:12], NT), ALU.mult), "da_ready")
                elif kind == "acs":
                    b = side_product(dve, (it, 0))
                    step.frees(v.tensor_scalar(nacs[:].rearrange("p c h -> p (c h)"), b[:, 0:96], -1.0, None, ALU.mult), (it, 0))
                elif kind == "wo2T":
                    if j == 0:
                        dve.wait_ge(x2_in, 32)
                    for h in range(2):
                        b = side_product(dve, (it, h))
                        d = tok_dest(it, h)
                        step.frees(v.tensor_tensor(d, b[:].rearrange("p (c n) -> p c n", c=4), x2[:, 4 * h:4 * h + 4, hslice(j)], ALU.add), (it, h))
                elif kind in tok_items:
                    b = side_product(dve, (it, 1))
                    if kind == "zT" and j > 0:
                        dve.wait_ge(z_out[1], 16 * j)
                    step.frees(v.tensor_copy(tok_dest(it, 1), b[:].rearrange("p (c n) -> p c n", c=4)), (it, 1))
                    if kind == "q2T":
                        side_consumed(dve, (it, 0))
                        if j == 0:
                            dve.wait_ge(rope_loaded, 16 * 3)
                        tk = tok[:].rearrange("p c (h d) -> p (c h) d", d=64)
                        r1, r2 = (t[:].rearrange("p c n -> p (c n)") for t in (rp1, rp2))
                        step(v.tensor_tensor(rp2[:], tok[:], tok[:], ALU.mult))
                        step(v.reduce_sum(rr[:, 0:16], rp2[:].rearrange("p c (h d) -> p (c h) d", d=64), axis=AX))
                        rsqrt(rr[:, 16:32], rr[:, 0:16], 1.0 / 64)
                        step(v.tensor_tensor(tk, tk, widen(rr[:, 16:32], 64), ALU.mult))
                        step(v.tensor_tensor(tk, tk, over(qkg[:, j // 4, :], 16), ALU.mult))
                        if j > 0:
                            side_product(dve, (("q2B", j - 1), 1))
                        step(v.tensor_tensor(rp1[:], tok[:], rope[:, 0], ALU.mult))
                        sw = tok[:].rearrange("p c (g x n) -> p (c g) x n", x=2, n=16)
                        sn = rope[:, 1].rearrange("p c (g x n) -> p (c g) x n", x=2, n=16)
                        ro = rp2[:].rearrange("p c (g x n) -> p (c g) x n", x=2, n=16)
                        for x in range(2):
                            step(v.tensor_tensor(ro[:, :, x, :], sw[:, :, 1 - x, :], sn[:, :, x, :], ALU.mult))
                        step(v.tensor_tensor(r1, r1, r2, ALU.add), "rope_done")
                elif kind == "prep":
                    qk = qkv[:, :, 0:512]
                    for h in range(2):
                        for q in (8, 9, 10, 11):
                            side_consumed(dve, (("convT", q), h))
                    step(v.tensor_tensor(psq[:], qk, qk, ALU.mult))
                    step(v.reduce_sum(rr[:].rearrange("p (c h) -> p c h", c=NT), psq[:].rearrange("p c (h d) -> p c h d", d=64), axis=AX))
                    rsqrt(psq[:, 0, 0:64], rr[:], 1.0)
                    r = psq[:, 0, 0:64].rearrange("p (c h) -> p c h", c=NT)
                    step(v.tensor_scalar(r[:, :, 0:4], r[:, :, 0:4], 0.125, None, ALU.mult))
                    for c in range(NT):
                        q = qkv[:, c, 0:512].rearrange("p (h d) -> p h d", d=64)
                        step(v.tensor_tensor(q, q, widen(r[:, c, :], 64), ALU.mult))
                    step(v.memset(akT[:], 0.0))
                    step(v.memset(av[:, 0, :], 0.0), "prep_done")
                elif kind == "as":
                    c = j
                    if c > 0:
                        side_product(dve, (("ap", c - 1), 1))
                    for p in range(2):
                        b = side_product(dve, (it, p))
                        bb = b[:].rearrange("p (i n) -> p i n", i=2)
                        al = con[:, C_ALI + 512 * p:C_ALI + 512 * p + 512].rearrange("p (i n) -> p i n", i=2)
                        n0 = P if c == 0 else 0
                        if c == 0:
                            step(v.memset(asb[:, 2 * p:2 * p + 2, 0:P], NEG))
                        step.frees(v.scalar_tensor_tensor(out=asb[:, 2 * p:2 * p + 2, n0:], in0=bb[:, :, n0:], scalar=0.125,
                                                          in1=al[:, :, n0:], op0=ALU.mult, op1=ALU.add), (it, p))
                    step(v.reduce_max(amx[:], asb[:], axis=AX))
                    step(v.tensor_tensor(amx[:], amx[:], sinkb[:], ALU.max))
                    step(v.tensor_scalar(anm[:], amx[:], -1.0, None, ALU.mult))
                    step(v.tensor_tensor(ads[:], sinkb[:], amx[:], ALU.subtract), "att_max")
                elif kind == "ap":
                    dve.wait_ge(N["att_exp"], j + 1)
                    step(v.tensor_tensor(aden[:], asum[:], ads[:], ALU.add))
                    step(v.reciprocal(aden[:], aden[:]))
                    b = side_product(dve, (it, 1))
                    step.frees(v.tensor_copy(apT[:, 2:4], b[:].rearrange("p (i s n) -> p i s n", i=2, s=2)), (it, 1))
                elif kind == "ao":
                    b = side_product(dve, (it, 0))
                    for p in range(2):
                        o = atts[:, j, :].rearrange("p (k q d) -> p q k d", k=2, q=2)[:, p]
                        s = b[:, 0:256].rearrange("p (k q d) -> p q k d", k=2, q=2)[:, p]
                        ins = v.tensor_tensor(o, s, widen(aden[:, 2 * p:2 * p + 2], 64), ALU.mult)
                        if p == 0:
                            step(ins)
                        else:
                            step.frees(ins, (it, 0))
                elif kind == "ra":
                    c, z = j, j % 2
                    if c == 0:
                        for u in range(4):
                            gemm_product(dve, unit_of["av", 0] - u)
                        step(v.memset(kTp[0][:], 0.0))
                        step(v.memset(kTp[1][:], 0.0))
                        step(v.memset(Sbd[:], 0.0))
                        step(v.memset(Sst[:], 0.0), "init_done")
                        dve.wait_ge(N["eacs_ready"], 1)
                        step(v.tensor_tensor(bge[:], beta[:], eacs[:, :, 8:12], ALU.mult))
                    k_, v_, x_ = h64(qkv[:, c, 256:512]), h64(qkv[:, c, 512:768]), h64(xs[:, c, :])
                    kb4 = [h64(kbv[z][:, i, :]) for i in range(4)]
                    step(v.tensor_tensor(kb4[1], v_, widen(beta[:, c, :], 64), ALU.mult))
                    step(v.tensor_tensor(kb4[2], k_, widen(bge[:, c, :], 64), ALU.mult))
                    step(v.tensor_tensor(kb4[0], k_, widen(beta[:, c, :], 64), ALU.mult), "rec_kb")
                    step(v.tensor_tensor(h64(xc[z][:, 0]), x_, widen(dts[:, c, 0:8], 64), ALU.mult))
                    for i in range(3):
                        side_consumed(dve, (it, f"bc{i}"))
                    b = side_product(dve, (it, "qT"))
                    step.frees(v.tensor_copy(kq[z][:, :, 1, :], b[:, 0:256].rearrange("p (a n) -> p a n", a=2)), (it, "qT"))
                    step(v.tensor_tensor(kb4[3], k_, widen(E[z][:, 8:12, P - 1], 64), ALU.mult))
                    step(v.tensor_tensor(h64(xc[z][:, 1]), h64(xc[z][:, 0]), widen(E[z][:, 0:8, P - 1], 64), ALU.mult))
                    for r in range(2):
                        step(v.tensor_copy(cdc[z][64 * r:64 * r + 64, :], cd[z][64 * r:64 * r + 64, 8:12].rearrange("p (a b) -> p a b", b=2)[:, :, r]))
                    b = side_product(dve, (it, "g"))
                    step(v.tensor_tensor(E[z][:, 0:4, :], E[z][:, 0:4, :], over(b[:, 0:P], 4), ALU.mult))
                    step.frees(v.tensor_tensor(E[z][:, 4:8, :], E[z][:, 4:8, :], over(b[:, P:2 * P], 4), ALU.mult), (it, "g"))
                    for p in range(2):
                        b = side_product(dve, (it, f"kq{p}"))
                        e = E[z][:, 8 + 2 * p:10 + 2 * p, :].unsqueeze(2).to_broadcast([P, 2, 2, P])
                        step.frees(v.tensor_tensor(SQ[z][:, 2 * p:2 * p + 2], b[:].rearrange("p (h a n) -> p h a n", h=2, a=2), e, ALU.mult), (it, f"kq{p}"))
                    step(v.tensor_tensor(XT[z][:], SQ[z][:, :, 0, :], over(con[:, C_LV:C_LV + P], 4), ALU.mult))
                    step(v.scalar_tensor_tensor(out=XT[z][:], in0=XT[z][:], scalar=-1.0, in1=over(ident, 4), op0=ALU.mult, op1=ALU.add), "rec_x0")
                elif kind == "ly":
                    c, lv = j
                    b = side_product(dve, (it, 0))
                    step.frees(v.tensor_tensor(Y[c % 2][:], four(b), over(con[:, C_LV + lv * P:C_LV + (lv + 1) * P], 4), ALU.mult), (it, 0))
                elif kind == "lx":
                    c, lv = j
                    z = c % 2
                    side_product(dve, (it, "t"))
                    if lv == 1:
                        side_consumed(dve, (("ra", c), "xT"))
                    if lv < 6:
                        b = side_product(dve, (it, "x"))
                        step.frees(v.tensor_tensor(X[z][:], X[z][:], four(b), ALU.subtract), (it, "x"))
                    b = side_product(dve, (it, "t"))
                    step.frees(v.tensor_tensor(XT[z][:], XT[z][:], four(b), ALU.subtract), (it, "t"))
                elif kind == "r1":
                    c, z = j, j % 2
                    side_consumed(dve, (("uw", c), 0))
                    b = side_product(dve, (it, 0))
                    step(v.tensor_tensor(vn[:], uw[z][:, 0:256], b[:, 0:256], ALU.subtract), "rec_vn")
                    step.frees(v.tensor_tensor(h64(o1[:]), h64(b[:, 256:512]), widen(eacs[:, c, 8:12], 64), ALU.mult), (it, 0))
                elif kind == "r2":
                    c, z = j, j % 2
                    b = side_product(dve, (it, 0))
                    step(v.tensor_tensor(mix[:, 512:768], o1[:], b[:, 0:256], ALU.add))
                    step.frees(v.tensor_tensor(tS[:], b[:, 256:512].rearrange("p (a n) -> p a n", a=2), over(blk, 2), ALU.mult), (it, 0))
                    for p in range(2):
                        step(v.scalar_tensor_tensor(out=Sbd[:, p, :], in0=Sbd[:, p, :], scalar=cdc[z][:, p:p + 1], in1=tS[:, p, :],
                                                    op0=ALU.mult, op1=ALU.add), "rec_S" if p else None)
                elif kind == "yo":
                    c, z = j, j % 2
                    b = side_product(dve, (it, 0))
                    step.frees(v.tensor_tensor(h64(mix[:, 0:512]), h64(b[:]), widen(eacs[:, c, 0:8], 64), ALU.mult), (it, 0))
                    step(v.tensor_tensor(h64(Sst[:]), h64(Sst[:]), widen(cd[z][:, 0:8], 64), ALU.mult))
                elif kind == "yd":
                    b = side_product(dve, (it, 0))
                    step.frees(v.tensor_tensor(mix[:, 0:512], mix[:, 0:512], b[:], ALU.add), (it, 0))
                elif kind == "st":
                    c, z = j, j % 2
                    b = side_product(dve, (it, 0))
                    step.frees(v.tensor_tensor(Sst[:], Sst[:], b[:], ALU.add), (it, 0))
                    side_product(dve, (("uw", c), 0))
                    step(v.tensor_tensor(h64(msq[z][:, 0:512]), h64(xs[:, c, :]), widen(dskip[:], 64), ALU.mult))
                    step(v.tensor_tensor(mix[:, 0:512], mix[:, 0:512], msq[z][:, 0:512], ALU.add))
                    dve.wait_ge(z_in, 16 * (c + 1))
                    step(v.tensor_tensor(mix[:, 0:512], mix[:, 0:512], zt[:, 0:512], ALU.mult))
                elif kind == "rn":
                    c, z = j, j % 2
                    step(v.tensor_tensor(msq[z][:], mix[:], mix[:], ALU.mult))
                    step(v.reduce_sum(nss[:, 0:2], msq[z][:, 0:512].rearrange("p (g n) -> p g n", g=2), axis=AX))
                    step(v.reduce_sum(nss[:, 2:6], h64(msq[z][:, 512:768]), axis=AX))
                    step(v.tensor_scalar(nss[:, 0:2], nss[:, 0:2], 0.25, None, ALU.mult))
                    rsqrt(nrs, nss, 1.0 / 64)
                    m2, m4 = mix[:, 0:512].rearrange("p (g n) -> p g n", g=2), h64(mix[:, 512:768])
                    step(v.tensor_tensor(m2, m2, widen(nrs[:, 0:2], 256), ALU.mult))
                    step(v.tensor_tensor(m4, m4, widen(nrs[:, 2:6], 64), ALU.mult))
                    step(v.tensor_tensor(mix[:, 512:768], mix[:, 512:768], zt[:, 512:768], ALU.mult))
                    dve.wait_ge(gain_loaded, 32)
                    step(v.tensor_tensor(xs[:, c, :], mix[:, 0:512], gmix[:, 0:512], ALU.mult))
                    step(v.tensor_tensor(qkv[:, c, 0:256], mix[:, 512:768], gmix[:, 512:768], ALU.mult), "rec_mix")
                elif kind == "resid":
                    r, hf = j
                    h4 = slice(4 * hf, 4 * hf + 4)
                    sums_ready()
                    rsqrt(rs[:, h4], ss[:, h4], 1.0 / D)
                    src = mo if r == 0 else fo
                    if r == 0:
                        dve.wait_ge(res_loaded, 32)
                    else:
                        dve.wait_ge(gain_loaded, 48)
                    gb = gbc[:, 0, :] if r == 0 else gbc2[:]
                    for c in range(4 * hf, 4 * hf + 4):
                        step(v.scalar_tensor_tensor(out=src[:, c, :], in0=src[:, c, :], scalar=rs[:, c:c + 1], in1=gb,
                                                    op0=ALU.mult, op1=ALU.mult))
                        step(v.tensor_tensor(x1[:, c, :], x1[:, c, :], src[:, c, :], ALU.add), "resid_done" if c % 4 == 3 else None)
                elif kind == "downT":
                    for n in range(1, 8, 2):
                        b = side_product(dve, (it, n))
                        step.frees(v.tensor_copy(fo[:, 4 * j + n // 2, 512:1024], b[:]), (it, n))
                elif kind == "q2B":
                    if j == 0:
                        dve.wait_ge(x2_out, 16)
                    b = side_product(dve, (it, 1))
                    if j < 4:
                        step.frees(v.tensor_copy(qT2[:, j, 512:1024], b[:]), (it, 1))
                    else:
                        step(v.memset(kT2[64:P, 0, :], 0.0))
                        step(v.memset(kT2[0:64, 1, :], 0.0))
                        step(v.tensor_copy(kT2[0:64, 0, 512:1024], b[0:64, :]))
                        step.frees(v.tensor_copy(kT2[64:P, 1, 512:1024], b[64:P, :]), (it, 1))
                elif kind == "ln":
                    b = side_product(dve, (it, 1))
                    step.frees(v.tensor_copy(wsT[:, 4:8], b[:].rearrange("p (i n) -> p i n", i=4)), (it, 1))
                    for q in range(4):
                        side_consumed(dve, (("viT", q), 0))
                    step(v.reduce_sum(mean[:], vv[:], axis=AX))
                    step(v.tensor_scalar(mean[:], mean[:], -1.0 / 512, None, ALU.mult))
                    for c in range(NT):
                        step(v.tensor_scalar(vv[:, c, :], vv[:, c, :], mean[:, c:c + 1], None, ALU.add), "mean_done" if c == NT - 1 else None)
                    sums_ready()
                    rsqrt(rs[:], ss[:], 1.0 / 512)
                    for c in range(NT):
                        step(v.scalar_tensor_tensor(out=vv[:, c, :], in0=vv[:, c, :], scalar=rs[:, c:c + 1], in1=lnp[:, 0, :],
                                                    op0=ALU.mult, op1=ALU.mult))
                        step(v.tensor_tensor(vv[:, c, :], vv[:, c, :], lnp[:, 1, :], ALU.add), "ln_done" if c == NT - 1 else None)
                elif kind == "a2s":
                    m = a2m[:, 2 * (j % 2):2 * (j % 2) + 2]
                    for s in range(2):
                        b = side_product(dve, (it, s))
                        step(v.reduce_max(m[:, s:s + 1], b[:], axis=AX))
                    if j >= 2:
                        side_consumed(dve, (("a2s", j - 2), 1))
                    d = a2m[:, 4 + j % 2:5 + j % 2]
                    step(v.tensor_scalar(d, m[:, 0:1], m[:, 1:2], -0.125, ALU.max, ALU.mult), "a2_max")
                elif kind == "a2x":
                    b = side_product(dve, (it, 1))
                    if j >= 2:
                        side_product(dve, (("a2o", j - 2), 0))
                    step.frees(v.tensor_copy(PT[j % 2][:, 4:8, :], b[:].rearrange("p (i n) -> p i n", i=4)), (it, 1))
                    r = a2r[:, j % 2:j % 2 + 1]
                    side_consumed(dve, (("a2s", j), 0))
                    side_consumed(dve, (("a2s", j), 1))
                    step(v.tensor_tensor(r, a2s_[:, j % 2, 0:1], a2s_[:, j % 2, 1:2], ALU.add))
                    step(v.reciprocal(r, r))
                elif kind == "a2o":
                    h = j % 8
                    kv = h // 4
                    b = side_product(dve, (it, 0))
                    step.frees(v.tensor_scalar(ot[:, h * 64:h * 64 + 64], b[:, kv * 64:kv * 64 + 64], a2r[:, j % 2:j % 2 + 1], None, ALU.mult), (it, 0))
                elif kind == "a2t":
                    if j == 0:
                        for q in range(4):
                            gemm_consumed(dve, unit_of["ga", q])
                    b = side_product(dve, (it, 0))
                    step.frees(v.tensor_tensor(gaT[:, :, hslice(j)], gaT[:, :, hslice(j)], b[:].rearrange("p (i n) -> p i n", i=4), ALU.mult), (it, 0))
                elif kind == "sp":
                    b = side_product(dve, (it, 0))
                    step.frees(v.tensor_tensor(spt[:], b[:].rearrange("p (i n) -> p i n", i=4), bsp[:], ALU.add), (it, 0))
                    step(v.tensor_tensor(uT[:, :, hslice(j)], uT[:, :, hslice(j)], spt[:], ALU.mult), "y_ready" if j == NT - 1 else None)
                elif kind in ("split4", "splity"):
                    for k in range(8):
                        if kind == "split4":
                            dve.wait_ge(N["split_hi"], k + 1)
                            d = atT if k < 4 else gmT
                            step(v.tensor_tensor(d[1][:, k % 4, :], (gaT if k < 4 else uT)[:, k % 4, :], d[0][:, k % 4, :], ALU.subtract), "split_lo")
                        else:
                            dve.wait_ge(N["yT_hi"], k + 1)
                            step(v.tensor_tensor(hT[1][:, k, :], yT[:, k, :], hT[0][:, k, :], ALU.subtract), "yT_lo")
                elif kind == "final":
                    sums_ready()
                    h4 = slice(4 * j, 4 * j + 4)
                    rsqrt(rs[:, h4], ss[:, h4], 1.0 / D)
                    for c in range(4 * j, 4 * j + 4):
                        step(v.scalar_tensor_tensor(out=ob[:, c, :], in0=ob[:, c, :], scalar=rs[:, c:c + 1], in1=fgb[:],
                                                    op0=ALU.mult, op1=ALU.mult), "final_done")



def kernel(**inputs):
    import concourse.bacc as bacc
    from concourse.bass_utils import run_bass_kernel_spmd

    nc = bacc.Bacc("TRN2", target_bir_lowering=False, num_devices=1, dynamic_dma_scratch_size=SWDGE_RING)
    arrays, aps = {}, {}
    for name, value in inputs.items():
        v = np.ascontiguousarray(value)
        arrays[f"in_{name}"] = v
        ap = nc.dram_tensor(f"in_{name}", v.shape, mybir.dt.from_np(v.dtype), kind="ExternalInput").ap()
        aps[name] = ap[0] if name != "final_gain_2" else ap
    for name, v in zip(("con1", "con2"), consts_of_shapes()):
        arrays[name] = v
        aps[name] = nc.dram_tensor(name, v.shape, F32, kind="ExternalInput").ap()
    out = nc.dram_tensor("out", (1, T, D), F32, kind="ExternalOutput").ap()
    build_program(nc, aps, out[0])
    r = run_bass_kernel_spmd(nc, [arrays], core_ids=[0])
    return r.results[0]["out"]
```

```python
from contextlib import ExitStack

import numpy as np
import concourse.bass as bass
from concourse import mybir

F32 = mybir.dt.float32
F32R = mybir.dt.float32r
BF16 = mybir.dt.bfloat16
I32 = mybir.dt.int32
ALU = mybir.AluOpType
ACT = mybir.ActivationFunctionType
AX = mybir.AxisListType.X

P = 128
T = 1024
NT = T // P
D = 1024
KD = D // P
FF = 2816
NF = FF // P
EPS = 1e-6
NEG = -1e30
SWDGE_RING = 1024
SBUF_BASE = SWDGE_RING + 128

O_AQ, O_AK, O_AV, O_SZ, O_XBC, O_DT, O_QKV, O_GZ, O_B = 0, 256, 384, 512, 1024, 2048, 2056, 2824, 3080
O2_Q, O2_K, O2_V, O2_GA, O2_U, O2_VI, O2_GB, O2_M = 0, 512, 640, 768, 1280, 1792, 2304, 2816


def consts_of_shapes():
    i = np.arange(P)
    ident = np.eye(P)
    upper = (i[:, None] <= i[None, :]).astype(float)
    block = (i[:, None] // 64 == i[None, :] // 64).astype(float)
    levels = []
    for b in range(7):
        n = 1 << b
        m = ((i[:, None] // (2 * n) == i[None, :] // (2 * n)) & (i[:, None] // n % 2 == 1) & (i[None, :] // n % 2 == 0))
        levels.append(m.T if b == 0 else m)
    neg = np.where(upper > 0, 0.0, NEG)
    j = np.arange(2 * P)
    dist = np.abs(i[:, None] + P - j[None, :])
    seen = np.where(i[:, None] < 64, j[None, :] < 192, j[None, :] >= 64)
    alibi = [np.where(seen, -(2.0 ** (-2.0 * (h + 1))) * dist, NEG) for h in (0, 2, 1, 3)]
    c1 = np.concatenate([ident, upper, block, *levels, neg, *alibi], axis=1).astype(np.float32)
    t = np.arange(T)
    inv = (10000.0 ** (-np.arange(0, 32, 2, dtype=np.float32) / 32)).astype(np.float32)
    ang = np.stack([(t // 64).astype(np.float32)[:, None] * inv, (t % 64).astype(np.float32)[:, None] * inv], 1)
    cos, sin = np.cos(ang), np.sin(ang)
    ct = np.stack([cos, cos], 2).reshape(T, 64)
    st = np.stack([-sin, sin], 2).reshape(T, 64)
    two = [np.tile(m, (1, 2)).reshape(NT, P, 2 * 64).transpose(1, 0, 2).reshape(P, NT * P) for m in (ct, st)]
    return np.ascontiguousarray(c1), np.ascontiguousarray(np.concatenate(two, 1).astype(np.float32))


C_ID, C_UP, C_BLK, C_LV, C_NEG, C_ALI = 0, 128, 256, 384, 384 + 7 * 128, 512 + 7 * 128
C_END = C_ALI + 4 * 256


def weight_units():
    ws, units = [], []

    def add(name, kt, row, pieces, kinds):
        ws.append((name, kt, row, pieces))
        per = (1024 // kt) // P
        assert len(kinds) == per
        for s, kind in enumerate(kinds):
            units.append(dict(w=len(ws) - 1, kt=kt, sub=s, kind=kind, last=s == per - 1))

    for j in range(4):
        add("w_in", 8, 0, [(O_XBC + 128 * j, 128)], [("conv", j)])
    for j in range(4, 8):
        add("w_in", 8, 0, [(O_XBC + 128 * j, 128)], [("conv", j)])
    for j in range(6):
        add("w_in", 8, 0, [(O_QKV + 128 * j, 128)], [("conv", 8 + j)])
    add("w_in", 8, 0, [(O_DT, 8), (O_B, 8), (0, 112)], [("sm", 0)])
    for j in range(4):
        add("w_in", 8, 0, [(O_SZ + 128 * j, 128)], [("z", j)])
    for j in range(2):
        add("w_in", 8, 0, [(O_GZ + 128 * j, 128)], [("z", 4 + j)])
    for j in range(2):
        add("w_in", 8, 0, [(O_AQ + 64 * j, 64), (O_AQ + 64 * (j + 2), 64)], [("aq", j)])
    add("w_in", 8, 0, [(O_AK, 128)], [("ak", 0)])
    add("w_in", 8, 0, [(O_AV, 128)], [("av", 0)])
    for j in range(8):
        add("w_out", 8, 0, [(128 * j, 128)], [("wo", j)])
    groups = ffn_groups()

    def gate(f):
        add("ffn_w_gate", 8, 0, [(128 * f, 128)], [("gate", f)])

    def up(f):
        add("ffn_w_up", 8, 0, [(128 * f, 128)], [("up", f)])

    gate(0)
    for g, (f0, n) in enumerate(groups):
        up(f0)
        for f in range(f0 + 1, f0 + n):
            gate(f)
            up(f)
        if g + 1 < len(groups):
            gate(f0 + n)
        per = (1024 // n) // P
        for j in range(8 // per):
            add("ffn_w_down", n, f0, [(j * 1024 // n, 1024 // n)],
                [("down", (g, j * per + s)) for s in range(per)])
    add("w_in_2", 8, 0, [(O2_K, 128)], [("q2", 4)])
    for j in range(4):
        add("w_in_2", 8, 0, [(O2_Q + 128 * j, 128)], [("q2", j)])
    add("w_in_2", 8, 0, [(O2_V, 128)], [("v2", 0)])
    add("w_in_2", 8, 0, [(O2_GA, 128)], [("ga", 0)])
    for o, kind in ((O2_VI, "vi"), (O2_GA, "ga"), (O2_U, "u2"), (O2_GB, "gb")):
        for j in range(kind == "ga", 4):
            add("w_in_2", 8, 0, [(o + 128 * j, 128)], [(kind, j)])
    for j in range(0, 8, 2):
        for s in range(2):
            add("w_in_2", 8, 0, [(O2_M + 128 * (j + s), 128)], [("sga", j + s)])
        for s in range(2):
            add("w_in_2", 8, 0, [(O2_M + 1024 + 128 * (j + s), 128)], [("sgb", j + s)])
        add("w_proj_attn_2", 4, 0, [(128 * j, 256)], [("ya", j), ("ya", j + 1)])
        add("w_proj_gmlp_2", 4, 0, [(128 * j, 256)], [("yb", j), ("yb", j + 1)])
    for j in range(8):
        add("w_out_2", 8, 0, [(128 * j, 128)], [("wo2", j)])
    return ws, units


def ffn_groups():
    return [(f, min(4, NF - f)) for f in range(0, NF, 4)]


def schedule(units):
    by = {u["kind"]: n for n, u in enumerate(units)}
    s, late, begun = [], [], set()

    def begin(kds, before, between):
        begun.update(kds)
        s.extend(before + [("half", (by[kd], 0)) for kd in kds] + between + [("half", (by[kd], 1)) for kd in kds])

    def run(kinds, after=lambda kd: []):
        for kd in kinds:
            if kd not in begun:
                s.append(("unit", by[kd]))
            s.extend([x for d, x in late if d <= 0])
            late[:] = [(d - 1, x) for d, x in late if d > 0] + list(after(kd))

    def flush():
        s.extend([it for _, it in sorted(late, key=lambda x: x[0])])
        late.clear()

    s.append(("cols", 0))
    begin([("conv", 0), ("conv", 1)], [("norm", (0, 0))], [("norm", (0, 1))])
    run([("conv", j) for j in range(14)], lambda kd: [(0, ("convT", kd[1]))] if kd[1] not in (6, 7) else [])
    run([("sm", 0)], lambda kd: [(0, ("smT", 0)), (1, ("prep", 0)), (2, ("acs", 0))])
    run([("z", j) for j in range(6)], lambda kd: [(0, ("zT", kd[1]))])
    run([("aq", 0), ("aq", 1), ("ak", 0)])
    run([("av", 0)], lambda kd: [(0, ("avT", 0))])
    flush()
    s += [(k, 0) for k in ("ra", "rk", "rj", "rx")]
    for c in range(NT + 1):
        fill = [[] for _ in range(13)]
        if c > 0:
            for i, k in enumerate(("r1", "yo", "yd", "r2", "st")):
                fill[i].append((k, c - 1))
            if c + 1 < NT:
                fill[8].append(("ra", c + 1))
            if c < NT:
                fill[8] += [("rq", c - 1), ("rn", c - 1)]
        if c < NT:
            fill[5].append(("as", c))
            fill[7].append(("ap", c))
            fill[9].append(("ao", c))
        if c == 0:
            fill[8].append(("ra", 1))
        if c + 1 < NT:
            for i, k in ((9, "rk"), (11, "rj"), (12, "rx")):
                fill[i].append((k, c + 1))
        s.extend(fill[0])
        for lv in range(1, 7):
            if c < NT:
                s.append(("ly", (c, lv)))
            s.extend(fill[2 * lv - 1])
            if c < NT:
                s.append(("lx", (c, lv)))
            s.extend(fill[2 * lv])
        if c < NT:
            s.append(("uw", c))
    begin([("wo", 0), ("wo", 1)], [("mx", 0)], [("rq", NT - 1), ("rn", NT - 1), ("mx", 1), ("load", 0)])
    run([("wo", j) for j in range(8)], lambda kd: [(0, ("woT", kd[1]))])
    flush()
    begin([("gate", 0), ("up", 0)], [("resid", (0, 0)), ("norm", (1, 0)), ("resid", (0, 1))], [("norm", (1, 1))])
    s.append(("load", 5))
    run([u["kind"] for u in units if u["kind"][0] in ("gate", "up", "down")],
        lambda kd: [(0, ("downT", kd[1][1]))] if kd[0] == "down" and kd[1][0] == len(ffn_groups()) - 1 else [])
    flush()
    begin([("q2", 4), ("q2", 0)], [("resid", (1, 0)), ("norm", (2, 0)), ("load", 1), ("resid", (1, 1))],
          [("norm", (2, 1)), ("load", 2)])
    run([("q2", j) for j in (4, 0, 1, 2, 3)], lambda kd: [(0, ("q2T", kd[1])), (1, ("q2B", kd[1]))])
    run([("v2", 0)], lambda kd: [(0, ("v2T", 0))])
    run([("ga", 0)])
    flush()
    pairs = NT * 4

    def scores(n):
        return [("a2s", n)] if n < 2 * pairs else []

    def exps(n):
        return [("a2e", n)] if n < 2 * pairs else []

    s += [("a2s", 0), ("a2s", 1), ("a2e", 0), ("a2s", 2), ("a2e", 1), ("a2s", 3), ("a2x", (0, 0)), ("a2e", 2),
          ("a2x", (0, 1)), ("a2s", 4), ("a2e", 3)]
    for m in range(pairs):
        nxt = m + 1 < pairs
        s += [("a2x", (m, 2))] + [("a2v", (m, 0)), ("a2x", (m, 3))] + exps(2 * m + 4) + [("a2v", (m, 1))] + scores(2 * m + 5)
        s += [("a2x", (m + 1, 0))] * nxt + [("a2v", (m, 2))] + [("a2x", (m + 1, 1))] * nxt
        s += [("a2v", (m, 3))] + exps(2 * m + 5) + scores(2 * m + 6)
        s += [("a2t", m // 4 - 1)] * (m % 4 == 0 and m > 0) + [("a2o", m)]
    s += [("a2t", NT - 1), ("load", 3)]
    run([("vi", j) for j in range(4)], lambda kd: [(0, ("viT", kd[1]))])
    run([("ga", 1)], lambda kd: [(0, ("ln", 0))])
    run([("ga", 2), ("ga", 3)])
    run([("u2", j) for j in range(4)])
    run([("gb", 0)], lambda kd: [(0, ("sp", c)) for c in range(4)])
    run([("gb", 1)], lambda kd: [(0, ("sp", c)) for c in range(4, 8)])
    run([("gb", 2), ("gb", 3)])
    s.append(("split4", 0))
    for j in range(0, 8, 2):
        run([("sga", j), ("sga", j + 1), ("sgb", j), ("sgb", j + 1), ("ya", j), ("ya", j + 1), ("yb", j), ("yb", j + 1)])
    s += [("splity", 0), ("load", 4)]
    run([("wo2", j) for j in range(8)], lambda kd: [(0, ("wo2T", kd[1]))])
    flush()
    s.append(("final", 0))
    return s


def products_of(item):
    kind, a = item
    made = {"ra": ["bc0", "bc1", "bc2"], "rk": ["kT", "qT", "g"], "rj": ["kq0", "kq1"], "rx": ["xT"]}
    if kind in made:
        return made[kind]
    if kind == "lx":
        return ["x", "t"] if a[1] < 6 else ["t"]
    return list(range({"cols": 1, "norm": 8, "mx": 8, "smT": 1, "acs": 1, "convT": 2, "zT": 2, "avT": 2, "woT": 2,
                       "downT": 2, "q2T": 2, "q2B": 4, "v2T": 2, "viT": 2, "ln": 2, "a2x": 1, "a2v": 0 if kind != "a2v" or a[1] else 1, "a2o": 1,
                       "a2t": 1, "sp": 1, "wo2T": 2, "ly": 1, "uw": 1, "yo": 1, "yd": 1, "st": 1, "r1": 1, "r2": 1,
                       "as": 2, "ap": 2, "ao": 1}.get(kind, 0)))


def build_program(nc, a, out):
    ws, units = weight_units()
    unit_of = {u["kind"]: n for n, u in enumerate(units)}
    last_unit_of = {u["w"]: n for n, u in enumerate(units) if u["last"]}
    sched = schedule(units)
    assert [x[1] if x[0] == "unit" else x[1][0] for x in sched if x[0] == "unit" or x[0] == "half" and x[1][1]] \
        == list(range(len(units)))
    prod, n = {}, 0
    for it in sched:
        for key in products_of(it):
            prod[it, key] = n
            n += 1
    stage_uses = {}
    for it in sched:
        if it[0] == "unit" or it[0] == "half" and it[1][1]:
            kd = units[it[1] if it[0] == "unit" else it[1][0]]["kind"]
            reader = {"conv": "convT", "sm": "smT", "z": "zT", "av": "avT", "wo": "woT", "q2": "q2T", "v2": "v2T", "vi": "viT",
                      "wo2": "wo2T"}.get(kd[0])
            if reader:
                stage_uses[kd] = (len(stage_uses), (reader, kd[1]))
    stage_reader = {m: r for m, r in stage_uses.values()}

    z_dram = nc.dram_tensor("z_spill", [T, 768], F32).ap()
    x2_dram = nc.dram_tensor("x2_spill", [T, D], F32).ap()

    ctx = ExitStack()
    with ctx:
        def sem(name):
            return ctx.enter_context(nc.semaphore(name))

        def sbuf(name, shape, kb, dt=F32):
            return nc.alloc_sbuf_tensor_at(name, [P] + list(shape), dt, offset=SBUF_BASE + int(kb * 1024), align_bytes=8)

        hT = [sbuf("h_hi", [KD, T], 0, F32R), sbuf("h_lo", [KD, T], 32, F32R)]
        raw = [sbuf(f"w_raw{i}", [1024], 64 + 4 * i) for i in range(4)]
        whi = [sbuf(f"w_hi{i}", [1024], 80 + 4 * i, F32R) for i in range(2)]
        wlo = [sbuf(f"w_lo{i}", [1024], 88 + 4 * i, F32R) for i in range(2)]
        con = sbuf("con", [C_END], 96)
        ident = con[:, C_ID:C_ID + P]
        upper = con[:, C_UP:C_UP + P]
        blk = con[:, C_BLK:C_BLK + P]
        identb = sbuf("identb", [P], 105.5, BF16)
        negb = sbuf("negb", [P], 105.75, BF16)
        cols = sbuf("cols", [112], 106)
        bias16 = sbuf("bias16", [16], 106.5)
        alog = sbuf("alog", [12], 106.5625)
        dskip = sbuf("dskip", [8], 106.625)
        sinkb = sbuf("sinkb", [4], 106.6875)
        ss = sbuf("ss", [NT], 106.75)
        rs = sbuf("rs", [NT], 106.8125)
        nv = sbuf("nv", [64], 106.875)
        nt_ = sbuf("nt_", [64], 107.125)
        mean = sbuf("mean", [NT], 107.375)
        a2m = sbuf("a2m", [4], 107.4375)
        a2d = sbuf("a2d", [8], 107.5)
        a2r = sbuf("a2r", [2], 107.625)
        rs_res = sbuf("rs_res", [NT], 107.65625)
        rr = sbuf("rr", [64], 107.75)
        diag = sbuf("diag", [NT, P], 218.75)

        xin = sbuf("xin", [NT, D], 108)
        nsq = sbuf("nsq", [D], 176)
        BC = sbuf("BC", [4, T], 108)
        xs = sbuf("xs", [NT, 512], 124)
        Bt = sbuf("Bt", [NT, 256], 140)
        qkv = sbuf("qkv", [NT, 768], 148)
        aqT = sbuf("aqT", [2, T], 172)
        akT = sbuf("akT", [2, P + T], 180)
        av = sbuf("av", [1 + NT, P], 189)
        da = sbuf("da", [NT, 12], 193.5)
        nacs = sbuf("nacs", [NT, 12], 193.875)
        eacs = sbuf("eacs", [NT, 12], 194.25)
        dts = sbuf("dts", [NT, 16], 194.625)
        beta = sbuf("beta", [NT, 4], 195.125)
        bge = sbuf("bge", [NT, 4], 195.25)
        cin = sbuf("cin", [3 + T], 196)
        cacc = [sbuf(f"cacc{i}", [T], 200.5 + 4 * i) for i in range(2)]
        zst = sbuf("zst", [2, 4, P], 208.5)
        sm = [sbuf(f"sm{i}", [NT, 16], 212.5 + 0.5 * i) for i in range(6)]
        rows = sbuf("rows", [P], 217)
        easm = sbuf("easm", [12], 217.5)
        psq = sbuf("psq", [NT, 512], 172)

        asb = sbuf("asb", [4, 256], 195.5)
        apT = sbuf("apT", [4, 2, P], 199.5)
        atts = sbuf("atts", [NT, 256], 203.5)
        amx = sbuf("amx", [4], 221.5)
        anm = sbuf("anm", [4], 221.5625)
        ads = sbuf("ads", [4], 221.625)
        asum = sbuf("asum", [4], 221.6875)
        aden = sbuf("aden", [4], 221.75)

        def slots(name, shape, kb):
            return [sbuf(f"{name}{i}", shape, kb + 30 * i) for i in range(2)]

        E = slots("E", [12, P], 0)
        kTp = slots("kTp", [4, P], 6)
        kq = slots("kq", [2, 2, P], 8)
        SQ = slots("SQ", [4, 2, P], 10)
        X = slots("X", [4, P], 14)
        XT = slots("XT", [4, P], 16)
        Y = slots("Y", [4, P], 18)
        kbv = slots("kbv", [4, 256], 20)
        uw = slots("uw", [512], 24)
        xc = slots("xc", [2, 512], 26)
        msq = slots("msq", [768], 14)
        msq7 = sbuf("msq7", [768], 195.5)
        vn = sbuf("vn", [256], 60)
        Sbd = sbuf("Sbd", [2, P], 61)
        Sst = sbuf("Sst", [512], 62)
        cd = [sbuf(f"cd{i}", [12], 195.375 + i * 0.046875) for i in range(2)]
        ed = [sbuf(f"ed{i}", [12], 221.8125 + i * 0.046875) for i in range(2)]
        cdc = [sbuf(f"cdc{i}", [2], 195.46875 + i * 0.0078125) for i in range(2)]
        nss, nrs = rr[:, 0:6], rr[:, 6:12]
        o1 = sbuf("o1", [256], 211.5)
        tS = sbuf("tS", [2, P], 211.5)
        mix = sbuf("mix", [768], 212.5)
        zt = sbuf("zt", [768], 215.5)
        gmix = sbuf("gmix", [768], 218.5)

        mo = sbuf("mo", [NT, D], 108)
        x1 = sbuf("x1", [NT, D], 140)
        ost = [sbuf(f"ost{i}", [T], 172 + 4 * i) for i in range(2)]
        gbc = sbuf("gbc", [D], 180)
        fT = [sbuf("f_hi", [4, T], 108, F32R), sbuf("f_lo", [4, T], 124, F32R)]
        accT = sbuf("accT", [KD, T], 172)
        sg = [sbuf(f"sg{i}", [T], 204 + 4 * i) for i in range(2)]
        ft = sbuf("ft", [T], 212)
        fo = [sbuf(f"fo{i}", [NT, 2, 512], 32 * i)[:, :, 1, :] for i in range(2)]
        rsq = sbuf("rsq", [D], 212)
        gbc2 = sbuf("gbc2", [D], 216)
        sqp = sbuf("sqp", [P], 220.25)
        ssp = rr[:].rearrange("p (c j) -> p c j", c=NT)

        aoT = sbuf("aoT", [4, T], 108)
        qp = sbuf("qp", [8, T], 124, F32R)
        kp = sbuf("kp", [2, 2, T], 156, F32R)
        vp = sbuf("vp", [NT, 2, P], 172, F32R)
        st2 = [sbuf(f"st2_{i}", [T], 180 + 4 * i) for i in range(2)]
        tok = sbuf("tok", [NT, P], 188)
        rp1 = sbuf("rp1", [NT, P], 192)
        rope = sbuf("rope", [2, NT, P], 196)
        rp2 = sbuf("rp2", [NT, P], 204)
        rpd = sbuf("rpd", [NT, 2, 2, 64], 208)
        fold = sbuf("fold", [P], 216)
        qkg = sbuf("qkg", [2, 64], 216.5)
        Pb = [sbuf(f"Pb{i}", [T], 180 + 4 * i) for i in range(4)]
        PT = [[sbuf(f"PT{i}_{k}", [512], 196 + 4 * i + 2 * k, F32R) for k in range(2)] for i in range(4)]
        ot = sbuf("ot", [512], 212)
        ovt = [sbuf(f"ovt{i}", [256], 214 + i) for i in range(2)]

        uT = sbuf("uT", [4, T], 124)
        vv = sbuf("vv", [NT, 512], 140)
        gaT = sbuf("gaT", [3, T], 156)
        gaT0 = sbuf("gaT0", [T], 218.75)
        wsr = sbuf("wsr", [8, P], 188)
        wsT = sbuf("wsT", [8, P], 192)
        bsp = sbuf("bsp", [4, P], 196)
        lnp = sbuf("lnp", [2, 512], 198)
        lsq = sbuf("lsq", [512], 202)
        gbt = sbuf("gbt", [T], 204)
        spt = sbuf("spt", [4, P], 208)

        atT = [sbuf("at_hi", [4, T], 140, F32R), sbuf("at_lo", [4, T], 156, F32R)]
        gmT = [sbuf("gm_hi", [4, T], 172, F32R), sbuf("gm_lo", [4, T], 188, F32R)]
        yT = sbuf("yT", [KD, T], 108)
        sig = [[sbuf(f"sig{i}{k}", [T], 204 + 4 * (2 * i + k)) for k in range(2)] for i in range(2)]
        ob = sbuf("ob", [NT, D], 108)
        x2 = sbuf("x2", [NT, D], 140)
        fst = [sbuf(f"fst{i}", [T], 204 + 4 * i) for i in range(2)]
        fgb = sbuf("fgb", [D], 172)

        G = [ctx.enter_context(nc.psum_tensor(f"gemm{i}", [P, T], F32)) for i in range(2)]
        S = [ctx.enter_context(nc.psum_tensor(f"side{i}", [P, 512], F32)) for i in range(4)]

        con_loaded, rest_loaded, small_loaded = sem("con_loaded"), sem("rest_loaded"), sem("small_loaded")
        x_loaded = [sem(f"x_loaded{i}") for i in range(NT)]
        raw_loaded = [sem(f"raw_loaded{i}") for i in range(4)]
        w_split = sem("w_split")
        pool_hi = sem("pool_hi")
        gemm_done = [sem(f"gemm_done{i}") for i in range(2)]
        gemm_read = [sem(f"gemm_read{i}") for i in range(2)]
        side_done = [sem(f"side_done{i}") for i in range(4)]
        side_read = [sem(f"side_read{i}") for i in range(4)]
        act_step, dve_step = sem("act_step"), sem("dve_step")
        N = {k: sem(k) for k in (
            "init_done", "ss_ready", "diag_ready", "hi_ready", "conv_acc", "conv_act", "sm_abs", "sm_exp",
            "sm_arg", "beta_ready", "da_ready", "eacs_ready", "prep_done", "att_max", "att_exp", "rec_kb",
            "rec_x0", "rec_vn", "rec_S", "rec_mix", "resid_done", "f_hi", "f_lo", "rope_done", "gb_used",
            "mean_done", "ln_done", "a2_max", "split_hi", "split_lo", "y_done", "yT_hi", "yT_lo", "final_done",
            "ga_gated", "pt_used", "fold_ready", "tok_sq", "kx_ready", "ed_ready", "y_summed", "sq_mix",
            "nrs_ready", "pool_step", "sq_part", "rs_ready")}
        z_out = [sem(f"z_out{i}") for i in range(2)]
        z_in, res_loaded, x2_out, gain_loaded, rope_loaded, ln_loaded, x2_in, out_stored = (
            sem(x) for x in ("z_in", "res_loaded", "x2_out", "gain_loaded", "rope_loaded", "ln_loaded", "x2_in",
                             "out_stored"))

        first_after = unit_of["vi", 0]

        def wide(n):
            return n if n < first_after else n + NT * 8

        def scores_number(h):
            return first_after + h

        def gemm_product(eng, n):
            eng.wait_ge(gemm_done[n % 2], wide(n) // 2 + 1)

        def gemm_consumed(eng, n):
            eng.wait_ge(gemm_read[n % 2], wide(n) // 2 + 1)

        def scores_product(eng, h):
            w = scores_number(h)
            eng.wait_ge(gemm_done[w % 2], w // 2 + 1)
            return G[w % 2]

        def scores_consumed(eng, h):
            w = scores_number(h)
            eng.wait_ge(gemm_read[w % 2], w // 2 + 1)

        def side_product(eng, key):
            p = prod[key]
            eng.wait_ge(side_done[p % 4], p // 4 + 1)
            return S[p % 4]

        def side_consumed(eng, key):
            p = prod[key]
            eng.wait_ge(side_read[p % 4], p // 4 + 1)

        class Steps:

            def __init__(self, eng, own):
                self.eng, self.own, self.count = eng, own, {}

            def __call__(self, ins, name=None):
                s = N[name] if name else self.own
                self.count[name] = self.count.get(name, 0) + 1
                ins.then_inc(s, 1)
                self.eng.wait_ge(s, self.count[name])

            def frees(self, ins, key):
                p = prod[key]
                ins.then_inc(side_read[p % 4], 1)
                self.eng.wait_ge(side_read[p % 4], p // 4 + 1)

            def frees_gemm(self, ins, n):
                ins.then_inc(gemm_read[n % 2], 1)
                self.eng.wait_ge(gemm_read[n % 2], wide(n) // 2 + 1)

            def frees_scores(self, ins, h):
                w = scores_number(h)
                ins.then_inc(gemm_read[w % 2], 1)
                self.eng.wait_ge(gemm_read[w % 2], w // 2 + 1)

        block = ctx.enter_context(nc.Block())

        def hslice(c):
            return slice(c * P, (c + 1) * P)

        def widen(ap, n):
            return ap.unsqueeze(2).to_broadcast([P, ap.shape[1], n])

        def h64(x):
            return x.rearrange("p (h d) -> p h d", d=64)

        def over(ap, m):
            return ap.unsqueeze(1).to_broadcast([P, m, ap.shape[1]])

        def stage_of(kd):
            m = stage_uses[kd][0]
            bufs = {"conv": cacc, "sm": cacc, "z": cacc, "av": cacc, "wo": ost, "wo2": fst}.get(kd[0], st2)
            return m, bufs[m % 2]

        def stage_free(eng, m):
            r = stage_reader.get(m - 2)
            if r is not None and (r, 0) in prod:
                p = prod[r, 1 if (r, 1) in prod else 0]
                eng.wait_ge(side_done[p % 4], p // 4 + 1)

        tok_items = {"convT", "zT", "avT", "viT", "q2T"}

        def tok_dest(it, hf):
            kind, j = it
            t = slice(4 * hf, 4 * hf + 4)
            if kind == "convT":
                if j < 4:
                    return xs[:, t, hslice(j)]
                return Bt[:, t, hslice(j - 4)] if j < 6 else qkv[:, t, hslice(j - 8)]
            if kind == "zT":
                return zst[:, hf]
            if kind == "avT":
                return av[:, 1 + 4 * hf:5 + 4 * hf, :]
            return {"woT": mo, "viT": vv, "wo2T": ob}[kind][:, t, hslice(j)] if kind in ("woT", "viT", "wo2T") else \
                tok[:, t, :]

        norm_src = [xin, x1, x1]
        sq_scratch = [nsq, rsq, rsq]
        act_ready = {("conv", 0): lambda hf: ("norm", (0, hf)), ("wo", 0): lambda hf: ("mx", hf),
                     ("gate", 0): lambda hf: ("norm", (1, hf)), ("q2", 4): lambda hf: ("norm", (2, hf))}

        rec_weight = units[unit_of["av", 0]]["w"] + 7

        def bcast(ap, n):
            return bass.AP(ap.tensor, ap.offset, [[0, P], [1, n]])

        @block.sync
        def _(sp):
            def load_weights(w):
                name, kt, row, pieces = ws[w]
                if w >= 4:
                    sp.wait_ge(w_split, w - 3)
                src = a[name].rearrange("(k p) n -> p k n", p=P)
                dst = raw[w % 4][:].rearrange("p (k n) -> p k n", k=kt)
                o = 0
                for c0, width in pieces:
                    sp.dma_start(dst[:, :, o:o + width], src[:, row:row + kt, c0:c0 + width]).then_inc(raw_loaded[w % 4], 16)
                    o += width

            def load_x(tiles):
                for c in tiles:
                    sp.dma_start(xin[:, c, :], a["x"][hslice(c), :]).then_inc(x_loaded[c], 16)

            load_x(range(0, 2))
            sp.dma_start(con[:, 0:P], a["con1"][:, 0:P]).then_inc(con_loaded, 16)
            load_x(range(2, 4))
            for r0, src in ((0, a["ssd_conv_w"].rearrange("i (j p) -> (i j) p", p=P)),
                            (32, a["gdn_conv_w"].rearrange("i (j p) -> (i j) p", p=P)),
                            (56, a["ssd_conv_b"].rearrange("(j p) -> j p", p=P)),
                            (64, a["pre_mix_norm"].rearrange("(j p) -> j p", p=P)),
                            (72, a["pre_ffn_norm"].rearrange("(j p) -> j p", p=P)),
                            (80, a["norm_gain_2"].rearrange("(j p) -> j p", p=P)),
                            (88, a["b_merge_2"].rearrange("i (j p) -> (i j) p", p=P))):
                sp.dma_start(rows[r0:r0 + src.shape[0], :], src).then_inc(con_loaded, 16)
            load_weights(0)
            load_x(range(4, NT))
            load_weights(1)
            sp.dma_start(bias16[:, 0:8], bcast(a["ssd_dt_bias"], 8)).then_inc(small_loaded, 16)
            sp.dma_start(bias16[:, 12:16], bcast(a["gdn_dt_bias"], 4)).then_inc(small_loaded, 16)
            sp.dma_start(alog[:, 0:8], bcast(a["ssd_A_log"], 8)).then_inc(small_loaded, 16)
            sp.dma_start(alog[:, 8:12], bcast(a["gdn_A_log"], 4)).then_inc(small_loaded, 16)
            sp.dma_start(dskip[:], bcast(a["ssd_D"], 8)).then_inc(small_loaded, 16)
            s = a["attn_sinks"]
            for p in range(2):
                sp.dma_start(sinkb[:, 2 * p:2 * p + 2], bass.AP(s.tensor, s.offset + p, [[0, P], [2, 2]]), allow_slow_non_contiguous=True).then_inc(small_loaded, 16)
            sp.dma_start(con[:, P:], a["con1"][:, P:]).then_inc(rest_loaded, 16)
            for w in range(2, len(ws)):
                if w == rec_weight:
                    for c in range(1, NT):
                        sp.wait_ge(N["rec_mix"], c)
                        sp.dma_start(zt[:], z_dram[hslice(c), :]).then_inc(z_in, 16)
                load_weights(w)
            sp.wait_ge(out_stored, 16 * NT)

        @block.gpsimd
        def _(pool):
            step = Steps(pool, N["pool_step"])
            gp = nc.gpsimd
            pieces_so_far = [0] * 4

            def split(w):
                pieces_so_far[w % 4] += len(ws[w][3])
                pool.wait_ge(raw_loaded[w % 4], 16 * pieces_so_far[w % 4])
                if w >= 2:
                    gemm_product(pool, last_unit_of[w - 2])
                gp.tensor_scalar(whi[w % 2][:], raw[w % 4][:], 1.0, 0.0, ALU.mult, ALU.add).then_inc(pool_hi, 1)
                pool.wait_ge(pool_hi, w + 1)
                gp.tensor_tensor(wlo[w % 2][:], raw[w % 4][:], whi[w % 2][:], ALU.subtract).then_inc(w_split, 1)
                pool.wait_ge(w_split, w + 1)

            split(0)
            split(1)
            for it in sched:
                kind, j = it
                if kind == "unit" or kind == "half" and j[1]:
                    u = units[j if kind == "unit" else j[0]]
                    if u["last"] and u["w"] + 2 < len(ws):
                        split(u["w"] + 2)
                elif kind == "ra":
                    c, z = j, j % 2
                    if c == 0:
                        pool.wait_ge(N["init_done"], 1)
                        pool.wait_ge(N["eacs_ready"], 1)
                        for q in range(14):
                            if q not in (6, 7):
                                for h in range(2):
                                    side_consumed(pool, (("convT", q), h))
                        step(gp.tensor_tensor(bge[:], beta[:], eacs[:, :, 8:12], ALU.mult))
                    if c >= 2:
                        side_consumed(pool, (("st", c - 2), 0))
                    k_, v_, x_ = h64(qkv[:, c, 256:512]), h64(qkv[:, c, 512:768]), h64(xs[:, c, :])
                    kb4 = [h64(kbv[z][:, i, :]) for i in range(4)]
                    step(gp.tensor_tensor(kb4[0], k_, widen(beta[:, c, :], 64), ALU.mult), "rec_kb")
                    step(gp.tensor_tensor(kb4[1], v_, widen(beta[:, c, :], 64), ALU.mult))
                    step(gp.tensor_tensor(kb4[2], k_, widen(bge[:, c, :], 64), ALU.mult))
                    step(gp.tensor_tensor(h64(xc[z][:, 0]), x_, widen(dts[:, c, 0:8], 64), ALU.mult))
                    pool.wait_ge(N["ed_ready"], c + 1)
                    step(gp.tensor_tensor(kb4[3], k_, widen(ed[z][:, 8:12], 64), ALU.mult))
                    step(gp.tensor_tensor(h64(xc[z][:, 1]), h64(xc[z][:, 0]), widen(ed[z][:, 0:8], 64), ALU.mult), "kx_ready")
                elif kind == "st":
                    c = j
                    sq = msq[c % 2] if c < NT - 1 else msq7
                    side_product(pool, (("uw", c), 0))
                    if c == NT - 1:
                        side_product(pool, (("ap", c), 1))
                    step(gp.tensor_tensor(h64(sq[:, 0:512]), h64(xs[:, c, :]), widen(dskip[:], 64), ALU.mult))
                    pool.wait_ge(N["y_summed"], c + 1)
                    step(gp.tensor_tensor(mix[:, 0:512], mix[:, 0:512], sq[:, 0:512], ALU.add))
                    pool.wait_ge(z_in, 16 * (c + 1))
                    step(gp.tensor_tensor(mix[:, 0:512], mix[:, 0:512], zt[:, 0:512], ALU.mult))
                    step(gp.tensor_tensor(sq[:], mix[:], mix[:], ALU.mult), "sq_mix")
                elif kind == "rn":
                    c = j
                    pool.wait_ge(N["nrs_ready"], c + 1)
                    m2, m4 = mix[:, 0:512].rearrange("p (g n) -> p g n", g=2), h64(mix[:, 512:768])
                    step(gp.tensor_tensor(m2, m2, widen(nrs[:, 0:2], 256), ALU.mult))
                    step(gp.tensor_tensor(m4, m4, widen(nrs[:, 2:6], 64), ALU.mult))
                    step(gp.tensor_tensor(mix[:, 512:768], mix[:, 512:768], zt[:, 512:768], ALU.mult))
                    pool.wait_ge(gain_loaded, 32)
                    step(gp.tensor_tensor(xs[:, c, :], mix[:, 0:512], gmix[:, 0:512], ALU.mult))
                    step(gp.tensor_tensor(qkv[:, c, 0:256], mix[:, 512:768], gmix[:, 512:768], ALU.mult), "rec_mix")

        @block.tensor
        def _(pe):
            mm, tr = nc.tensor.matmul, nc.tensor.transpose

            def bank(key):
                p = prod[key]
                if p >= 4:
                    pe.wait_ge(side_read[p % 4], p // 4)
                return S[p % 4]

            def done(last, key):
                last.then_inc(side_done[prod[key] % 4], 1)

            def unit(n, halves=(0, 1)):
                u = units[n]
                kd, kt, w = u["kind"], u["kt"], u["w"]
                if 0 in halves:
                    pe.wait_ge(w_split, w + 1)
                    if n >= 2:
                        pe.wait_ge(gemm_read[n % 2], wide(n) // 2)
                act = {"down": fT, "ya": atT, "yb": gmT}.get(kd[0], hT)
                if kd[0] == "down":
                    pe.wait_ge(N["f_lo"], min(4 * kd[1][0] + 4, NF))
                if kd[0] in ("ya", "yb"):
                    pe.wait_ge(N["split_lo"], 4 if kd[0] == "ya" else 8)
                hi = whi[w % 2][:].rearrange("p (k n) -> p k n", k=kt)
                lo = wlo[w % 2][:].rearrange("p (k n) -> p k n", k=kt)
                m = slice(u["sub"] * P, u["sub"] * P + P)
                for hf in halves:
                    t = slice(hf * 512, hf * 512 + 512)
                    o = G[n % 2][:, t]
                    for k in range(kt):
                        if kd in act_ready:
                            side_consumed(pe, (act_ready[kd](hf), k))
                        if kd == ("wo2", 0) and hf == 0:
                            pe.wait_ge(N["yT_lo"], k + 1)
                        mm(o, hi[:, k, m], act[0][:, k, t], start=k == 0, stop=False)
                        mm(o, hi[:, k, m], act[1][:, k, t], start=False, stop=False)
                        last = mm(o, lo[:, k, m], act[0][:, k, t], start=False, stop=k == kt - 1)
                if 1 in halves:
                    last.then_inc(gemm_done[n % 2], 1)

            def transposed(it, blocks):
                for h in range(2):
                    b = bank((it, h))
                    for i, x in enumerate(blocks(h)):
                        last = tr(b[:, hslice(i)], x, ident)
                    done(last, (it, h))

            for it in sched:
                kind, j = it
                if kind == "unit":
                    unit(j)
                elif kind == "half":
                    unit(j[0], (j[1],))
                elif kind == "cols":
                    pe.wait_ge(con_loaded, 16 * 8)
                    b = bank((it, 0))
                    done(tr(b[:, 0:104], rows[0:104, :], ident[0:104, 0:104]), (it, 0))
                elif kind == "norm":
                    stage, hf = j
                    pe.wait_ge(N["diag_ready"], 2 * stage + hf + 1)
                    for k in range(KD):
                        b = bank((it, k))
                        for i in range(4):
                            c = 4 * hf + i
                            last = mm(b[:, hslice(i)], norm_src[stage][:, c, hslice(k)], diag[:, c, :], start=True, stop=True)
                        done(last, (it, k))
                elif kind == "mx":
                    pe.wait_ge(N["rec_mix"], 4 * j + 4)
                    side_consumed(pe, (("ao", 4 * j + 3), 0))
                    for k in range(KD):
                        b = bank((it, k))
                        for i in range(4):
                            c = 4 * j + i
                            src = atts[:, c, hslice(k)] if k < 2 else xs[:, c, hslice(k - 2)] if k < 6 else qkv[:, c, hslice(k - 6)]
                            last = tr(b[:, hslice(i)], src, ident)
                        done(last, (it, k))
                elif kind == "smT":
                    gemm_consumed(pe, unit_of["sm", 0])
                    b = bank((it, 0))
                    src = stage_of(("sm", 0))[1]
                    for c in range(NT):
                        last = tr(b[:, 16 * c:16 * c + 16], src[0:16, hslice(c)], ident[0:16, 0:16])
                    done(last, (it, 0))
                elif kind == "acs":
                    pe.wait_ge(N["da_ready"], 1)
                    pe.wait_ge(rest_loaded, 16)
                    b = bank((it, 0))
                    done(mm(b[:, 0:96], upper, da[:].rearrange("p c h -> p (c h)"), start=True, stop=True), (it, 0))
                elif kind in ("convT", "zT", "avT", "v2T", "viT", "woT", "wo2T", "q2T"):
                    kd = {"convT": "conv", "zT": "z", "avT": "av", "v2T": "v2", "viT": "vi", "woT": "wo",
                          "wo2T": "wo2", "q2T": "q2"}[kind], j
                    src = stage_of(kd)[1]
                    if kind == "convT":
                        pe.wait_ge(N["conv_act"], j + 1)
                        if j in (4, 5):
                            src = BC[:, j - 4, :]
                    else:
                        gemm_consumed(pe, unit_of[kd])
                    transposed(it, lambda h, src=src: [src[:, (4 * h + i) * P:(4 * h + i + 1) * P] for i in range(4)])
                elif kind == "as":
                    if j == 0:
                        for kd in (("aq", 0), ("aq", 1), ("ak", 0)):
                            gemm_consumed(pe, unit_of[kd])
                    for p in range(2):
                        b = bank((it, p))
                        for kv in range(2):
                            last = mm(b[:, kv * 256:kv * 256 + 256], aqT[:, p, hslice(j)], akT[:, kv, j * P:j * P + 2 * P],
                                      start=True, stop=True)
                        done(last, (it, p))
                elif kind == "ap":
                    pe.wait_ge(N["att_exp"], j + 1)
                    for p in range(2):
                        b = bank((it, p))
                        for i in range(4):
                            last = tr(b[:, hslice(i)], asb[:, 2 * p + i // 2, hslice(i % 2)], ident)
                        done(last, (it, p))
                elif kind == "ao":
                    if j == 0:
                        side_consumed(pe, (("avT", 0), 0))
                        side_consumed(pe, (("avT", 0), 1))
                    side_consumed(pe, (("ap", j), 0))
                    side_consumed(pe, (("ap", j), 1))
                    b = bank((it, 0))
                    for i in range(4):
                        p, kv = i // 2, i % 2
                        h = p + 2 * kv
                        for s in range(2):
                            last = mm(b[:, h * 64:h * 64 + 64], apT[:, i, s, :], av[:, j + s, kv * 64:kv * 64 + 64],
                                      start=s == 0, stop=s == 1)
                    done(last, (it, 0))
                elif kind in ("ra", "rk", "rj", "rx"):
                    c, z = j, j % 2
                    for key in products_of(it):
                        b = bank((it, key))
                        if key[:2] == "bc":
                            i = int(key[2])
                            if c == 0 and i == 0:
                                pe.wait_ge(N["da_ready"], 1)
                                pe.wait_ge(N["init_done"], 1)
                            mm(b[:].rearrange("p (h n) -> p h n", h=4), identb[:], over(negb[:], 4), start=True, stop=False)
                            for h in range(4):
                                last = mm(b[:, hslice(h)], da[:, c, 4 * i + h:4 * i + h + 1].to_broadcast([P, P]), upper,
                                          start=False, stop=h == 3)
                        elif key == "kT":
                            pe.wait_ge(N["rec_kb"], c + 1)
                            for p in range(2):
                                tr(b[:, hslice(p)], qkv[:, c, 256 + p * P:256 + (p + 1) * P], ident)
                            for p in range(2):
                                last = tr(b[:, hslice(2 + p)], kbv[z][:, 0, hslice(p)], ident)
                        elif key == "qT":
                            for p in range(2):
                                last = tr(b[:, hslice(p)], qkv[:, c, hslice(p)], ident)
                        elif key == "g":
                            for g in range(2):
                                last = mm(b[:, hslice(g)], BC[:, g, hslice(c)], BC[:, 2 + g, hslice(c)], start=True, stop=True)
                        elif key[:2] == "kq":
                            p = int(key[2])
                            if p == 0:
                                side_consumed(pe, (("rk", c), "kT"))
                                side_consumed(pe, (("rk", c), "qT"))
                            for h in range(2):
                                last = mm(b[:, h * 256:h * 256 + 256], kTp[z][:, 2 * p + h, :],
                                          kq[z][:, p, :, :].rearrange("p a n -> p (a n)"), start=True, stop=True)
                        elif key == "xT":
                            pe.wait_ge(N["rec_x0"], c + 1)
                            for h in range(4):
                                last = tr(b[:, hslice(h)], XT[z][:, h, :], ident)
                        done(last, (it, key))
                elif kind == "ly":
                    c, lv = j
                    z = c % 2
                    side_consumed(pe, (("rx", c), "xT") if lv == 1 else (("lx", (c, lv - 1)), "x"))
                    b = bank((it, 0))
                    for h in range(4):
                        last = mm(b[:, hslice(h)], SQ[z][:, h, 0, :], X[z][:, h, :], start=True, stop=True)
                    done(last, (it, 0))
                elif kind == "lx":
                    c, lv = j
                    z = c % 2
                    side_consumed(pe, (("ly", j), 0))
                    if lv > 1:
                        side_consumed(pe, (("lx", (c, lv - 1)), "t"))
                    for key in products_of(it):
                        b = bank((it, key))
                        for h in range(4):
                            l, r = (XT, Y) if key == "x" else (Y, XT)
                            last = mm(b[:, hslice(h)], l[z][:, h, :], r[z][:, h, :], start=True, stop=True)
                        done(last, (it, key))
                elif kind in ("uw", "yo", "yd", "st", "r1", "r2"):
                    c, z = j, j % 2
                    b = bank((it, 0))
                    if kind == "yo":
                        if c > 0:
                            side_consumed(pe, (("st", c - 1), 0))
                        for g in range(2):
                            last = mm(b[:, g * 256:g * 256 + 256], BC[:, 2 + g, hslice(c)], Sst[:, g * 256:g * 256 + 256],
                                      start=True, stop=True)
                    elif kind == "yd":
                        for h in range(8):
                            last = mm(b[:, h * 64:h * 64 + 64], E[z][:, h, :], xc[z][:, 0, h * 64:h * 64 + 64], start=True, stop=True)
                    elif kind == "st":
                        for g in range(2):
                            last = mm(b[:, g * 256:g * 256 + 256], Bt[:, c, hslice(g)], xc[z][:, 1, g * 256:g * 256 + 256],
                                      start=True, stop=True)
                    elif kind == "uw":
                        side_consumed(pe, (("lx", (c, 6)), "t"))
                        pe.wait_ge(N["kx_ready"], c + 1)
                        for h in range(4):
                            mm(b[:, h * 64:h * 64 + 64], XT[z][:, h, :], kbv[z][:, 1, h * 64:h * 64 + 64], start=True, stop=True)
                        for h in range(4):
                            r = 64 * (h % 2)
                            last = mm(b[r:r + 64, 256 + (h // 2) * P:256 + (h // 2) * P + P], kbv[z][:, 2, h * 64:h * 64 + 64],
                                      XT[z][:, h, :], start=True, stop=True)
                    elif kind == "r1":
                        side_consumed(pe, (("uw", c), 0))
                        if c > 0:
                            pe.wait_ge(N["rec_S"], c)
                        for p in range(2):
                            mm(b[:, hslice(p)], uw[z][:, 256 + p * P:256 + (p + 1) * P], Sbd[:, p, :], start=True, stop=True)
                        for p in range(2):
                            last = mm(b[:, hslice(2 + p)], kq[z][:, p, 1, :], Sbd[:, p, :], start=True, stop=True)
                    elif kind == "r2":
                        pe.wait_ge(N["rec_vn"], c + 1)
                        for h in range(4):
                            mm(b[:, h * 64:h * 64 + 64], SQ[z][:, h, 1, :], vn[:, h * 64:h * 64 + 64], start=True, stop=True)
                        for p in range(2):
                            last = mm(b[:, hslice(2 + p)], kbv[z][:, 3, hslice(p)], vn[:, hslice(p)], start=True, stop=True)
                    done(last, (it, 0))
                elif kind == "downT":
                    gemm_consumed(pe, unit_of["down", (len(ffn_groups()) - 1, j)])
                    transposed(it, lambda h: [accT[:, j, hslice(4 * h + i)] for i in range(4)])
                elif kind == "q2B":
                    pe.wait_ge(N["rope_done"], (j + 1) % 5 + 1)
                    for n in range(4):
                        b = bank((it, n))
                        for i in range(4):
                            last = tr(b[:, hslice(i)], rpd[:, 4 * (n % 2) + i, n // 2].rearrange("p a d -> p (a d)"), ident)
                        done(last, (it, n))
                elif kind == "ln":
                    pe.wait_ge(ln_loaded, 16 * 5)
                    transposed(it, lambda h: [wsr[:, 4 * h + i, :] for i in range(4)])
                elif kind == "a2s":
                    c, h = j // 8, j % 8
                    w = scores_number(j)
                    if j == 0:
                        for s in range(4):
                            side_consumed(pe, (("q2B", 4), s))
                            side_consumed(pe, (("q2B", 3), s))
                    pe.wait_ge(gemm_read[w % 2], w // 2)
                    for s in range(2):
                        t = slice(s * 512, s * 512 + 512)
                        for part in range(2):
                            last = mm(G[w % 2][:, t], qp[:, h, hslice(c)], kp[:, h // 4, part, t], start=part == 0, stop=part == 1)
                    last.then_inc(gemm_done[w % 2], 1)
                elif kind == "a2x":
                    m, q = j
                    if q == 0:
                        scores_consumed(pe, 2 * m)
                        scores_consumed(pe, 2 * m + 1)
                    b = bank((it, 0))
                    for i in range(4):
                        last = tr(b[:, hslice(i)], Pb[(2 * m + i % 2) % 4][:, hslice(2 * q + i // 2)], ident)
                    done(last, (it, 0))
                elif kind == "a2v":
                    m, q = j
                    if j == (0, 0):
                        for s in range(2):
                            side_consumed(pe, (("v2T", 0), s))
                    key = ("a2v", (m, 0)), 0
                    b = bank(key) if q == 0 else S[prod[key] % 4]
                    side_consumed(pe, (("a2x", j), 0))
                    for i in range(2):
                        for part in range(2):
                            last = mm(b[:, 0:256], vp[:, 2 * q + i, m % 4 // 2, :], PT[q][part][:, 256 * i:256 * i + 256],
                                      start=q == 0 and i == 0 and part == 0, stop=q == 3 and i == 1 and part == 1)
                    if q < 3:
                        last.then_inc(N["pt_used"], 1)
                    else:
                        done(last, key)
                elif kind == "a2o":
                    side_consumed(pe, (("a2v", (j, 0)), 0))
                    if j == 0:
                        pe.wait_ge(N["fold_ready"], 1)
                    b = bank((it, 0))
                    for i in range(2):
                        last = mm(b[:, hslice(i)], ovt[j % 2][:, hslice(i)], fold[:], start=True, stop=True)
                    done(last, (it, 0))
                elif kind == "a2t":
                    side_consumed(pe, (("a2o", 4 * j + 3), 0))
                    b = bank((it, 0))
                    for i in range(4):
                        last = tr(b[:, hslice(i)], ot[:, hslice(i)], ident)
                    done(last, (it, 0))
                elif kind == "sp":
                    if j == 0:
                        pe.wait_ge(N["ln_done"], 1)
                        side_consumed(pe, (("ln", 0), 0))
                        side_consumed(pe, (("ln", 0), 1))
                    b = bank((it, 0))
                    for g in range(8):
                        r = 64 * (g % 2)
                        last = mm(b[r:r + 64, hslice(g // 2)], vv[:, j, g * 64:g * 64 + 64], wsT[:, g, :], start=True, stop=True)
                    done(last, (it, 0))

        @block.scalar
        def _(act):
            step = Steps(act, act_step)
            af = nc.scalar.activation

            def tokens_copied(it, hf):
                b = side_product(act, (it, hf))
                if it[0] == "zT" and it[1] > 0:
                    act.wait_ge(z_out[hf], 16 * it[1])
                step.frees(af(tok_dest(it, hf), b[:].rearrange("p (c n) -> p c n", c=4), ACT.Copy), (it, hf))

            def z_store(it, hf):
                j = it[1]
                dst = z_dram[hf * 512:hf * 512 + 512, hslice(j)].rearrange("(c p) n -> p c n", p=P)
                act.dma_start(dst, zst[:, hf]).then_inc(z_out[hf], 16)

            def squares_of_blocks(it, blocks, by_half):
                for h in range(2):
                    by_half(h)
                    for i in range(4):
                        step(af(sqp[:], blocks(h, i), ACT.Square, accum_out=ssp[:, 4 * h + i, it[1]:it[1] + 1]), "sq_part")

            def squares(src, scratch, tiles, ready=lambda c: None):
                for c in tiles:
                    ready(c)
                    ins = af(scratch, src[:, c, :], ACT.Square, accum_out=ss[:, c:c + 1])
                    step(ins, "ss_ready" if c == tiles[-1] else None)

            def unit(n):
                kd = units[n]["kind"]
                kind, j = kd
                g = G[n % 2]
                if kind == "conv":
                    m, buf = stage_of(kd)
                    if j > 0:
                        act.wait_ge(N["conv_acc"], j)
                    gemm_product(act, n)
                    stage_free(act, m)
                    bcol, wcol = (56 + j, 24 + j) if j < 8 else (104, 50 + j - 8)
                    step(af(cin[:, 3:3 + T], g[:], ACT.Copy))
                    step.frees_gemm(af(buf[:], g[:], ACT.Identity, bias=cols[:, bcol:bcol + 1], scale=cols[:, wcol:wcol + 1]), n)
                    act.wait_ge(N["conv_acc"], j + 1)
                    step(af(BC[:, j - 4, :] if 4 <= j < 8 else buf[:], buf[:], ACT.Silu), "conv_act")
                elif kind == "sm":
                    m, buf = stage_of(kd)
                    gemm_product(act, n)
                    stage_free(act, m)
                    step.frees_gemm(af(buf[0:16, :], g[0:16, :], ACT.Copy), n)
                elif kind in ("z", "av", "wo", "q2", "v2", "vi", "wo2"):
                    m, buf = stage_of(kd)
                    gemm_product(act, n)
                    stage_free(act, m)
                    f = {"z": ACT.Silu, "vi": ACT.Gelu_apprx_tanh}.get(kind, ACT.Copy)
                    step.frees_gemm(af(buf[:], g[:], f), n)
                elif kind == "aq":
                    gemm_product(act, n)
                    step.frees_gemm(af(aqT[:, j, :], g[:], ACT.Copy), n)
                elif kind == "ak":
                    gemm_product(act, n)
                    step(af(akT[0:64, 0, P:], g[0:64, :], ACT.Copy))
                    step.frees_gemm(af(akT[64:P, 1, P:], g[64:P, :], ACT.Copy), n)
                elif kind == "gate":
                    gemm_product(act, n)
                    if j >= 2:
                        gemm_consumed(act, unit_of["up", j - 2])
                    step.frees_gemm(af(sg[j % 2][:], g[:], ACT.Silu), n)
                elif kind == "up":
                    gemm_consumed(act, n)
                    step(af(fT[0][:, j % 4, :], ft[:], ACT.Copy), "f_hi")
                elif kind == "down" and j[0] == 0:
                    gemm_product(act, n)
                    step.frees_gemm(af(accT[:, j[1], :], g[:], ACT.Copy), n)
                elif kind in ("ga", "u2"):
                    gemm_product(act, n)
                    dst = uT[:, j, :] if kind == "u2" else gaT[:, j - 1, :] if j else gaT0[:]
                    step.frees_gemm(af(dst, g[:], ACT.Silu if kind == "ga" else ACT.Gelu_apprx_tanh), n)
                elif kind == "gb":
                    gemm_product(act, n)
                    if j > 0:
                        act.wait_ge(N["gb_used"], j)
                    step.frees_gemm(af(gbt[:], g[:], ACT.Silu), n)
                elif kind in ("sga", "sgb"):
                    gemm_product(act, n)
                    i = 0 if kind == "sga" else 1
                    if j >= 2:
                        act.wait_ge(N["y_done"], j - 1)
                    step.frees_gemm(af(sig[i][j % 2][:], g[:], ACT.Sigmoid, bias=cols[:, 88 + 8 * i + j:89 + 8 * i + j]), n)

            for it in sched:
                kind, j = it
                if kind == "unit":
                    unit(j)
                elif kind == "half":
                    if j[1]:
                        unit(j[0])
                elif kind == "norm":
                    stage, hf = j
                    squares(norm_src[stage], sq_scratch[stage][:], range(4 * hf, 4 * hf + 4),
                            lambda c: act.wait_ge(N["resid_done"], 8 * stage - 7 + c) if stage else act.wait_ge(x_loaded[c], 16))
                    if it == ("norm", (0, 0)):
                        side_consumed(act, (("cols", 0), 0))
                    for k in range(KD):
                        b = side_product(act, (it, k))
                        g0 = 64 + 8 * stage + k
                        step(af(hT[0][:, k, hf * 512:hf * 512 + 512], b[:], ACT.Identity, scale=cols[:, g0:g0 + 1]), "hi_ready")
                elif kind == "mx":
                    for k in range(KD):
                        b = side_product(act, (it, k))
                        step(af(hT[0][:, k, j * 512:j * 512 + 512], b[:], ACT.Copy), "hi_ready")
                elif kind == "smT":
                    act.wait_ge(small_loaded, 16 * 7)
                    step(af(easm[:], alog[:], ACT.Exp))
                    act.wait_ge(N["sm_abs"], 1)
                    step(af(sm[2][:], sm[1][:], ACT.Exp, scale=-1.0), "sm_exp")
                elif kind == "acs":
                    act.wait_ge(N["sm_arg"], 1)
                    step(af(beta[:], sm[3][:, :, 8:12], ACT.Exp), "beta_ready")
                    side_consumed(act, (it, 0))
                    step(af(eacs[:], nacs[:], ACT.Exp, scale=-1.0), "eacs_ready")
                elif kind in ("woT", "downT"):
                    squares_of_blocks(it, lambda h, i: S[prod[it, h] % 4][:, hslice(i)], lambda h: side_product(act, (it, h)))
                elif kind == "wo2T":
                    squares_of_blocks(it, lambda h, i: ob[:, 4 * h + i, hslice(it[1])], lambda h: side_consumed(act, (it, h)))
                elif kind in tok_items:
                    if kind == "q2T" and j < 4:
                        act.wait_ge(N["rope_done"], j + 1)
                    tokens_copied(it, 0)
                    if kind == "q2T":
                        side_consumed(act, (it, 1))
                        step(af(rp2[:], tok[:], ACT.Square), "tok_sq")
                    if kind == "zT":
                        z_store(it, 0)
                        side_consumed(act, (it, 1))
                        z_store(it, 1)
                elif kind == "as":
                    act.wait_ge(N["att_max"], j + 1)
                    for i in range(4):
                        step(af(asb[:, i, :], asb[:, i, :], ACT.Exp, bias=anm[:, i:i + 1], accum_out=asum[:, i:i + 1]))
                    step(af(ads[:], ads[:], ACT.Exp), "att_exp")
                elif kind == "ap":
                    b = side_product(act, (it, 0))
                    if j > 0:
                        side_product(act, (("ao", j - 1), 0))
                    step.frees(af(apT[:, 0:2], b[:].rearrange("p (i s n) -> p i s n", i=2, s=2), ACT.Copy), (it, 0))
                elif kind == "ra":
                    c, z = j, j % 2
                    if c == 0:
                        act.wait_ge(z_out[0], 16 * 6)
                        act.wait_ge(z_out[1], 16 * 6)
                        act.wait_ge(N["init_done"], 1)
                        src = a["ssd_norm_w"]
                        act.dma_start(gmix[:, 0:512], bass.AP(src.tensor, src.offset, [[0, P], [1, 512]])).then_inc(gain_loaded, 16)
                        src = a["gdn_norm_w"]
                        act.dma_start(gmix[:, 512:768].rearrange("p (h d) -> p h d", h=4),
                                      bass.AP(src.tensor, src.offset, [[0, P], [0, 4], [1, 64]])).then_inc(gain_loaded, 16)
                        act.dma_start(zt[:], z_dram[0:P, :]).then_inc(z_in, 16)
                    if c >= 2:
                        side_consumed(act, (("st", c - 2), 0))
                    for i in range(3):
                        b = side_product(act, (it, f"bc{i}"))
                        for h in range(4):
                            step(af(E[z][:, 4 * i + h, :], b[:, hslice(h)], ACT.Exp, bias=nacs[:, c, 4 * i + h:4 * i + h + 1]))
                        step.frees(af(cd[z][:, 4 * i:4 * i + 4], b[:].rearrange("p (h n) -> p h n", h=4)[:, :, P - 1], ACT.Exp), (it, f"bc{i}"))
                    if c >= 2:
                        act.wait_ge(N["kx_ready"], c - 1)
                    step(af(ed[z][:], E[z][:, :, P - 1], ACT.Copy), "ed_ready")
                elif kind == "rk":
                    z = j % 2
                    b = side_product(act, (it, "kT"))
                    v = b[:].rearrange("p (i n) -> p i n", i=4)
                    kv = kTp[z][:].rearrange("p (a b) n -> p a b n", b=2)
                    step(af(kv[0:64, :, 0, :], v[0:64, 0:2, :], ACT.Copy))
                    step(af(kv[64:P, :, 1, :], v[64:P, 0:2, :], ACT.Copy))
                    step.frees(af(kq[z][:, :, 0, :], v[:, 2:4, :], ACT.Copy), (it, "kT"))
                elif kind == "rx":
                    z = j % 2
                    if j >= 2:
                        act.wait_ge(N["rec_mix"], j - 1)
                    b = side_product(act, (it, "xT"))
                    step.frees(af(X[z][:], b[:].rearrange("p (i n) -> p i n", i=4), ACT.Copy), (it, "xT"))
                elif kind == "uw":
                    b = side_product(act, (it, 0))
                    step.frees(af(uw[j % 2][:], b[:], ACT.Copy), (it, 0))
                elif kind == "load":
                    if j == 0:
                        for k in range(4, 8):
                            side_consumed(act, (("mx", 1), k))
                        src = a["post_mix_norm"]
                        act.dma_start(gbc[:], bass.AP(src.tensor, src.offset, [[0, P], [1, D]])).then_inc(gain_loaded, 16)
                        act.dma_start(x1[:], a["x"].rearrange("(c p) n -> p c n", p=P)).then_inc(res_loaded, 16)
                    elif j == 5:
                        for k in range(4, 8):
                            side_consumed(act, (("norm", (1, 1)), k))
                        src = a["post_ffn_norm"]
                        act.dma_start(gbc2[:], bass.AP(src.tensor, src.offset, [[0, P], [1, D]])).then_inc(gain_loaded, 16)
                    elif j in (1, 2):
                        t = slice(4 * j - 4, 4 * j)
                        act.wait_ge(N["resid_done"], 8 + 4 * j)
                        act.dma_start(x2_dram.rearrange("(c p) n -> p c n", p=P)[:, t], x1[:, t]).then_inc(x2_out, 16)
                        if j == 2:
                            continue
                        act.dma_start(rope[:].rearrange("p a c n -> p (a c n)"), a["con2"]).then_inc(rope_loaded, 16)
                        for i, name in enumerate(("q_gain_2", "k_gain_2")):
                            src = a[name]
                            act.dma_start(qkg[:, i, :], bass.AP(src.tensor, src.offset, [[0, P], [1, 64]])).then_inc(rope_loaded, 16)
                    elif j == 3:
                        side_consumed(act, (("a2t", NT - 1), 0))
                        side_product(act, (("a2v", (NT * 4 - 1, 0)), 0))
                        act.dma_start(wsr[:], a["w_spatial_2"].rearrange("g i j -> i g j")).then_inc(ln_loaded, 16)
                        src = a["b_spatial_2"]
                        for h in range(2):
                            act.dma_start(bsp[64 * h:64 * h + 64], bass.AP(src.tensor, src.offset + h * P, [[0, 64], [2 * P, 4], [1, P]])).then_inc(ln_loaded, 16)
                        for i, name in enumerate(("ln_v_gain_2", "ln_v_bias_2")):
                            src = a[name]
                            act.dma_start(lnp[:, i, :], bass.AP(src.tensor, src.offset, [[0, P], [1, 512]])).then_inc(ln_loaded, 16)
                    elif j == 4:
                        gemm_consumed(act, unit_of["yb", 7])
                        gemm_consumed(act, unit_of["yb", 6])
                        act.dma_start(x2[:], x2_dram.rearrange("(c p) n -> p c n", p=P)).then_inc(x2_in, 16)
                        src = a["final_gain_2"]
                        act.dma_start(fgb[:], bass.AP(src.tensor, src.offset, [[0, P], [1, D]])).then_inc(x2_in, 16)
                elif kind == "q2B":
                    if j == 4:
                        act.wait_ge(x2_out, 32)
                    for n in range(4):
                        t = slice(n % 2 * 512, n % 2 * 512 + 512)
                        b = side_product(act, (it, n))
                        dst = qp[:, 2 * j + n // 2, t] if j < 4 else kp[:, n // 2, 0, t]
                        step(af(dst, b[:], ACT.Copy), "hi_ready")
                elif kind == "v2T":
                    for h in range(2):
                        b = side_product(act, (it, h))
                        dst = vp[:, 4 * h:4 * h + 4].rearrange("p c k (s d) -> p c k s d", s=2)[:, :, :, 0, :]
                        step(af(dst, b[:].rearrange("p (c k d) -> p c k d", c=4, k=2), ACT.Copy), "hi_ready")
                elif kind == "ln":
                    b = side_product(act, (it, 0))
                    step.frees(af(wsT[:, 0:4], b[:].rearrange("p (i n) -> p i n", i=4), ACT.Copy), (it, 0))
                    act.wait_ge(N["mean_done"], 1)
                    squares(vv, lsq[:], range(NT))
                elif kind == "a2e":
                    act.wait_ge(N["a2_max"], j + 1)
                    if j >= 4:
                        side_product(act, (("a2x", (j // 2 - 2, 3)), 0))
                    g = scores_product(act, j)
                    step.frees_scores(af(Pb[j % 4][:], g[:], ACT.Exp, bias=a2m[:, 2 + j % 2:3 + j % 2], scale=0.125,
                                         accum_out=a2d[:, j % 8:j % 8 + 1]), j)
                elif kind == "a2x":
                    m, q = j
                    if m > 0 and q < 3:
                        act.wait_ge(N["pt_used"], 3 * (m - 1) + q + 1)
                    elif m > 0:
                        side_product(act, (("a2v", (m - 1, 0)), 0))
                    b = side_product(act, (it, 0))
                    step(af(PT[q][0][:], b[:], ACT.Copy), "hi_ready")
                elif kind == "a2v" and j[1] == 3:
                    key = ("a2v", (j[0], 0)), 0
                    if j[0] >= 2:
                        side_product(act, (("a2o", j[0] - 2), 0))
                    b = side_product(act, key)
                    step.frees(af(ovt[j[0] % 2][:], b[:, 0:256], ACT.Copy), key)
                elif kind in ("split4", "splity"):
                    for k in range(8):
                        if kind == "split4":
                            if k == 0:
                                act.wait_ge(N["ga_gated"], 4)
                                act.wait_ge(N["gb_used"], 4)
                            step(af((atT if k < 4 else gmT)[0][:, k % 4, :], (aoT if k < 4 else uT)[:, k % 4, :], ACT.Copy), "split_hi")
                        else:
                            if k == 0:
                                act.wait_ge(N["y_done"], 8)
                            step(af(hT[0][:, k, :], yT[:, k, :], ACT.Copy), "yT_hi")
                elif kind == "final":
                    act.wait_ge(N["rs_ready"], 1)
                    for c in range(NT):
                        if c % 2 == 0:
                            step(af(ob[:, c, :], ob[:, c, :], ACT.Identity, scale=rs[:, c:c + 1]))
                        else:
                            act.wait_ge(N["final_done"], c // 2 + 1)
                        act.dma_start(out[hslice(c), :], ob[:, c, :]).then_inc(out_stored, 16)

        @block.vector
        def _(dve):
            step = Steps(dve, dve_step)
            v = nc.vector
            hi_count = [0]
            ss_count = [0]

            def sums_ready():
                ss_count[0] += 1
                dve.wait_ge(N["ss_ready"], ss_count[0])


            def rsqrt(dst, src, scale, name=None):
                x, t = nv[:, 0:src.shape[1]], nt_[:, 0:src.shape[1]]
                step(v.tensor_scalar(x, src, scale, EPS, ALU.mult, ALU.add))
                step(v.tensor_scalar(dst.bitcast(I32), x.bitcast(I32), -0.5, float(0x5F3759DF), ALU.mult, ALU.add))
                step(v.tensor_scalar(x, x, -0.5, None, ALU.mult))
                for i in range(3):
                    step(v.tensor_tensor(t, x, dst, ALU.mult))
                    step(v.tensor_tensor(t, t, dst, ALU.mult))
                    step(v.scalar_tensor_tensor(out=dst, in0=t, scalar=1.5, in1=dst, op0=ALU.add, op1=ALU.mult),
                         name if i == 2 else None)

            def low(dst, b, hi, key=None, gain=None):
                hi_count[0] += 1
                dve.wait_ge(N["hi_ready"], hi_count[0])
                if gain is None:
                    ins = v.tensor_tensor(dst, b, hi, ALU.subtract)
                else:
                    ins = v.scalar_tensor_tensor(out=dst, in0=b, scalar=gain, in1=hi, op0=ALU.mult, op1=ALU.subtract)
                step.frees(ins, key)

            def final_gain(j):
                dve.wait_ge(N["sq_part"], 128 + 8 * j + 8)
                step(v.tensor_tensor(ob[:, :, hslice(j)], ob[:, :, hslice(j)], over(fgb[:, hslice(j)], NT), ALU.mult))

            def four(b):
                return b[:].rearrange("p (h n) -> p h n", h=4)

            def unit(n):
                kd = units[n]["kind"]
                kind, j = kd
                g = G[n % 2]
                if kind == "conv":
                    m, buf = stage_of(kd)
                    gemm_consumed(dve, n)
                    for i in range(3):
                        wcol = i * 8 + j if j < 8 else 32 + i * 6 + j - 8
                        step(v.scalar_tensor_tensor(out=buf[:], in0=cin[:, i:i + T], scalar=cols[:, wcol:wcol + 1], in1=buf[:],
                                                    op0=ALU.mult, op1=ALU.add), "conv_acc" if i == 2 else None)
                elif kind == "up":
                    gemm_consumed(dve, unit_of["gate", j])
                    gemm_product(dve, n)
                    step.frees_gemm(v.tensor_tensor(ft[:], sg[j % 2][:], g[:], ALU.mult), n)
                    dve.wait_ge(N["f_hi"], j + 1)
                    step(v.tensor_tensor(fT[1][:, j % 4, :], ft[:], fT[0][:, j % 4, :], ALU.subtract), "f_lo")
                elif kind == "down" and j[0] > 0:
                    gemm_consumed(dve, unit_of["down", (j[0] - 1, j[1])])
                    gemm_product(dve, n)
                    step.frees_gemm(v.tensor_tensor(accT[:, j[1], :], accT[:, j[1], :], g[:], ALU.add), n)
                elif kind == "ga" and j > 0:
                    if j == 1:
                        gemm_consumed(dve, unit_of["ga", 0])
                        step(v.tensor_tensor(aoT[:, 0, :], aoT[:, 0, :], gaT0[:], ALU.mult), "ga_gated")
                    gemm_consumed(dve, n)
                    step(v.tensor_tensor(aoT[:, j, :], aoT[:, j, :], gaT[:, j - 1, :], ALU.mult), "ga_gated")
                elif kind == "gb":
                    gemm_consumed(dve, n)
                    gemm_consumed(dve, unit_of["u2", j])
                    step(v.tensor_tensor(uT[:, j, :], uT[:, j, :], gbt[:], ALU.mult), "gb_used")
                elif kind == "ya":
                    gemm_consumed(dve, unit_of["sga", j])
                    gemm_product(dve, n)
                    step.frees_gemm(v.tensor_tensor(yT[:, j, :], sig[0][j % 2][:], g[:], ALU.mult), n)
                elif kind == "yb":
                    gemm_consumed(dve, unit_of["sgb", j])
                    gemm_product(dve, n)
                    step.frees_gemm(v.tensor_tensor(sig[1][j % 2][:], sig[1][j % 2][:], g[:], ALU.mult), n)
                    step(v.tensor_tensor(yT[:, j, :], yT[:, j, :], sig[1][j % 2][:], ALU.add), "y_done")

            step(v.memset(cols[:, 104:105], 0.0))
            step(v.memset(cin[:, 0:3], 0.0))
            step(v.memset(bias16[:, 8:12], 0.0))
            step(v.memset(nt_[:], 0.0))
            dve.wait_ge(con_loaded, 16 * 8)

            for it in sched:
                kind, j = it
                if kind == "unit":
                    unit(j)
                elif kind == "half":
                    if j[1]:
                        unit(j[0])
                elif kind == "cols":
                    b = side_product(dve, (it, 0))
                    step.frees(v.tensor_copy(cols[:, 0:104], b[:, 0:104]), (it, 0))
                elif kind == "norm":
                    stage, hf = j
                    h4 = slice(4 * hf, 4 * hf + 4)
                    sums_ready()
                    rsqrt(rs[:, h4], ss[:, h4], 1.0 / D)
                    for c in range(4 * hf, 4 * hf + 4):
                        step(v.tensor_scalar(diag[:, c, :], ident, rs[:, c:c + 1], None, ALU.mult),
                             "diag_ready" if c % 4 == 3 else None)
                    t = slice(hf * 512, hf * 512 + 512)
                    for k in range(KD):
                        b = side_product(dve, (it, k))
                        g0 = 64 + 8 * stage + k
                        low(hT[1][:, k, t], b[:], hT[0][:, k, t], (it, k), cols[:, g0:g0 + 1])
                elif kind == "mx":
                    t = slice(j * 512, j * 512 + 512)
                    for k in range(KD):
                        b = side_product(dve, (it, k))
                        low(hT[1][:, k, t], b[:], hT[0][:, k, t], (it, k))
                elif kind == "smT":
                    x, t1, e, s, s2, p = (t[:] for t in sm)
                    b = side_product(dve, (it, 0))
                    dve.wait_ge(small_loaded, 16 * 7)
                    step.frees(v.tensor_tensor(x, b[:, 0:P].rearrange("p (c h) -> p c h", c=NT), over(bias16[:], NT), ALU.add), (it, 0))
                    step(v.tensor_scalar(t1, x, -1.0, None, ALU.mult))
                    step(v.tensor_tensor(t1, t1, x, ALU.max), "sm_abs")
                    dve.wait_ge(N["sm_exp"], 1)
                    step(v.tensor_scalar(s, e, 2.0, None, ALU.add))
                    step(v.reciprocal(s, s))
                    step(v.tensor_tensor(s, s, e, ALU.mult))
                    step(v.tensor_tensor(s2, s, s, ALU.mult))
                    step(v.tensor_scalar(p, s2, 1.0 / 19, None, ALU.mult))
                    for n in range(8, 0, -1):
                        step(v.scalar_tensor_tensor(out=p, in0=p, scalar=1.0 / (2 * n + 1), in1=s2, op0=ALU.add, op1=ALU.mult))
                    step(v.scalar_tensor_tensor(out=p, in0=p, scalar=1.0, in1=s, op0=ALU.add, op1=ALU.mult))
                    step(v.tensor_scalar(t1, x, 0.0, None, ALU.max))
                    step(v.scalar_tensor_tensor(out=dts[:], in0=p, scalar=2.0, in1=t1, op0=ALU.mult, op1=ALU.add))
                    step(v.tensor_tensor(s, x, dts[:], ALU.subtract), "sm_arg")
                    step(v.tensor_scalar(easm[:], easm[:], -1.0, None, ALU.mult))
                    step(v.tensor_tensor(da[:, :, 0:8], dts[:, :, 0:8], over(easm[:, 0:8], NT), ALU.mult))
                    step(v.tensor_tensor(da[:, :, 8:12], dts[:, :, 12:16], over(easm[:, 8:12], NT), ALU.mult), "da_ready")
                elif kind == "acs":
                    b = side_product(dve, (it, 0))
                    step.frees(v.tensor_scalar(nacs[:].rearrange("p c h -> p (c h)"), b[:, 0:96], -1.0, None, ALU.mult), (it, 0))
                elif kind == "wo2T":
                    if j == 0:
                        dve.wait_ge(x2_in, 32)
                    for h in range(2):
                        b = side_product(dve, (it, h))
                        d = tok_dest(it, h)
                        step.frees(v.tensor_tensor(d, b[:].rearrange("p (c n) -> p c n", c=4), x2[:, 4 * h:4 * h + 4, hslice(j)], ALU.add), (it, h))
                    if j > 0:
                        final_gain(j - 1)
                elif kind in ("woT", "downT"):
                    last, gain = (kind == "downT"), (gbc2 if kind == "downT" else gbc)
                    if j == 0:
                        dve.wait_ge(gain_loaded, 64 if last else 48)
                    for h in range(2):
                        b = side_product(dve, (it, h))
                        dve.wait_ge(N["sq_part"], 64 * last + 8 * j + 4 * h + 4)
                        t = slice(4 * h, 4 * h + 4)
                        d = fo[j // 4][:, t, hslice(j % 4)] if last else mo[:, t, hslice(j)]
                        step.frees(v.tensor_tensor(d, b[:].rearrange("p (c n) -> p c n", c=4), over(gain[:, hslice(j)], 4), ALU.mult), (it, h))
                elif kind in tok_items:
                    b = side_product(dve, (it, 1))
                    if kind == "zT" and j > 0:
                        dve.wait_ge(z_out[1], 16 * j)
                    step.frees(v.tensor_copy(tok_dest(it, 1), b[:].rearrange("p (c n) -> p c n", c=4)), (it, 1))
                    if kind == "q2T":
                        side_consumed(dve, (it, 0))
                        swapped = lambda t: t.rearrange("p c (g x n) -> p (c g) x n", x=2, n=16)
                        tk = tok[:].rearrange("p c (h d) -> p (c h) d", d=64)
                        sn = swapped(rope[:, 1])
                        if j == 4:
                            dve.wait_ge(rope_loaded, 16 * 3)
                        elif j == 0:
                            g = qkg[:, 0, :]
                            c16 = rope[:, 0].rearrange("p c (h d) -> p (c h) d", d=64)
                            step(v.tensor_tensor(c16, c16, over(g, 16), ALU.mult))
                            gx = g.rearrange("p (g x n) -> p g x n", x=2, n=16)
                            sg_ = rope[:, 1].rearrange("p c (h g x n) -> p (c h) g x n", h=2, g=2, x=2)
                            for x in range(2):
                                for b2 in range(2):
                                    d = sg_[:, :, b2, x, :]
                                    step(v.tensor_tensor(d, d, over(gx[:, b2, 1 - x, :], 16), ALU.mult))
                        dve.wait_ge(N["tok_sq"], (j + 1) % 5 + 1)
                        step(v.reduce_sum(rr[:, 0:16], rp2[:].rearrange("p c (h d) -> p (c h) d", d=64), axis=AX))
                        rsqrt(rr[:, 16:32], rr[:, 0:16], 1.0 / 64)
                        step(v.tensor_tensor(tk, tk, widen(rr[:, 16:32], 64), ALU.mult))
                        if j == 4:
                            step(v.tensor_tensor(tk, tk, over(qkg[:, 1, :], 16), ALU.mult))
                        step(v.tensor_tensor(rp1[:], tok[:], rope[:, 0], ALU.mult))
                        sw, ro = swapped(tok[:]), swapped(rp2[:])
                        for x in range(2):
                            step(v.tensor_tensor(ro[:, :, x, :], sw[:, :, 1 - x, :], sn[:, :, x, :], ALU.mult))
                        if j < 4:
                            side_product(dve, (("q2B", j - 1 if j else 4), 3))
                        one, two = (t[:].rearrange("p c (h d) -> p (c h) d", d=64).unsqueeze(2).to_broadcast([P, 2 * NT, 2, 64])
                                    for t in (rp1, rp2))
                        step(v.tensor_tensor(rpd[:].rearrange("p c h a d -> p (c h) a d"), one, two, ALU.add), "rope_done")
                elif kind == "prep":
                    qk = qkv[:, :, 0:512]
                    for h in range(2):
                        for q in (8, 9, 10, 11):
                            side_consumed(dve, (("convT", q), h))
                    step(v.tensor_tensor(psq[:], qk, qk, ALU.mult))
                    step(v.reduce_sum(rr[:].rearrange("p (c h) -> p c h", c=NT), psq[:].rearrange("p c (h d) -> p c h d", d=64), axis=AX))
                    rsqrt(psq[:, 0, 0:64], rr[:], 1.0)
                    r = psq[:, 0, 0:64].rearrange("p (c h) -> p c h", c=NT)
                    step(v.tensor_scalar(r[:, :, 0:4], r[:, :, 0:4], 0.125, None, ALU.mult))
                    for c in range(NT):
                        q = qkv[:, c, 0:512].rearrange("p (h d) -> p h d", d=64)
                        step(v.tensor_tensor(q, q, widen(r[:, c, :], 64), ALU.mult))
                    step(v.memset(akT[:], 0.0))
                    step(v.memset(av[:, 0, :], 0.0), "prep_done")
                elif kind == "as":
                    c = j
                    if c > 0:
                        side_product(dve, (("ap", c - 1), 1))
                    for p in range(2):
                        b = side_product(dve, (it, p))
                        bb = b[:].rearrange("p (i n) -> p i n", i=2)
                        al = con[:, C_ALI + 512 * p:C_ALI + 512 * p + 512].rearrange("p (i n) -> p i n", i=2)
                        n0 = P if c == 0 else 0
                        if c == 0:
                            step(v.memset(asb[:, 2 * p:2 * p + 2, 0:P], NEG))
                        step.frees(v.scalar_tensor_tensor(out=asb[:, 2 * p:2 * p + 2, n0:], in0=bb[:, :, n0:], scalar=0.125,
                                                          in1=al[:, :, n0:], op0=ALU.mult, op1=ALU.add), (it, p))
                    step(v.reduce_max(amx[:], asb[:], axis=AX))
                    step(v.tensor_tensor(amx[:], amx[:], sinkb[:], ALU.max))
                    step(v.tensor_scalar(anm[:], amx[:], -1.0, None, ALU.mult))
                    step(v.tensor_tensor(ads[:], sinkb[:], amx[:], ALU.subtract), "att_max")
                elif kind == "ap":
                    dve.wait_ge(N["att_exp"], j + 1)
                    step(v.tensor_tensor(aden[:], asum[:], ads[:], ALU.add))
                    step(v.reciprocal(aden[:], aden[:]))
                    b = side_product(dve, (it, 1))
                    step.frees(v.tensor_copy(apT[:, 2:4], b[:].rearrange("p (i s n) -> p i s n", i=2, s=2)), (it, 1))
                elif kind == "ao":
                    b = side_product(dve, (it, 0))
                    for p in range(2):
                        o = atts[:, j, :].rearrange("p (k q d) -> p q k d", k=2, q=2)[:, p]
                        s = b[:, 0:256].rearrange("p (k q d) -> p q k d", k=2, q=2)[:, p]
                        ins = v.tensor_tensor(o, s, widen(aden[:, 2 * p:2 * p + 2], 64), ALU.mult)
                        if p == 0:
                            step(ins)
                        else:
                            step.frees(ins, (it, 0))
                elif kind == "ra":
                    c, z = j, j % 2
                    if c == 0:
                        for u in range(4):
                            gemm_product(dve, unit_of["av", 0] - u)
                        step(v.memset(kTp[0][:], 0.0))
                        step(v.memset(kTp[1][:], 0.0))
                        step(v.memset(Sbd[:], 0.0))
                        dve.wait_ge(rest_loaded, 16)
                        step(v.tensor_copy(identb[:], ident))
                        step(v.tensor_copy(negb[:], con[:, C_NEG:C_NEG + P]))
                        step(v.memset(Sst[:], 0.0), "init_done")
                elif kind == "rk":
                    c, z = j, j % 2
                    b = side_product(dve, (it, "qT"))
                    step.frees(v.tensor_copy(kq[z][:, :, 1, :], b[:, 0:256].rearrange("p (a n) -> p a n", a=2)), (it, "qT"))
                    dve.wait_ge(N["ed_ready"], c + 1)
                    for r in range(2):
                        step(v.tensor_copy(cdc[z][64 * r:64 * r + 64, :], cd[z][64 * r:64 * r + 64, 8:12].rearrange("p (a b) -> p a b", b=2)[:, :, r]))
                    b = side_product(dve, (it, "g"))
                    step(v.tensor_tensor(E[z][:, 0:4, :], E[z][:, 0:4, :], over(b[:, 0:P], 4), ALU.mult))
                    step.frees(v.tensor_tensor(E[z][:, 4:8, :], E[z][:, 4:8, :], over(b[:, P:2 * P], 4), ALU.mult), (it, "g"))
                elif kind == "rj":
                    c, z = j, j % 2
                    for p in range(2):
                        b = side_product(dve, (it, f"kq{p}"))
                        e = E[z][:, 8 + 2 * p:10 + 2 * p, :].unsqueeze(2).to_broadcast([P, 2, 2, P])
                        step.frees(v.tensor_tensor(SQ[z][:, 2 * p:2 * p + 2], b[:].rearrange("p (h a n) -> p h a n", h=2, a=2), e, ALU.mult), (it, f"kq{p}"))
                    if c >= 2:
                        dve.wait_ge(N["rec_mix"], c - 1)
                    step(v.tensor_tensor(XT[z][:], SQ[z][:, :, 0, :], over(con[:, C_LV:C_LV + P], 4), ALU.mult))
                    step(v.scalar_tensor_tensor(out=XT[z][:], in0=XT[z][:], scalar=-1.0, in1=over(ident, 4), op0=ALU.mult, op1=ALU.add), "rec_x0")
                elif kind == "ly":
                    c, lv = j
                    b = side_product(dve, (it, 0))
                    step.frees(v.tensor_tensor(Y[c % 2][:], four(b), over(con[:, C_LV + lv * P:C_LV + (lv + 1) * P], 4), ALU.mult), (it, 0))
                elif kind == "lx":
                    c, lv = j
                    z = c % 2
                    side_product(dve, (it, "t"))
                    if lv == 1:
                        side_consumed(dve, (("rx", c), "xT"))
                    if lv < 6:
                        b = side_product(dve, (it, "x"))
                        step.frees(v.tensor_tensor(X[z][:], X[z][:], four(b), ALU.subtract), (it, "x"))
                    b = side_product(dve, (it, "t"))
                    step.frees(v.tensor_tensor(XT[z][:], XT[z][:], four(b), ALU.subtract), (it, "t"))
                elif kind == "r1":
                    c, z = j, j % 2
                    side_consumed(dve, (("uw", c), 0))
                    b = side_product(dve, (it, 0))
                    step(v.tensor_tensor(vn[:], uw[z][:, 0:256], b[:, 0:256], ALU.subtract), "rec_vn")
                    step.frees(v.tensor_tensor(h64(o1[:]), h64(b[:, 256:512]), widen(eacs[:, c, 8:12], 64), ALU.mult), (it, 0))
                elif kind == "r2":
                    c, z = j, j % 2
                    b = side_product(dve, (it, 0))
                    step(v.tensor_tensor(mix[:, 512:768], o1[:], b[:, 0:256], ALU.add), "y_summed")
                    step.frees(v.tensor_tensor(tS[:], b[:, 256:512].rearrange("p (a n) -> p a n", a=2), over(blk, 2), ALU.mult), (it, 0))
                    for p in range(2):
                        step(v.scalar_tensor_tensor(out=Sbd[:, p, :], in0=Sbd[:, p, :], scalar=cdc[z][:, p:p + 1], in1=tS[:, p, :],
                                                    op0=ALU.mult, op1=ALU.add), "rec_S" if p else None)
                elif kind == "yo":
                    c, z = j, j % 2
                    if c == 0:
                        dve.wait_ge(N["eacs_ready"], 1)
                    else:
                        dve.wait_ge(N["rec_mix"], c)
                    b = side_product(dve, (it, 0))
                    step.frees(v.tensor_tensor(h64(mix[:, 0:512]), h64(b[:]), widen(eacs[:, c, 0:8], 64), ALU.mult), (it, 0))
                    step(v.tensor_tensor(h64(Sst[:]), h64(Sst[:]), widen(cd[z][:, 0:8], 64), ALU.mult))
                elif kind == "yd":
                    b = side_product(dve, (it, 0))
                    step.frees(v.tensor_tensor(mix[:, 0:512], mix[:, 0:512], b[:], ALU.add), (it, 0))
                elif kind == "st":
                    b = side_product(dve, (it, 0))
                    step.frees(v.tensor_tensor(Sst[:], Sst[:], b[:], ALU.add), (it, 0))
                elif kind == "rq":
                    c = j
                    sq = msq[c % 2] if c < NT - 1 else msq7
                    dve.wait_ge(N["sq_mix"], c + 1)
                    step(v.reduce_sum(nss[:, 0:2], sq[:, 0:512].rearrange("p (g n) -> p g n", g=2), axis=AX))
                    step(v.reduce_sum(nss[:, 2:6], h64(sq[:, 512:768]), axis=AX))
                    step(v.tensor_scalar(nss[:, 0:2], nss[:, 0:2], 0.25, None, ALU.mult))
                    rsqrt(nrs, nss, 1.0 / 64, "nrs_ready")
                elif kind == "resid":
                    r, hf = j
                    h4 = slice(4 * hf, 4 * hf + 4)
                    if hf == 0:
                        dve.wait_ge(N["sq_part"], 64 * r + 64)
                        step(v.reduce_sum(ss[:], ssp, axis=AX))
                        rsqrt(rs[:], ss[:], 1.0 / D)
                        step(v.tensor_copy(rs_res[:], rs[:]))
                        if r == 0:
                            dve.wait_ge(res_loaded, 16)
                    for c in range(4 * hf, 4 * hf + 4):
                        for s in range(1 + r):
                            src = mo[:, c, :] if r == 0 else fo[s][:, c, :]
                            x = x1[:, c, :] if r == 0 else x1[:, c, 512 * s:512 * s + 512]
                            step(v.scalar_tensor_tensor(out=x, in0=src, scalar=rs_res[:, c:c + 1], in1=x, op0=ALU.mult, op1=ALU.add),
                                 "resid_done" if s == r else None)
                elif kind == "q2B":
                    for n in range(4):
                        t = slice(n % 2 * 512, n % 2 * 512 + 512)
                        b = side_product(dve, (it, n))
                        if j < 4:
                            d = qp[64:P, 2 * j + n // 2, t]
                            low(d, b[64:P, :], d, (it, n))
                        else:
                            low(kp[:, n // 2, 1, t], b[:], kp[:, n // 2, 0, t], (it, n))
                elif kind == "v2T":
                    for h in range(2):
                        b = side_product(dve, (it, h))
                        d = vp[:, 4 * h:4 * h + 4].rearrange("p c k (s d) -> p c k s d", s=2)
                        low(d[:, :, :, 1, :], b[:].rearrange("p (c k d) -> p c k d", c=4, k=2), d[:, :, :, 0, :], (it, h))
                    for h in range(2):
                        r = slice(64 * h, 64 * h + 64)
                        for k in range(2):
                            step(v.tensor_copy(fold[r, 64 * k:64 * k + 64], ident[r, r]), "fold_ready" if h and k else None)
                elif kind == "ln":
                    b = side_product(dve, (it, 1))
                    step.frees(v.tensor_copy(wsT[:, 4:8], b[:].rearrange("p (i n) -> p i n", i=4)), (it, 1))
                    for q in range(4):
                        side_consumed(dve, (("viT", q), 0))
                    step(v.reduce_sum(mean[:], vv[:], axis=AX))
                    step(v.tensor_scalar(mean[:], mean[:], -1.0 / 512, None, ALU.mult))
                    for c in range(NT):
                        step(v.tensor_scalar(vv[:, c, :], vv[:, c, :], mean[:, c:c + 1], None, ALU.add), "mean_done" if c == NT - 1 else None)
                    sums_ready()
                    rsqrt(rs[:], ss[:], 1.0 / 512)
                    for c in range(NT):
                        step(v.scalar_tensor_tensor(out=vv[:, c, :], in0=vv[:, c, :], scalar=rs[:, c:c + 1], in1=lnp[:, 0, :],
                                                    op0=ALU.mult, op1=ALU.mult))
                        step(v.tensor_tensor(vv[:, c, :], vv[:, c, :], lnp[:, 1, :], ALU.add), "ln_done" if c == NT - 1 else None)
                elif kind == "a2s":
                    g = scores_product(dve, j)
                    mx, neg = a2m[:, j % 2:j % 2 + 1], a2m[:, 2 + j % 2:3 + j % 2]
                    step(v.reduce_max(mx, g[:], axis=AX))
                    step(v.tensor_scalar(neg, mx, -0.125, None, ALU.mult), "a2_max")
                elif kind == "a2x":
                    q = j[1]
                    b = side_product(dve, (it, 0))
                    low(PT[q][1][:], b[:], PT[q][0][:], (it, 0))
                elif kind == "a2o":
                    h = 2 * j % 8
                    for i in range(2):
                        scores_consumed(dve, 2 * j + i)
                    step(v.reciprocal(a2r[:], a2d[:, h:h + 2]))
                    b = side_product(dve, (it, 0))
                    step.frees(v.tensor_tensor(h64(ot[:, h * 64:h * 64 + P]), b[:, 0:256].rearrange("p (h n) -> p h n", h=2)[:, :, 0:64],
                                               widen(a2r[:], 64), ALU.mult), (it, 0))
                elif kind == "a2t":
                    b = side_product(dve, (it, 0))
                    step.frees(v.tensor_copy(aoT[:, :, hslice(j)], b[:].rearrange("p (i n) -> p i n", i=4)), (it, 0))
                elif kind == "sp":
                    if j == 0:
                        for q in range(4):
                            gemm_consumed(dve, unit_of["u2", q])
                    b = side_product(dve, (it, 0))
                    step.frees(v.tensor_tensor(spt[:], b[:].rearrange("p (i n) -> p i n", i=4), bsp[:], ALU.add), (it, 0))
                    step(v.tensor_tensor(uT[:, :, hslice(j)], uT[:, :, hslice(j)], spt[:], ALU.mult))
                elif kind in ("split4", "splity"):
                    for k in range(8):
                        if kind == "split4":
                            dve.wait_ge(N["split_hi"], k + 1)
                            d = atT if k < 4 else gmT
                            step(v.tensor_tensor(d[1][:, k % 4, :], (aoT if k < 4 else uT)[:, k % 4, :], d[0][:, k % 4, :], ALU.subtract), "split_lo")
                        else:
                            dve.wait_ge(N["yT_hi"], k + 1)
                            step(v.tensor_tensor(hT[1][:, k, :], yT[:, k, :], hT[0][:, k, :], ALU.subtract), "yT_lo")
                elif kind == "final":
                    dve.wait_ge(N["sq_part"], 192)
                    step(v.reduce_sum(ss[:], ssp, axis=AX))
                    final_gain(7)
                    rsqrt(rs[:], ss[:], 1.0 / D, "rs_ready")
                    for c in range(1, NT, 2):
                        step(v.tensor_scalar(ob[:, c, :], ob[:, c, :], rs[:, c:c + 1], None, ALU.mult), "final_done")



def kernel(**inputs):
    import concourse.bacc as bacc
    from concourse.bass_utils import run_bass_kernel_spmd

    nc = bacc.Bacc("TRN2", target_bir_lowering=False, num_devices=1, dynamic_dma_scratch_size=SWDGE_RING)
    arrays, aps = {}, {}
    for name, value in inputs.items():
        v = np.ascontiguousarray(value)
        arrays[f"in_{name}"] = v
        ap = nc.dram_tensor(f"in_{name}", v.shape, mybir.dt.from_np(v.dtype), kind="ExternalInput").ap()
        aps[name] = ap[0] if name != "final_gain_2" else ap
    for name, v in zip(("con1", "con2"), consts_of_shapes()):
        arrays[name] = v
        aps[name] = nc.dram_tensor(name, v.shape, F32, kind="ExternalInput").ap()
    out = nc.dram_tensor("out", (1, T, D), F32, kind="ExternalOutput").ap()
    build_program(nc, aps, out[0])
    r = run_bass_kernel_spmd(nc, [arrays], core_ids=[0])
    return r.results[0]["out"]
```
